# Optimizing a Trainium2 kernel written in Bass

```python
import jax
import jax.numpy as jnp
from jax import lax
import numpy as np
import math
import jax, jax.numpy as jnp

D_MODEL = 1024
BATCH = 1
SEQ = 256
DEPTH = 2

EPS = 1e-6
ROPE_THETA = 10000.0
NEG_INF = -1e30
D_FF = 2816
N_BRANCH = 3
MIX_WIDTH = 512

MLA_HEADS = 8
MLA_Q_RANK = 256
MLA_KV_RANK = 128
MLA_NOPE = 64
MLA_ROPE = 32
MLA_V = 64
MLA_QK = MLA_NOPE + MLA_ROPE
ATTN_BLOCK_Q = 128

GDN_HEADS = 4
GDN_DK = 128
GDN_DV = 128
GDN_CONV = 4
GDN_CHUNK = 64

MOBA_HEADS = 8
MOBA_DH = 64
MOBA_BLOCK = 256
MOBA_TOPK = 3
MOBA_QCHUNK = 64

IN_SPLITS = (
    MLA_Q_RANK,
    MLA_KV_RANK,
    MLA_ROPE,
    GDN_HEADS * GDN_DK,
    GDN_HEADS * GDN_DK,
    GDN_HEADS * GDN_DV,
    GDN_HEADS,
    GDN_HEADS,
    GDN_HEADS * GDN_DV,
    3 * MOBA_HEADS * MOBA_DH,
    N_BRANCH * D_MODEL,
)
D_IN = sum(IN_SPLITS)


def split_cols(t, sizes):
    offs = np.cumsum(sizes)[:-1].tolist()
    return jnp.split(t, offs, axis=-1)

def rms_norm(x, g):
    xf = x.astype(jnp.float32)
    y = xf * lax.rsqrt(jnp.mean(xf * xf, axis=-1, keepdims=True) + EPS)
    return (y * g.astype(jnp.float32)).astype(x.dtype)

def l2norm(x):
    return x * lax.rsqrt(jnp.sum(x * x, axis=-1, keepdims=True) + EPS)

def rope(x, pos):
    d = x.shape[-1]
    half = d // 2
    inv_freq = ROPE_THETA ** (-jnp.arange(half, dtype=jnp.float32) * 2.0 / d)
    ang = pos.astype(jnp.float32)[:, None] * inv_freq[None, :]
    cos = jnp.cos(ang)[None, :, None, :]
    sin = jnp.sin(ang)[None, :, None, :]
    xf = x.astype(jnp.float32)
    x1, x2 = xf[..., :half], xf[..., half:]
    return jnp.concatenate([x1 * cos - x2 * sin, x2 * cos + x1 * sin], axis=-1).astype(x.dtype)

def swiglu(h, w_in, w_out):
    gate, up = jnp.split(h @ w_in, 2, axis=-1)
    return (jax.nn.silu(gate) * up) @ w_out

def causal_dwconv(x, w):
    c = x.shape[-1]
    k = w.shape[0]
    return lax.conv_general_dilated(
        x, w[:, None, :].astype(x.dtype), window_strides=(1,), padding=[(k - 1, 0)],
        dimension_numbers=('NWC', 'WIO', 'NWC'), feature_group_count=c)

def causal_attention_blocked(q, k, v, scale):
    b, h, s, dk = q.shape
    nb = s // ATTN_BLOCK_Q
    qb = jnp.moveaxis(q.reshape(b, h, nb, ATTN_BLOCK_Q, dk), 2, 0)
    k_pos = jnp.arange(s)

    def one_block(args):
        i, q_i = args
        logits = jnp.einsum('bhqd,bhkd->bhqk', q_i, k, preferred_element_type=jnp.float32) * scale
        q_pos = i * ATTN_BLOCK_Q + jnp.arange(ATTN_BLOCK_Q)
        logits = jnp.where(k_pos[None, :] <= q_pos[:, None], logits, NEG_INF)
        p = jax.nn.softmax(logits, axis=-1).astype(v.dtype)
        return jnp.einsum('bhqk,bhkd->bhqd', p, v)

    o = lax.map(one_block, (jnp.arange(nb), qb))
    return jnp.moveaxis(o, 0, 2).reshape(b, h, s, v.shape[-1])

def mla_branch(c_q, c_kv, k_rope, pos, cq_norm, ckv_norm, w_uq, w_ukv, q_norm, k_norm):
    b, s, _ = c_q.shape
    h = MLA_HEADS
    q = (rms_norm(c_q, cq_norm) @ w_uq).reshape(b, s, h, MLA_QK)
    kv = (rms_norm(c_kv, ckv_norm) @ w_ukv).reshape(b, s, h, MLA_NOPE + MLA_V)
    k_nope, v = kv[..., :MLA_NOPE], kv[..., MLA_NOPE:]
    k = jnp.concatenate([k_nope, jnp.broadcast_to(k_rope[:, :, None, :], (b, s, h, MLA_ROPE))], axis=-1)
    q = rms_norm(q, q_norm)
    k = rms_norm(k, k_norm)
    q = jnp.concatenate([q[..., :MLA_NOPE], rope(q[..., MLA_NOPE:], pos)], axis=-1)
    k = jnp.concatenate([k[..., :MLA_NOPE], rope(k[..., MLA_NOPE:], pos)], axis=-1)
    to_bhsd = lambda t: jnp.transpose(t, (0, 2, 1, 3))
    o = causal_attention_blocked(to_bhsd(q), to_bhsd(k), to_bhsd(v), MLA_QK ** -0.5)
    return jnp.transpose(o, (0, 2, 1, 3)).reshape(b, s, h * MLA_V)

def gated_delta_rule_chunked(q, k, v, beta, g):
    b, s, h, dk = q.shape
    dv = v.shape[-1]
    c = GDN_CHUNK
    n = s // c

    def chunks(t):
        return jnp.moveaxis(t.reshape((b, n, c, h) + t.shape[3:]), 3, 1)

    q, k, v, beta, g = (chunks(t) for t in (q, k, v, beta, g))
    gcum = jnp.cumsum(g, axis=-1)
    tril = jnp.tril(jnp.ones((c, c), dtype=bool))
    strict = jnp.tril(jnp.ones((c, c), dtype=bool), -1)
    decay = jnp.exp(jnp.where(tril, gcum[..., :, None] - gcum[..., None, :], NEG_INF))
    k_beta = k * beta[..., None]
    a = jnp.where(strict, jnp.einsum('bhnid,bhnjd->bhnij', k_beta, k) * decay, 0.0)
    eye = jnp.eye(c, dtype=q.dtype)
    rhs = jnp.concatenate([v * beta[..., None], k_beta * jnp.exp(gcum)[..., None]], axis=-1)
    sol = lax.linalg.triangular_solve(eye + a, rhs, left_side=True, lower=True, unit_diagonal=True)
    u, w = sol[..., :dv], sol[..., dv:]
    qk = jnp.einsum('bhnid,bhnjd->bhnij', q, k) * decay
    q_dec = q * jnp.exp(gcum)[..., None]
    g_last = gcum[..., -1]
    k_dec = k * jnp.exp(g_last[..., None] - gcum)[..., None]

    def step(state, xs):
        q_i, w_i, u_i, qk_i, k_i, gl_i = xs
        v_new = u_i - jnp.einsum('bhcd,bhde->bhce', w_i, state)
        o_i = jnp.einsum('bhcd,bhde->bhce', q_i, state) + jnp.einsum('bhcj,bhje->bhce', qk_i, v_new)
        state = state * jnp.exp(gl_i)[..., None, None] + jnp.einsum('bhcd,bhce->bhde', k_i, v_new)
        return state, o_i

    xs = tuple(jnp.moveaxis(t, 2, 0) for t in (q_dec, w, u, qk, k_dec, g_last))
    state0 = jnp.zeros((b, h, dk, dv), q.dtype)
    _, o = lax.scan(step, state0, xs)
    return jnp.transpose(o, (1, 0, 3, 2, 4)).reshape(b, s, h, dv)

def gdn_branch(q, k, v, b_logit, a_logit, z, conv_w, a_log, dt_bias, out_norm):
    b, s, _ = q.shape
    f32 = jnp.float32
    qkv = jax.nn.silu(causal_dwconv(jnp.concatenate([q, k, v], axis=-1), conv_w)).astype(f32)
    q, k, v = jnp.split(qkv, [GDN_HEADS * GDN_DK, 2 * GDN_HEADS * GDN_DK], axis=-1)
    q = l2norm(q.reshape(b, s, GDN_HEADS, GDN_DK)) * (GDN_DK ** -0.5)
    k = l2norm(k.reshape(b, s, GDN_HEADS, GDN_DK))
    v = v.reshape(b, s, GDN_HEADS, GDN_DV)
    beta = jax.nn.sigmoid(b_logit.astype(f32))
    g = -jnp.exp(a_log.astype(f32)) * jax.nn.softplus(a_logit.astype(f32) + dt_bias.astype(f32))
    o = gated_delta_rule_chunked(q, k, v, beta, g)
    o = rms_norm(o, out_norm).astype(z.dtype) * jax.nn.silu(z.reshape(b, s, GDN_HEADS, GDN_DV))
    return o.reshape(b, s, GDN_HEADS * GDN_DV)

def moba_branch(qkv, pos, q_norm, k_norm):
    b, s, _ = qkv.shape
    h, dh, bs = MOBA_HEADS, MOBA_DH, MOBA_BLOCK
    q, k, v = (t.reshape(b, s, h, dh) for t in jnp.split(qkv, 3, axis=-1))
    q = rope(rms_norm(q, q_norm), pos)
    k = rope(rms_norm(k, k_norm), pos)
    nb = -(-s // bs)
    s_pad = nb * bs

    def prep(t):
        return jnp.pad(jnp.transpose(t, (0, 2, 1, 3)), ((0, 0), (0, 0), (0, s_pad - s), (0, 0)))

    q, k, v = prep(q), prep(k), prep(v)
    kb = k.reshape(b, h, nb, bs, dh)
    vb = v.reshape(b, h, nb, bs, dh)
    k_mean = jnp.mean(kb.astype(jnp.float32), axis=3)
    gate = jnp.einsum('bhsd,bhnd->bhsn', q.astype(jnp.float32), k_mean)
    q_blk = jnp.arange(s_pad) // bs
    gate = jnp.where(jnp.arange(nb)[None, :] < q_blk[:, None], gate, NEG_INF)
    n_sel = min(MOBA_TOPK, nb)
    _, sel = lax.top_k(gate, n_sel)
    sel_valid = sel < q_blk[:, None]
    scale = dh ** -0.5
    b_idx = jnp.arange(b)[:, None, None, None]
    h_idx = jnp.arange(h)[None, :, None, None]
    key_off = jnp.arange(bs)

    def one_chunk(ci):
        start = ci * MOBA_QCHUNK
        q_c = lax.dynamic_slice_in_dim(q, start, MOBA_QCHUNK, axis=2)
        sel_c = lax.dynamic_slice_in_dim(sel, start, MOBA_QCHUNK, axis=2)
        valid_c = lax.dynamic_slice_in_dim(sel_valid, start, MOBA_QCHUNK, axis=2)
        k_sel = kb[b_idx, h_idx, sel_c]
        v_sel = vb[b_idx, h_idx, sel_c]
        s_sel = jnp.einsum('bhqd,bhqnkd->bhqnk', q_c, k_sel, preferred_element_type=jnp.float32) * scale
        s_sel = jnp.where(valid_c[..., None], s_sel, NEG_INF)
        j = start // bs
        k_own = lax.dynamic_index_in_dim(kb, j, axis=2, keepdims=False)
        v_own = lax.dynamic_index_in_dim(vb, j, axis=2, keepdims=False)
        s_own = jnp.einsum('bhqd,bhkd->bhqk', q_c, k_own, preferred_element_type=jnp.float32) * scale
        q_pos = start + jnp.arange(MOBA_QCHUNK)
        k_pos = j * bs + key_off
        s_own = jnp.where(k_pos[None, :] <= q_pos[:, None], s_own, NEG_INF)
        logits = jnp.concatenate([s_sel.reshape(b, h, MOBA_QCHUNK, n_sel * bs), s_own], axis=-1)
        p = jax.nn.softmax(logits, axis=-1).astype(v.dtype)
        p_sel = p[..., :n_sel * bs].reshape(b, h, MOBA_QCHUNK, n_sel, bs)
        p_own = p[..., n_sel * bs:]
        return (jnp.einsum('bhqnk,bhqnkd->bhqd', p_sel, v_sel)
                + jnp.einsum('bhqk,bhkd->bhqd', p_own, v_own))

    o = lax.map(one_chunk, jnp.arange(s_pad // MOBA_QCHUNK))
    o = jnp.transpose(o, (1, 0, 3, 2, 4)).reshape(b, s_pad, h * dh)
    return o[:, :s]

def first_inputs(seed: int = 0) -> dict:
    key = jax.random.key(seed)
    ks = jax.random.split(key, 24)
    L = DEPTH
    f32 = jnp.float32

    def nrm(k, shape, fan_in):
        return jax.random.normal(k, shape, f32) * (fan_in ** -0.5)

    def gain(k, shape):
        return 1.0 + 0.02 * jax.random.normal(k, shape, f32)

    dt = jnp.exp(jax.random.uniform(ks[14], (L, GDN_HEADS), f32, np.log(1e-3), np.log(1e-1)))
    return {
        'x': jax.random.normal(ks[0], (BATCH, SEQ, D_MODEL), f32),
        'ffa_norm': gain(ks[1], (L, D_MODEL)),
        'ffa_w_in': nrm(ks[2], (L, D_MODEL, 2 * D_FF), D_MODEL),
        'ffa_w_out': nrm(ks[3], (L, D_FF, D_MODEL), D_FF),
        'mix_norm': gain(ks[4], (L, D_MODEL)),
        'w_in': nrm(ks[5], (L, D_MODEL, D_IN), D_MODEL),
        'mla_cq_norm': gain(ks[6], (L, MLA_Q_RANK)),
        'mla_ckv_norm': gain(ks[7], (L, MLA_KV_RANK)),
        'mla_w_uq': nrm(ks[8], (L, MLA_Q_RANK, MLA_HEADS * MLA_QK), MLA_Q_RANK),
        'mla_w_ukv': nrm(ks[9], (L, MLA_KV_RANK, MLA_HEADS * (MLA_NOPE + MLA_V)), MLA_KV_RANK),
        'mla_q_norm': gain(ks[10], (L, MLA_QK)),
        'mla_k_norm': gain(ks[11], (L, MLA_QK)),
        'gdn_conv': nrm(ks[12], (L, GDN_CONV, GDN_HEADS * (2 * GDN_DK + GDN_DV)), GDN_CONV),
        'gdn_a_log': jnp.log(jax.random.uniform(ks[13], (L, GDN_HEADS), f32, 1.0, 16.0)),
        'gdn_dt_bias': dt + jnp.log(-jnp.expm1(-dt)),
        'gdn_out_norm': gain(ks[15], (L, GDN_DV)),
        'moba_q_norm': gain(ks[16], (L, MOBA_DH)),
        'moba_k_norm': gain(ks[17], (L, MOBA_DH)),
        'w_branch': nrm(ks[18], (L, N_BRANCH, MIX_WIDTH, D_MODEL), MIX_WIDTH),
        'w_out': nrm(ks[19], (L, D_MODEL, D_MODEL), D_MODEL),
        'ffb_norm': gain(ks[20], (L, D_MODEL)),
        'ffb_w_in': nrm(ks[21], (L, D_MODEL, 2 * D_FF), D_MODEL),
        'ffb_w_out': nrm(ks[22], (L, D_FF, D_MODEL), D_FF),
    }

def first_block(x, ffa_norm, ffa_w_in, ffa_w_out, mix_norm, w_in, mla_cq_norm, mla_ckv_norm,
              mla_w_uq, mla_w_ukv, mla_q_norm, mla_k_norm, gdn_conv, gdn_a_log, gdn_dt_bias,
              gdn_out_norm, moba_q_norm, moba_k_norm, w_branch, w_out, ffb_norm, ffb_w_in,
              ffb_w_out):
    b, s, _ = x.shape
    pos = jnp.arange(s, dtype=jnp.int32)
    for l in range(DEPTH):
        x = x + 0.5 * swiglu(rms_norm(x, ffa_norm[l]), ffa_w_in[l], ffa_w_out[l])
        h = rms_norm(x, mix_norm[l])
        (c_q, c_kv, k_rope, g_q, g_k, g_v, g_b, g_a, g_z, m_qkv, gate_logits) = split_cols(h @ w_in[l], IN_SPLITS)
        o_mla = mla_branch(c_q, c_kv, k_rope, pos, mla_cq_norm[l], mla_ckv_norm[l], mla_w_uq[l],
                           mla_w_ukv[l], mla_q_norm[l], mla_k_norm[l])
        o_gdn = gdn_branch(g_q, g_k, g_v, g_b, g_a, g_z, gdn_conv[l], gdn_a_log[l], gdn_dt_bias[l],
                           gdn_out_norm[l])
        o_moba = moba_branch(m_qkv, pos, moba_q_norm[l], moba_k_norm[l])
        branches = jnp.stack([o_mla, o_gdn, o_moba], axis=2)
        up = jnp.einsum('bsnw,nwd->bsnd', branches, w_branch[l])
        gates = jax.nn.sigmoid(gate_logits.reshape(b, s, N_BRANCH, D_MODEL))
        x = x + jnp.sum(gates * up, axis=2) @ w_out[l]
        x = x + 0.5 * swiglu(rms_norm(x, ffb_norm[l]), ffb_w_in[l], ffb_w_out[l])
    return x


SC_GROUPS = 8
SC_WIDTH = 512
SC_WIDTH_CONV = 3
CF_GROUPS = 8
CF_WIDTH = 512
CF_WIDTH_CONV = 31
EV_IN = 3 * SC_WIDTH + 2 * CF_WIDTH
EV_OUT_IN = SC_WIDTH + CF_WIDTH

LRU_HEADS = 8
LRU_WIDTH = 512
LRU_BLOCK = LRU_WIDTH // LRU_HEADS
LRU_CONV = 4
LRU_C = 8.0
DIL_PATTERNS = ((128, 1), (512, 4), (2048, 16))
N_DIL_GROUPS = len(DIL_PATTERNS)
DIL_HEADS = 4
DIL_HEAD_DIM = 64
DIL_OUT = DIL_HEADS * DIL_HEAD_DIM
DIL_QKV = N_DIL_GROUPS * DIL_OUT
ATTN_BLOCK = 128
OD_IN = 2 * LRU_WIDTH + 3 * DIL_QKV
OD_OUT_IN = LRU_WIDTH + DIL_OUT

FFN_CONV = 3

N_EVEN = (DEPTH + 1) // 2
N_ODD = DEPTH // 2


def rmsnorm(x, g):
    xf = x.astype(jnp.float32)
    y = xf * lax.rsqrt(jnp.mean(xf * xf, axis=-1, keepdims=True) + EPS)
    return (y * g.astype(jnp.float32)).astype(x.dtype)

def layernorm(x, g, b):
    xf = x.astype(jnp.float32)
    mu = jnp.mean(xf, axis=-1, keepdims=True)
    var = jnp.mean(jnp.square(xf - mu), axis=-1, keepdims=True)
    y = (xf - mu) * lax.rsqrt(var + EPS) * g.astype(jnp.float32) + b.astype(jnp.float32)
    return y.astype(x.dtype)

def causal_dwconv_2(x, w):
    K, C = w.shape
    return lax.conv_general_dilated(
        x, w[:, None, :].astype(x.dtype), window_strides=(1,), padding=[(K - 1, 0)],
        dimension_numbers=("NWC", "WIO", "NWC"), feature_group_count=C)

def even_mixer(h, w_in, sc_conv_w, cf_conv_w, cf_conv_b, cf_ln_g, cf_ln_b, w_out):
    z = h @ w_in
    sc_b, sc_c, sc_x, cf_a, cf_g = jnp.split(
        z, [SC_WIDTH, 2 * SC_WIDTH, 3 * SC_WIDTH, 3 * SC_WIDTH + CF_WIDTH], axis=-1)
    y_sc = sc_b * causal_dwconv_2(sc_c * sc_x, sc_conv_w)
    u = cf_a * jax.nn.sigmoid(cf_g)
    u = causal_dwconv_2(u, cf_conv_w) + cf_conv_b
    u = jax.nn.silu(layernorm(u, cf_ln_g, cf_ln_b))
    return jnp.concatenate([y_sc, u], axis=-1) @ w_out

def rg_lru(xc, w_a, b_a, w_x, b_x, lam):
    B, S, W = xc.shape
    xb = xc.reshape(B, S, LRU_HEADS, LRU_BLOCK)
    r = jax.nn.sigmoid(jnp.einsum("bshi,hij->bshj", xb, w_a).reshape(B, S, W) + b_a)
    i = jax.nn.sigmoid(jnp.einsum("bshi,hij->bshj", xb, w_x).reshape(B, S, W) + b_x)
    log_a = -LRU_C * r.astype(jnp.float32) * jax.nn.softplus(-lam.astype(jnp.float32))
    a = jnp.exp(log_a)
    mult = jnp.sqrt(-jnp.expm1(2.0 * log_a))
    bt = mult * (i * xc).astype(jnp.float32)

    def combine(left, right):
        a1, b1 = left
        a2, b2 = right
        return a1 * a2, a2 * b1 + b2

    _, hs = lax.associative_scan(combine, (a, bt), axis=1)
    return hs.astype(xc.dtype)

def dilated_group_attention(q, k, v, window, dilation):
    B, S, H, Dh = q.shape
    L = S // dilation
    nb = -(-L // ATTN_BLOCK)
    Lp = nb * ATTN_BLOCK
    span = window // dilation

    def strided(t):
        t = t.reshape(B, L, dilation, H, Dh).transpose(0, 2, 1, 3, 4)
        t = jnp.pad(t, ((0, 0), (0, 0), (0, Lp - L), (0, 0), (0, 0)))
        return t.reshape(B, dilation, nb, ATTN_BLOCK, H, Dh)

    def with_prev(t):
        prev = jnp.pad(t[:, :, :-1], ((0, 0), (0, 0), (1, 0), (0, 0), (0, 0), (0, 0)))
        return jnp.concatenate([prev, t], axis=3)

    qb = strided(q)
    kk = with_prev(strided(k))
    vv = with_prev(strided(v))
    s = jnp.einsum("brnqhd,brnkhd->brnhqk", qb, kk).astype(jnp.float32)
    qi = jnp.arange(ATTN_BLOCK)[:, None]
    kj = jnp.arange(2 * ATTN_BLOCK)[None, :]
    steps = ATTN_BLOCK + qi - kj
    band = (steps >= 0) & (steps <= span)
    blk_idx = jnp.arange(nb)[:, None, None]
    mask = band[None] & ((blk_idx > 0) | (kj >= ATTN_BLOCK)[None])
    s = jnp.where(mask[None, None, :, None], s, -jnp.inf)
    m = jnp.max(s, axis=-1, keepdims=True)
    p = jnp.exp(s - m)
    den = jnp.sum(p, axis=-1, keepdims=True)
    o = jnp.einsum("brnhqk,brnkhd->brnqhd", p, vv.astype(jnp.float32))
    o = o / jnp.swapaxes(den, 3, 4)
    lse = jnp.swapaxes((m + jnp.log(den))[..., 0], 3, 4)
    o = o.reshape(B, dilation, Lp, H, Dh)[:, :, :L].transpose(0, 2, 1, 3, 4).reshape(B, S, H, Dh)
    lse = lse.reshape(B, dilation, Lp, H)[:, :, :L].transpose(0, 2, 1, 3).reshape(B, S, H)
    return o, lse

def dilated_attention(q, k, v, q_norm_g, k_norm_g):
    B, S, _ = q.shape
    shp = (B, S, N_DIL_GROUPS, DIL_HEADS, DIL_HEAD_DIM)
    qn = rmsnorm(q.reshape(shp), q_norm_g) * (DIL_HEAD_DIM ** -0.5)
    kn = rmsnorm(k.reshape(shp), k_norm_g)
    vr = v.reshape(shp)
    outs, lses = [], []
    for g, (window, dilation) in enumerate(DIL_PATTERNS):
        o, lse = dilated_group_attention(qn[:, :, g], kn[:, :, g], vr[:, :, g], window, dilation)
        outs.append(o)
        lses.append(lse)
    o = jnp.stack(outs)
    wts = jax.nn.softmax(jnp.stack(lses), axis=0)
    out = jnp.einsum("gbsh,gbshd->bshd", wts, o)
    return out.reshape(B, S, DIL_OUT).astype(q.dtype)

def odd_mixer(h, w_in, lru_conv_w, lru_conv_b, lru_wa, lru_ba, lru_wx, lru_bx, lru_lam,
              q_norm_g, k_norm_g, w_out):
    z = h @ w_in
    lru_x, lru_gate, q, k, v = jnp.split(
        z, [LRU_WIDTH, 2 * LRU_WIDTH, 2 * LRU_WIDTH + DIL_QKV, 2 * LRU_WIDTH + 2 * DIL_QKV], axis=-1)
    xc = causal_dwconv_2(lru_x, lru_conv_w) + lru_conv_b
    y_lru = rg_lru(xc, lru_wa, lru_ba, lru_wx, lru_bx, lru_lam) * jax.nn.gelu(lru_gate)
    y_att = dilated_attention(q, k, v, q_norm_g, k_norm_g)
    return jnp.concatenate([y_lru, y_att], axis=-1) @ w_out

def conv_glu_ffn(h, w_gate, w_up, conv_w, conv_b, w_down):
    g = causal_dwconv_2(h @ w_gate, conv_w) + conv_b
    return (jax.nn.silu(g) * (h @ w_up)) @ w_down

def second_inputs(seed: int = 0) -> dict:
    key = jax.random.key(seed)
    ks = iter(jax.random.split(key, 40))
    f32 = jnp.float32

    def nrm(shape, fan_in):
        return jax.random.normal(next(ks), shape, f32) * (fan_in ** -0.5)

    def gain(shape):
        return 1.0 + 0.05 * jax.random.normal(next(ks), shape, f32)

    def bias(shape):
        return 0.01 * jax.random.normal(next(ks), shape, f32)

    u = jax.random.uniform(next(ks), (N_ODD, LRU_WIDTH), f32, minval=0.9, maxval=0.999)
    a0 = u ** (1.0 / LRU_C)
    lam = jnp.log(a0) - jnp.log1p(-a0)

    return {
        "x": jax.random.normal(next(ks), (BATCH, SEQ, D_MODEL), f32),
        "mix_norm_g": gain((DEPTH, D_MODEL)),
        "ffn_norm_g": gain((DEPTH, D_MODEL)),
        "ev_w_in": nrm((N_EVEN, D_MODEL, EV_IN), D_MODEL),
        "ev_sc_conv_w": nrm((N_EVEN, SC_WIDTH_CONV, SC_WIDTH), SC_WIDTH_CONV),
        "ev_cf_conv_w": nrm((N_EVEN, CF_WIDTH_CONV, CF_WIDTH), CF_WIDTH_CONV),
        "ev_cf_conv_b": bias((N_EVEN, CF_WIDTH)),
        "ev_cf_ln_g": gain((N_EVEN, CF_WIDTH)),
        "ev_cf_ln_b": bias((N_EVEN, CF_WIDTH)),
        "ev_w_out": nrm((N_EVEN, EV_OUT_IN, D_MODEL), EV_OUT_IN),
        "od_w_in": nrm((N_ODD, D_MODEL, OD_IN), D_MODEL),
        "od_lru_conv_w": nrm((N_ODD, LRU_CONV, LRU_WIDTH), LRU_CONV),
        "od_lru_conv_b": bias((N_ODD, LRU_WIDTH)),
        "od_lru_wa": nrm((N_ODD, LRU_HEADS, LRU_BLOCK, LRU_BLOCK), LRU_BLOCK),
        "od_lru_ba": bias((N_ODD, LRU_WIDTH)),
        "od_lru_wx": nrm((N_ODD, LRU_HEADS, LRU_BLOCK, LRU_BLOCK), LRU_BLOCK),
        "od_lru_bx": bias((N_ODD, LRU_WIDTH)),
        "od_lru_lam": lam,
        "od_q_norm_g": gain((N_ODD, DIL_HEAD_DIM)),
        "od_k_norm_g": gain((N_ODD, DIL_HEAD_DIM)),
        "od_w_out": nrm((N_ODD, OD_OUT_IN, D_MODEL), OD_OUT_IN),
        "ffn_w_gate": nrm((DEPTH, D_MODEL, D_FF), D_MODEL),
        "ffn_w_up": nrm((DEPTH, D_MODEL, D_FF), D_MODEL),
        "ffn_conv_w": nrm((DEPTH, FFN_CONV, D_FF), FFN_CONV),
        "ffn_conv_b": bias((DEPTH, D_FF)),
        "ffn_w_down": nrm((DEPTH, D_FF, D_MODEL), D_FF),
    }

def second_block(x, mix_norm_g, ffn_norm_g,
              ev_w_in, ev_sc_conv_w, ev_cf_conv_w, ev_cf_conv_b, ev_cf_ln_g, ev_cf_ln_b, ev_w_out,
              od_w_in, od_lru_conv_w, od_lru_conv_b, od_lru_wa, od_lru_ba, od_lru_wx, od_lru_bx,
              od_lru_lam, od_q_norm_g, od_k_norm_g, od_w_out,
              ffn_w_gate, ffn_w_up, ffn_conv_w, ffn_conv_b, ffn_w_down):
    for layer in range(DEPTH):
        j = layer // 2
        h = rmsnorm(x, mix_norm_g[layer])
        if layer % 2 == 0:
            x = x + even_mixer(h, ev_w_in[j], ev_sc_conv_w[j], ev_cf_conv_w[j], ev_cf_conv_b[j],
                               ev_cf_ln_g[j], ev_cf_ln_b[j], ev_w_out[j])
        else:
            x = x + odd_mixer(h, od_w_in[j], od_lru_conv_w[j], od_lru_conv_b[j], od_lru_wa[j],
                              od_lru_ba[j], od_lru_wx[j], od_lru_bx[j], od_lru_lam[j],
                              od_q_norm_g[j], od_k_norm_g[j], od_w_out[j])
        h = rmsnorm(x, ffn_norm_g[layer])
        x = x + conv_glu_ffn(h, ffn_w_gate[layer], ffn_w_up[layer], ffn_conv_w[layer],
                             ffn_conv_b[layer], ffn_w_down[layer])
    return x


def setup_inputs(seed=0):
    out = dict(first_inputs(seed))
    for name, value in second_inputs(seed + 1).items():
        if name != "x":
            out[name + "_2"] = value
    return out


def reference(
    x, ffa_norm, ffa_w_in, ffa_w_out, mix_norm, w_in, mla_cq_norm, mla_ckv_norm, mla_w_uq,
    mla_w_ukv, mla_q_norm, mla_k_norm, gdn_conv, gdn_a_log, gdn_dt_bias, gdn_out_norm,
    moba_q_norm, moba_k_norm, w_branch, w_out, ffb_norm, ffb_w_in, ffb_w_out, mix_norm_g_2,
    ffn_norm_g_2, ev_w_in_2, ev_sc_conv_w_2, ev_cf_conv_w_2, ev_cf_conv_b_2, ev_cf_ln_g_2,
    ev_cf_ln_b_2, ev_w_out_2, od_w_in_2, od_lru_conv_w_2, od_lru_conv_b_2, od_lru_wa_2,
    od_lru_ba_2, od_lru_wx_2, od_lru_bx_2, od_lru_lam_2, od_q_norm_g_2, od_k_norm_g_2,
    od_w_out_2, ffn_w_gate_2, ffn_w_up_2, ffn_conv_w_2, ffn_conv_b_2, ffn_w_down_2,
):
    x = first_block(
        x, ffa_norm, ffa_w_in, ffa_w_out, mix_norm, w_in, mla_cq_norm, mla_ckv_norm, mla_w_uq,
        mla_w_ukv, mla_q_norm, mla_k_norm, gdn_conv, gdn_a_log, gdn_dt_bias, gdn_out_norm,
        moba_q_norm, moba_k_norm, w_branch, w_out, ffb_norm, ffb_w_in, ffb_w_out,
    )
    return second_block(
        x, mix_norm_g_2, ffn_norm_g_2, ev_w_in_2, ev_sc_conv_w_2, ev_cf_conv_w_2,
        ev_cf_conv_b_2, ev_cf_ln_g_2, ev_cf_ln_b_2, ev_w_out_2, od_w_in_2, od_lru_conv_w_2,
        od_lru_conv_b_2, od_lru_wa_2, od_lru_ba_2, od_lru_wx_2, od_lru_bx_2, od_lru_lam_2,
        od_q_norm_g_2, od_k_norm_g_2, od_w_out_2, ffn_w_gate_2, ffn_w_up_2, ffn_conv_w_2,
        ffn_conv_b_2, ffn_w_down_2,
    )


_drawn_inputs = setup_inputs


def setup_inputs(seed=0):
    import zlib

    import numpy as np

    out = dict(_drawn_inputs(seed))
    spreads = {}
    factors = {'ffa_norm': 2.938,
     'mla_cq_norm': 8.0,
     'mla_ckv_norm': 8.0,
     'mla_q_norm': 8.0,
     'mla_k_norm': 8.0,
     'gdn_out_norm': 4.845,
     'moba_q_norm': 8.0,
     'moba_k_norm': 8.0,
     'ffb_norm': 3.761,
     'ev_cf_conv_b_2': 20.542,
     'ev_cf_ln_g_2': 21.388,
     'ev_cf_ln_b_2': 64.0,
     'od_lru_conv_b_2': 200.0,
     'od_lru_ba_2': 200.0,
     'od_lru_bx_2': 200.0,
     'od_q_norm_g_2': 143.672,
     'od_k_norm_g_2': 154.743,
     'ffn_conv_b_2': 64.0,
     'mix_norm_g_2': 2.86,
     'ffn_norm_g_2': 8.0,
     'od_lru_wa_2': 47.504,
     'od_lru_wx_2': 29.104,
     'od_lru_lam_2': 48.304,
     'od_lru_conv_w_2': 8.0}
    for name, (base, spread) in spreads.items():
        noise = np.random.default_rng([zlib.crc32(name.encode()), seed]).standard_normal(out[name].shape)
        drawn = base * np.exp(spread * noise) if base else spread * noise
        out[name] = jnp.asarray(drawn.astype(out[name].dtype))
    for name, factor in factors.items():
        out[name] = (out[name] * factor).astype(out[name].dtype)
    return out
```

```python
from contextlib import ExitStack

import numpy as np

import concourse.bass as bass
from concourse import mybir

F32 = mybir.dt.float32
F32R = mybir.dt.float32r
ACT = mybir.ActivationFunctionType
ALU = mybir.AluOpType
AX = mybir.AxisListType

PART = 128
TOK = 256
TT = TOK // PART
DM = 1024
KC = DM // PART
FF = 2816
FT = FF // PART
DEPTH = 2
EPS = 1e-6
NEG = -1e30
UC = 1024
RAW = 3
SLOTS = 6
AHEAD = SLOTS - 1

MH, MD = 8, 64
LH, LN, LR, LV = 8, 64, 32, 64
LD = LN + LR
QR, KVR = 256, 128
GH, GD, GK = 4, 128, 4
CFK, SCK = 31, 3
DG, DH, DD = 3, 4, 64
DW = DG * DH * DD
LK = 4
SMALL = QR + KVR + LR + 2 * GH
LEVELS = 7


def plan():
    at, n = {}, 0
    def run(name, count):
        nonlocal n
        at[name] = n
        n += count
    for l in range(DEPTH):
        run(("ffa", l), 3 * FT)
        run(("small", l), 4)
        run(("gdn", l), 12)
        run(("z", l), 4)
        run(("moba", l), 12)
        run(("gates_a", l), 8)
        run(("gates_b", l), 8)
        run(("up", l), 3)
        run(("gates_c", l), 8)
        run(("branch", l), 12)
        run(("out", l), 8)
        run(("ffb", l), 3 * FT)
    run("ev_in", 20)
    run("ev_out", 8)
    run(("ffn", 0), 3 * FT)
    run("lru_in", 8)
    run("dil_in", 18)
    run("od_out", 6)
    run(("ffn", 1), 3 * FT)
    at["end"] = n
    return at


AT = plan()
UNITS = AT["end"]
NORMS = 5 * DEPTH


def columns(items):
    at, n = {}, 0
    for name, width in items:
        at[name] = (n, n + width)
        n += width
    return at, n


HALVED, N_HALVED = columns(
    [(("gconv", l), 48) for l in range(DEPTH)] + [(("gout", l), 1) for l in range(DEPTH)]
    + [("cfconv", 4 * CFK), ("lng", 4), ("lnb", 4), ("lru_ba", 4), ("lru_bx", 4)]
    + [(("fconv", i), 4 * FT) for i in range(DEPTH)])
WHOLE, N_WHOLE = columns(
    [((n, l), 8) for n in ("ffa", "mix", "ffb", "mix2", "ffn2") for l in range(DEPTH)]
    + [(("cgain", l), 3) for l in range(DEPTH)]
    + [((n, l), w) for n, w in (("mlaq", LD), ("mlak", LD), ("mobaq", MD), ("mobak", MD), ("alog", GH), ("dtb", GH))
       for l in range(DEPTH)]
    + [("scconv", 12), ("cfbias", 4), ("lruconv", 16), ("lrubias", 4), ("lam", 4), ("dilq", DD), ("dilk", DD)])
CONST, N_CONST = columns(
    [("ident", 128), ("tri", 128), ("m0", 128), ("m0t", 128), ("mt", (LEVELS - 1) * 128), ("causal", 128),
     ("cosm", TT * 32), ("sinm", TT * 32), ("cosl", TT * 16), ("sinl", TT * 16)])
LATE, N_LATE = columns([("dneg", 9 * 128), ("wa", 512), ("wx", 512)])


def constants():
    out, late = np.zeros((PART, N_CONST), np.float32), np.zeros((PART, N_LATE), np.float32)
    i, j = np.arange(128)[:, None], np.arange(128)[None, :]

    def put(name, a):
        lo, hi = CONST[name]
        out[:, lo:hi] = a.reshape(128, hi - lo)

    put("ident", (i == j).astype(np.float32))
    put("tri", (i <= j).astype(np.float32))
    masks = []
    for m in range(LEVELS):
        s = 1 << m
        masks.append(((i // (2 * s) == j // (2 * s)) & ((i // s) % 2 == 1) & ((j // s) % 2 == 0)).astype(np.float32))
    put("m0", masks[0])
    put("m0t", masks[0].T)
    put("mt", np.stack([m.T for m in masks[1:]], 1))
    causal = j <= i
    neg = []
    for step, band in ((1, j >= i), (4, (i - j) % 4 == 0), (16, (i - j) % 16 == 0)):
        same = causal & ((i - j) % step == 0)
        neg += [same, band, same]
    put("causal", np.where(causal, 0.0, NEG).astype(np.float32))
    lo, hi = LATE["dneg"]
    late[:, lo:hi] = np.stack([np.where(m, 0.0, NEG).astype(np.float32) for m in neg], 1).reshape(128, hi - lo)
    for half, c, s in ((32, "cosm", "sinm"), (16, "cosl", "sinl")):
        inv = np.float32(10000.0) ** (-np.arange(half, dtype=np.float32) * np.float32(2.0) / np.float32(2 * half))
        ang = np.arange(TOK, dtype=np.float32)[:, None] * inv[None].astype(np.float32)
        for name, f in ((c, np.cos), (s, np.sin)):
            put(name, f(ang).astype(np.float32).reshape(TT, 128, half).transpose(1, 0, 2))
    return out, late


class Events:

    def __init__(self, sem, steps):
        self.sem, self.steps, self.done = sem, {s: n for n, s in enumerate(steps)}, 0

    def at(self, l, step):
        return self.sem, l * len(self.steps) + self.steps[step] + 1

    def sig(self, l, step):
        self.done += 1
        assert self.at(l, step)[1] == self.done, (l, step)
        return self.sem, 1


LV_STEPS = [(k, m, t) for m in range(1, LEVELS) for k, t in (("U", 0), ("U", 1), ("X", 0), ("T", 0), ("X", 1), ("T", 1))
            if not (m == LEVELS - 1 and k == "X")]
PE_STEPS = (["cums", "R", "stat", "bc", "ktok", "vtok", "G", "QK", "AT", "QKT"] + LV_STEPS
            + ["u", "wT", "S1", "ob0", "wS", "oa", "ob1", "oT", "mobaT", "cT", "mlaTq", "mlaTk"])
DVE_STEPS = (["z0", "silu", "g", "tg", "cumcp", "gld", "Et", "gvar", "diag", "qn", "kn", "kgd", "vb", "A", "QK", "X0", "XT0"]
             + [s for s in LV_STEPS if s[0] != "U"]
             + ["vn0", "S1", "tq", "vn1", "O1", "ovar", "on", "oz", "oz_lo", "mobavar", "mobaqk", "cvar", "cn", "c32", "c_lo",
                "kr", "mlavar", "mlaqk"])
ACT_STEPS = (["sm", "spe", "gsq", "egc", "kds", "E", "AT", "QKT"] + [s for s in LV_STEPS if s[0] == "U"]
             + ["u1", "wT", "O0", "osq", "oz_hi", "mobasq", "mobaT", "csq", "c_hi", "up", "mlasq", "mlaTq", "mlaTk"])
POOL_STEPS = (["grs"] + [("ATM", m) for m in range(1, LEVELS)] + ["ors", "mobars", "crs", "mlars"])

PE2_STEPS = ["mean", "lnstat", "lnbc", "r", "i", "dilT"]
DVE2_STEPS = ["cf", "cen", "lnvar", "lndiag", "yb", "o2", "o2_lo", "lamz", "xc", "sp4", "m2", "gin", "ylru", "ylru_lo",
              "dvar", "dqk"]
ACT2_STEPS = ["lnsq", "lnth", "o2_hi", "spe", "lgsq", "rth", "ith", "a", "tq", "mult", "gth", "ylru_hi", "dsq", "dilT"]
POOL2_STEPS = ["lnrs", "drs"]


def build(nc, stream, params, consts, late_in, x_in, out):
    with ExitStack() as ctx:
        def sb(name, shape, dt=F32):
            return ctx.enter_context(nc.sbuf_tensor(name, shape, dt))

        def sem(name):
            return ctx.enter_context(nc.semaphore(name))

        raw = sb("raw", [PART, RAW, UC])
        w_hi = sb("w_hi", [PART, SLOTS, UC], F32R)
        w_lo = sb("w_lo", [PART, SLOTS, UC], F32R)
        x = sb("x", [PART, KC, TOK])
        tmp = sb("tmp", [PART, KC, TOK])
        a_hi = sb("a_hi", [PART, 20, TOK], F32R)
        a_lo = sb("a_lo", [PART, 20, TOK], F32R)
        par = sb("par", [PART, N_HALVED + N_WHOLE])
        con = sb("con", [PART, N_CONST])
        ones = sb("ones", [PART, PART])
        nhalf = sb("nhalf", [PART, 64])
        sc = sb("sc", [PART, 512])
        diag = sb("diag", [PART, TOK])
        gates = sb("gates", [PART, 24, TOK])
        arena = sb("arena", [PART, 13184])
        ps = ctx.enter_context(nc.psum_tensor("ps", [PART, 8, 512], F32))

        raw_loaded = [sem(f"raw_loaded{i}") for i in range(RAW)]
        params_loaded, x_loaded, stored = sem("params_loaded"), sem("x_loaded"), sem("stored")
        consts_set, halved = sem("consts_set"), sem("halved")
        hi_ready, split_ready, unit_used = sem("hi_ready"), sem("split_ready"), sem("unit_used")
        x_ready, sq_ready, stat_ready, var_ready = sem("x_ready"), sem("sq_ready"), sem("stat_ready"), sem("var_ready")
        rs_ready, diag_ready, bc_ready = sem("rs_ready"), sem("diag_ready"), sem("bc_ready")
        hn_ready, h_hi_ready, h_ready = sem("hn_ready"), sem("h_hi_ready"), sem("h_ready")
        gate_act, gu_ready, gu_hi_ready, gu_split = sem("gate_act"), sem("gu_ready"), sem("gu_hi_ready"), sem("gu_split")
        conv_in, conv_used = sem("conv_in"), sem("conv_used")
        dve_chain, act_chain, pool_chain = sem("dve_chain"), sem("act_chain"), sem("pool_chain")
        loop_chain = sem("loop_chain")
        cb_ready, conv_ready, silu_th = sem("cb_ready"), sem("conv_ready"), sem("silu_th")
        z_th, zs_ready, m_ready, gate_evac = sem("z_th"), sem("zs_ready"), sem("m_ready"), sem("gate_evac")
        scores_ready, nmax_ready, exp_done, p_ready = sem("scores_ready"), sem("nmax_ready"), sem("exp_done"), sem("p_ready")
        pt_ps, pt_ready, o_ready, o_hi, o_split = sem("pt_ps"), sem("pt_ready"), sem("o_ready"), sem("o_hi"), sem("o_split")
        merge_read, mix_ready, mix_hi, mix_split = sem("merge_read"), sem("mix_ready"), sem("mix_hi"), sem("mix_split")
        pe_ev = [Events(sem("pe_step"), PE_STEPS)]
        dve_ev = [Events(sem("dve_step"), DVE_STEPS)]
        act_ev = [Events(sem("act_step"), ACT_STEPS)]
        pool_ev = [Events(sem("pool_step"), POOL_STEPS)]
        PE, DV, AC, PO = pe_ev[0], dve_ev[0], act_ev[0], pool_ev[0]
        PE2, DV2 = Events(sem("pe_step2"), PE2_STEPS), Events(sem("dve_step2"), DVE2_STEPS)
        AC2, PO2 = Events(sem("act_step2"), ACT2_STEPS), Events(sem("pool_step2"), POOL2_STEPS)
        late_loaded, loop_chain2 = sem("late_loaded"), sem("loop_chain2")
        cf_th, sc_copy, pair_read, b_read = sem("cf_th"), sem("sc_copy"), sem("pair_read"), sem("b_read")
        lru_copy, dil_copy = sem("lru_copy"), sem("dil_copy")
        d_scores, d_nmax, d_exp, d_p = sem("d_scores"), sem("d_nmax"), sem("d_exp"), sem("d_p")
        d_ptps, d_pt, d_o, d_hi, d_lo = sem("d_ptps"), sem("d_pt"), sem("d_o"), sem("d_hi"), sem("d_lo")

        def half(name, i=0, n=1):
            lo, _ = HALVED[name]
            return par[:, lo + i:lo + i + n]

        def whole(name, i=0, n=1):
            lo, _ = WHOLE[name]
            return par[:, N_HALVED + lo + i:N_HALVED + lo + i + n]

        def const(name, i=0, n=None):
            lo, hi = CONST[name]
            return con[:, lo + i:(hi if n is None else lo + i + n)]

        ident = const("ident")

        def bank(b, lo=0, hi=512):
            return ps[:, b, lo:hi]

        def flat(ap):
            return ap.rearrange("p a b -> p (a b)")

        def over(ap, n):
            return ap.unsqueeze(2).broadcast_to([PART, ap.shape[1], n])

        def each(ap, n):
            return ap.unsqueeze(1).broadcast_to([PART, n, ap.shape[1]])

        def reg(lo, *dims):
            n = int(np.prod(dims))
            v = arena[:, lo:lo + n]
            return v if len(dims) == 1 else v.rearrange("p (a b) -> p a b", b=dims[-1])

        gup = gates[:, 8:24, :].rearrange("p a b -> p (a b)")
        mqkv = reg(0, 6, 512)
        zs = reg(3072, 4, TOK)
        y = reg(4096, 12, TOK)
        yth = reg(7168, 12, TOK)
        X = reg(7168, 8, 128)
        XT = reg(8192, 8, 128)
        tg = reg(7168, 8, 128)
        vb = reg(9216, 8, 128)
        kgd = reg(10240, 8, 128)
        O = reg(11264, 8, 128)
        small = reg(12288, TT, SMALL)
        cb = gup[:, 0:12 * (TOK + 3)].rearrange("p (a b) -> p a b", b=TOK + 3)
        E = gup[:, 0:1024].rearrange("p (a b) -> p a b", b=128)
        QKT = E
        A = gup[:, 1024:2048].rearrange("p (a b) -> p a b", b=128)
        U = A
        QK = gup[:, 2048:3072].rearrange("p (a b) -> p a b", b=128)
        VN = QK
        ATr = gup[:, 3072:4096].rearrange("p (a b) -> p a b", b=128)
        S1 = gup[:, 1024:1536]
        wT = gup[:, 1536:2048]
        tmpf = flat(tmp[:, :, :])
        ATM = [tmpf[:, 0:1024].rearrange("p (a b) -> p a b", b=128), tmpf[:, 1024:2048].rearrange("p (a b) -> p a b", b=128)]
        diag16 = tmpf.rearrange("p (a b) -> p a b", b=128)
        qTm, kTm = reg(3072, 4, TOK), reg(4096, 4, TOK)
        rA, rB = reg(6144, 1536), reg(7680, 1536)
        Pb = [reg(9216, 384), reg(9600, 384)]
        PTb = [reg(9984, 384), reg(10368, 384)]
        ql, kl = reg(0, 16, LD), reg(1536, 16, LD)
        vl = reg(3072, TT, 512)
        cn = reg(4096, TT, QR + KVR)
        c32 = reg(4864, 3, TOK)
        qTl = arena[0:LD, 6144:8192].rearrange("p (a b) -> p a b", b=TOK)
        kTl = tmp[0:LD, :, :]
        th2, a2, gu2 = reg(0, 2, TOK), reg(512, 2, TOK), reg(1024, 2, TOK)
        mA, mB = reg(0, 2, 512), reg(1024, 512)
        gh2 = reg(1536, 2, TOK)
        F2 = 2 * DEPTH * FT
        gflat = gates[:, :, :].rearrange("p a b -> p (a b)")
        late = gflat[:, 0:N_LATE]
        dneg = late[:, 0:9 * 128].rearrange("p (a b) -> p a b", b=3 * 128)
        gr = lambda lo, *d: (gflat[:, lo:lo + int(np.prod(d))] if len(d) == 1 else
                             gflat[:, lo:lo + int(np.prod(d))].rearrange("p (a b) -> p a b", b=d[-1]))
        ub = reg(0, 4, TOK + CFK - 1)
        cf = reg(1152, 4, TOK)
        cx = reg(2304, 4, TOK + SCK - 1)
        csb = reg(3400, 4, TOK)
        ysc = reg(4500, 4, TOK)
        o2 = reg(5600, 8, TOK)
        lnth = reg(7700, 4, TOK)
        lx = reg(0, 4, TOK + LK - 1)
        lg = reg(1040, 4, TOK)
        xc = reg(2064, 4, TOK)
        qkv = reg(3088, TT, 3 * DW)
        Pd = [reg(7696, 3, 384), reg(8848, 3, 384)]
        PTd = [reg(10000, 3, 384), reg(11152, 3, 384)]
        dsq = arena[:, 7696:7696 + 2 * 2 * DW].rearrange("p (a b) -> p a b", b=2 * DW)
        qTd, kTd = reg(0, 6, TOK), reg(1536, 6, TOK)
        thr, thi, aa = gr(2200, 4, TOK), gr(3224, 4, TOK), gr(4248, 4, TOK)
        tqb, recb = tmp[:, 0:4, :], tmp[:, 4:8, :]

        block = ctx.enter_context(nc.Block())

        @block.sync
        def _(sp):
            sp.dma_start(x[:], x_in).then_inc(x_loaded, 16)
            for b in range(RAW):
                sp.dma_start(raw[:, b, :], stream[b]).then_inc(raw_loaded[b], 16)
            sp.dma_start(par[:], params).then_inc(params_loaded, 16)
            sp.dma_start(con[:], consts).then_inc(params_loaded, 16)
            rounds = (UNITS - RAW) // RAW
            with sp.Fori(0, rounds) as r:
                for b in range(RAW):
                    sp.wait_ge(split_ready, RAW * r + b + 1)
                    sp.dma_start(raw[:, b, :], stream[bass.ds(RAW * r + RAW + b, 1)].rearrange("o p n -> (o p) n")
                                 ).then_inc(raw_loaded[b], 16)
            for u in range(RAW + rounds * RAW, UNITS):
                sp.wait_ge(split_ready, u - RAW + 1)
                sp.dma_start(raw[:, u % RAW, :], stream[u]).then_inc(raw_loaded[u % RAW], 16)
            for c in range(KC):
                sp.wait_ge(x_ready, 8 * (NORMS - 1) + c + 1)
                sp.dma_start(out[:, c, :], x[:, c, :]).then_inc(stored, 16)
            sp.wait_ge(stored, 16 * KC)
            sp.wait_ge(late_loaded, 16)

        @block.scalar
        def _(act):
            chain = [0]

            def link(ins):
                chain[0] += 1
                ins.then_inc(act_chain, 1)
                act.wait_ge(act_chain, chain[0])

            def split(u, j=0):
                if u >= UNITS:
                    return
                act.wait_ge(raw_loaded[u % RAW], 16 * (u // RAW + 1 + 2 * j))
                if u >= SLOTS:
                    act.wait_ge(unit_used, u - SLOTS + 1 + 6 * j)
                nc.scalar.activation(w_hi[:, u % SLOTS, :], raw[:, u % RAW, :], ACT.Copy).then_inc(hi_ready, 1)

            def norm(t, first_unit_end):
                for c in range(KC):
                    if t == 0:
                        if c == 0:
                            act.wait_ge(x_loaded, 16)
                    else:
                        act.wait_ge(x_ready, 8 * (t - 1) + c + 1)
                    nc.scalar.activation(tmp[:, c, :], x[:, c, :], ACT.Square).then_inc(sq_ready, 1)
                for c in range(KC):
                    act.wait_ge(hn_ready, 8 * t + c + 1)
                    nc.scalar.activation(a_hi[:, c, :], tmp[:, c, :], ACT.Copy).then_inc(h_hi_ready, 1)

            def gating(F, p, u_end, j=0):
                act.wait_ge(unit_used, u_end + 6 * j)
                nc.scalar.activation(th2[:, p, :], bank(4 + p, 0, TOK), ACT.Tanh, scale=0.5).then_inc(gate_act, 1)

            def gu_high(F, p, j=0):
                act.wait_ge(gu_ready, F + 1 + 2 * j)
                nc.scalar.activation(a_hi[:, 8 + p, :], gu2[:, p, :], ACT.Copy).then_inc(gu_hi_ready, 1)

            def ffn(n0, F0, gate):
                split(n0 + AHEAD); split(n0 + 1 + AHEAD)
                gate(F0, 0, n0 + 2)
                gu_high(F0, 0)
                def tile(f, u, j=0):
                    split(u + AHEAD, j); split(u + 1 + AHEAD, j)
                    gate(F0 + f, f % 2, u + 2, j)
                    split(u + 2 + AHEAD, j)
                    gu_high(F0 + f, f % 2, j)
                last = int(n0 + 3 * FT == UNITS)
                with act.Fori(0, (FT - 2) // 2 - last) as j:
                    tile(1, n0 + 2, j)
                    tile(2, n0 + 5, j)
                for f in range(FT - 1 - 2 * last, FT):
                    tile(f, n0 + 3 * f - 1)
                split(n0 + 3 * FT - 1 + AHEAD)

            def gate_tile(l, i):
                u = AT["gates_" + "abc"[i // 8], l] + i % 8
                act.wait_ge(unit_used, u + 1)
                nc.scalar.activation(gates[:, i, :], bank(6 + i % 2, 0, TOK), ACT.Tanh, scale=0.5).then_inc(gate_evac, 1)

            def exp_scores(n, scale):
                p = n % 2
                act.wait_ge(nmax_ready, n + 1)
                s = sc[:, 8 + 4 * p:12 + 4 * p]
                nc.scalar.activation(Pb[p][:, 0:128], bank(p, 0, 128), ACT.Exp, bias=s[:, 0:1], scale=scale,
                                     accum_out=s[:, 2:3])
                nc.scalar.activation(Pb[p][:, 128:384], bank(p, 128, 384), ACT.Exp, bias=s[:, 1:2], scale=scale,
                                     accum_out=s[:, 3:4]).then_inc(exp_done, 1)

            def evac_pt(n):
                act.wait_ge(pt_ps, n + 1)
                nc.scalar.activation(PTb[n % 2], bank(2 + n % 2, 0, 384), ACT.Copy).then_inc(pt_ready, 1)

            def o_high(pair, chunk):
                act.wait_ge(o_ready, pair + 1)
                nc.scalar.activation(a_hi[:, chunk, :], bank(4 + pair % 2, 0, TOK), ACT.Copy).then_inc(o_hi, 1)

            def attention(l, kind, g0, scale, chunk):
                n0 = 16 * l + 8 * kind
                for n in range(8):
                    split(AT["gates_" + "abc"[g0 // 8], l] + n + AHEAD)
                    exp_scores(n0 + n, scale)
                    gate_tile(l, g0 + n)
                    evac_pt(n0 + n)
                    if n % 2 == 0 and n:
                        o_high(8 * l + 4 * kind + n // 2 - 1, chunk + n // 2 - 1)
                o_high(8 * l + 4 * kind + 3, chunk + 3)

            def mixer(l):
                a = sc[:, 32:40].rearrange("p (a b) -> p a b", b=4)
                for i in range(4):
                    split(AT["small", l] + i + AHEAD)
                act.wait_ge(unit_used, AT["small", l] + 4)
                nc.scalar.activation(small, ps[:, 0:2, 0:SMALL], ACT.Copy).then_inc(*AC.sig(l, "sm"))
                act.wait_ge(*AC.at(l, "sm"))
                nc.scalar.activation(sc[:, 40:48].rearrange("p (a b) -> p a b", b=4), small[:, :, 416:420], ACT.Tanh, scale=0.5)
                act.wait_ge(*DV.at(l, "z0"))
                link(nc.scalar.activation(sc[:, 48:56], sc[:, 32:40], ACT.Abs))
                nc.scalar.activation(sc[:, 56:60], whole(("alog", l), 0, 4), ACT.Exp)
                nc.scalar.activation(sc[:, 64:72], sc[:, 48:56], ACT.Exp, scale=-1.0).then_inc(*AC.sig(l, "spe"))
                def th(p):
                    act.wait_ge(conv_ready, 6 * l + p + 1)
                    nc.scalar.activation(yth[:, 2 * p:2 * p + 2, :], y[:, 2 * p:2 * p + 2, :], ACT.Tanh).then_inc(silu_th, 1)
                for p in range(6):
                    u = AT["gdn", l] + 2 * p
                    split(u + AHEAD); split(u + 1 + AHEAD)
                    act.wait_ge(unit_used, u + 2)
                    nc.scalar.activation(cb[:, 2 * p:2 * p + 2, 3:], bank((2 + p) % 6).rearrange("p (a b) -> p a b", b=TOK),
                                         ACT.Copy).then_inc(cb_ready, 1)
                    if p:
                        th(p - 1)
                for q in range(2):
                    u = AT["z", l] + 2 * q
                    split(u + AHEAD); split(u + 1 + AHEAD)
                    if q == 0:
                        th(5)
                    act.wait_ge(unit_used, u + 2)
                    nc.scalar.activation(flat(zs[:, 2 * q:2 * q + 2, :]), bank(6 + q), ACT.Tanh, scale=0.5).then_inc(z_th, 1)
                act.wait_ge(*DV.at(l, "silu"))
                nc.scalar.activation(flat(tmp[:, :, :]), flat(y[:, 0:8, :]), ACT.Square).then_inc(*AC.sig(l, "gsq"))
                for g in range(3):
                    for i in range(4):
                        split(AT["moba", l] + 4 * g + i + AHEAD)
                    act.wait_ge(unit_used, AT["moba", l] + 4 * g + 4)
                    b = (2, 4, 0)[g]
                    nc.scalar.activation(mqkv[:, 2 * g:2 * g + 2, :], ps[:, b:b + 2, :], ACT.Copy).then_inc(m_ready, 1)
                act.wait_ge(*DV.at(l, "cumcp"))
                nc.scalar.activation(sc[:, 88:96], sc[:, 72:80], ACT.Exp).then_inc(*AC.sig(l, "egc"))
                act.wait_ge(*DV.at(l, "gld"))
                nc.scalar.activation(sc[:, 100:104], sc[:, 96:100], ACT.Exp).then_inc(*AC.sig(l, "kds"))
                act.wait_ge(*DV.at(l, "Et"))
                for b in range(8):
                    e = nc.scalar.activation(E[:, b, :], E[:, b, :], ACT.Exp, bias=sc[:, 72 + b:73 + b])
                e.then_inc(*AC.sig(l, "E"))
                split(AT["gates_a", l] + AHEAD); gate_tile(l, 0)
                split(AT["gates_a", l] + 1 + AHEAD); gate_tile(l, 1)
                act.wait_ge(*PE.at(l, "AT"))
                nc.scalar.activation(ATr, ps[:, 0:2, :], ACT.Copy).then_inc(*AC.sig(l, "AT"))
                act.wait_ge(*PE.at(l, "QKT"))
                nc.scalar.activation(QKT, ps[:, 2:4, :], ACT.Copy).then_inc(*AC.sig(l, "QKT"))
                for m in range(1, LEVELS):
                    split(AT["gates_a", l] + 1 + m + AHEAD)
                    for t in range(2):
                        act.wait_ge(*PE.at(l, ("U", m, t)))
                        nc.scalar.activation(U[:, 4 * t:4 * t + 4, :], bank(t).rearrange("p (a b) -> p a b", b=128),
                                             ACT.Copy).then_inc(*AC.sig(l, ("U", m, t)))
                    gate_tile(l, 1 + m)
                act.wait_ge(*PE.at(l, "u"))
                nc.scalar.activation(O[:, 4:8, :], bank(1).rearrange("p (a b) -> p a b", b=128), ACT.Copy).then_inc(*AC.sig(l, "u1"))
                act.wait_ge(*PE.at(l, "wT"))
                nc.scalar.activation(wT, bank(2), ACT.Copy).then_inc(*AC.sig(l, "wT"))
                act.wait_ge(*PE.at(l, "ob0"))
                nc.scalar.activation(O[:, 0:4, :], bank(2).rearrange("p (a b) -> p a b", b=128), ACT.Copy).then_inc(*AC.sig(l, "O0"))
                act.wait_ge(*AC.at(l, "O0"))
                act.wait_ge(*DV.at(l, "O1"))
                nc.scalar.activation(ATM[0], O, ACT.Square).then_inc(*AC.sig(l, "osq"))
                act.wait_ge(*DV.at(l, "oz"))
                nc.scalar.activation(a_hi[:, 12:16, :], reg(8192, 4, TOK), ACT.Copy).then_inc(*AC.sig(l, "oz_hi"))
                act.wait_ge(m_ready, 3 * l + 3)
                act.wait_ge(*DV.at(l, "oz_lo"))
                nc.scalar.activation(rA[:, 0:1024], flat(mqkv[:, 0:2, :]), ACT.Square)
                nc.scalar.activation(rB[:, 0:1024], flat(mqkv[:, 2:4, :]), ACT.Square).then_inc(*AC.sig(l, "mobasq"))
                act.wait_ge(*PE.at(l, "mobaT"))
                nc.scalar.activation(flat(qTm), ps[:, 0:2, :], ACT.Copy)
                nc.scalar.activation(flat(kTm), ps[:, 2:4, :], ACT.Copy).then_inc(*AC.sig(l, "mobaT"))
                attention(l, 0, 8, MD ** -0.5, 16)
                nc.scalar.activation(rA[:, 0:768].rearrange("p (a b) -> p a b", b=384), small[:, :, 0:384], ACT.Square
                                     ).then_inc(*AC.sig(l, "csq"))
                act.wait_ge(*DV.at(l, "c32"))
                nc.scalar.activation(a_hi[:, 8:11, :], c32, ACT.Copy).then_inc(*AC.sig(l, "c_hi"))
                for i in range(3):
                    split(AT["up", l] + i + AHEAD)
                act.wait_ge(unit_used, AT["up", l] + 3)
                qv = ql.rearrange("p (j h) d -> p j (h d)", j=TT)
                for j in range(TT):
                    nc.scalar.activation(qv[:, j, 0:512], bank(j), ACT.Copy)
                nc.scalar.activation(qv[:, :, 512:768], bank(2).rearrange("p (j n) -> p j n", j=TT), ACT.Copy)
                for j in range(TT):
                    nc.scalar.activation(kl[:, 8 * j:8 * j + 8, 0:LN], bank(3 + j).rearrange("p (h d) -> p h d", d=LN), ACT.Copy)
                nc.scalar.activation(vl, ps[:, 5:7, :], ACT.Copy).then_inc(*AC.sig(l, "up"))
                act.wait_ge(*DV.at(l, "kr"))
                nc.scalar.activation(rA, flat(ql), ACT.Square)
                nc.scalar.activation(rB, flat(kl), ACT.Square).then_inc(*AC.sig(l, "mlasq"))
                act.wait_ge(*PE.at(l, "mlaTq"))
                nc.scalar.activation(qTl, ps[0:LD, 0:4, :], ACT.Copy).then_inc(*AC.sig(l, "mlaTq"))
                act.wait_ge(*PE.at(l, "mlaTk"))
                nc.scalar.activation(kTl, ps[0:LD, 0:4, :], ACT.Copy).then_inc(*AC.sig(l, "mlaTk"))
                attention(l, 1, 16, LD ** -0.5, 8)
                for i in range(12):
                    split(AT["branch", l] + i + AHEAD)
                    if i % 3 == 0 and i:
                        mix_high(l, i // 3 - 1)
                mix_high(l, 3)
                for k in range(KC):
                    split(AT["out", l] + k + AHEAD)

            def mix_high(l, dp):
                act.wait_ge(mix_ready, 4 * l + dp + 1)
                nc.scalar.activation(flat(a_hi[:, 2 * dp:2 * dp + 2, :]), mA[:, dp % 2, :], ACT.Copy).then_inc(mix_hi, 1)

            def gating2(F, p, u_end, j=0):
                lo = HALVED["fconv", (F - F2) // FT][0] + 4 * ((F - F2) % FT)
                w = par[:, lo + 2:lo + 3] if isinstance(j, int) else par[:, bass.ds(lo + 2 + 8 * j, 1)]
                b = par[:, lo + 3:lo + 4] if isinstance(j, int) else par[:, bass.ds(lo + 3 + 8 * j, 1)]
                act.wait_ge(unit_used, u_end + 6 * j)
                nc.scalar.activation(gh2[:, p, :], bank(4 + p, 0, TOK), ACT.Identity, scale=w, bias=b).then_inc(conv_in, 1)
                act.wait_ge(conv_used, F - F2 + 1 + 2 * j)
                nc.scalar.activation(th2[:, p, :], gh2[:, p, :], ACT.Tanh).then_inc(gate_act, 1)

            def even():
                n0 = AT["ev_in"]
                for i in range(4):
                    split(n0 + 2 * i + AHEAD); split(n0 + 2 * i + 1 + AHEAD)
                    act.wait_ge(unit_used, n0 + 2 * i + 2)
                    nc.scalar.activation(lnth[:, i, :], bank(i, TOK, 512), ACT.Tanh, scale=0.5).then_inc(cf_th, 1)
                for i in range(4):
                    u = n0 + 8 + 2 * i
                    split(u + AHEAD); split(u + 1 + AHEAD)
                    act.wait_ge(unit_used, u + 2)
                    nc.scalar.activation(csb[:, i, :], bank((4, 5, 0, 1)[i], 0, TOK), ACT.Copy).then_inc(sc_copy, 1)
                for i in range(4):
                    split(n0 + 16 + i + AHEAD)
                act.wait_ge(*DV2.at(0, "cen"))
                nc.scalar.activation(flat(tmp[:, 0:4, :]), flat(cf), ACT.Square).then_inc(*AC2.sig(0, "lnsq"))
                act.wait_ge(*DV2.at(0, "yb"))
                nc.scalar.activation(flat(lnth), flat(cf), ACT.Tanh).then_inc(*AC2.sig(0, "lnth"))
                act.wait_ge(*DV2.at(0, "o2"))
                nc.scalar.activation(a_hi[:, 8:16, :], o2, ACT.Copy).then_inc(*AC2.sig(0, "o2_hi"))
                for k in range(8):
                    split(AT["ev_out"] + k + AHEAD)

            def odd():
                n0 = AT["lru_in"]
                for q in range(4):
                    split(n0 + 2 * q + AHEAD); split(n0 + 2 * q + 1 + AHEAD)
                    act.wait_ge(unit_used, n0 + 2 * q + 2)
                    o = lx[:, 2 * q:2 * q + 2, LK - 1:] if q < 2 else lg[:, 2 * q - 4:2 * q - 2, :]
                    nc.scalar.activation(o, bank(q).rearrange("p (a b) -> p a b", b=TOK), ACT.Copy).then_inc(lru_copy, 1)
                act.wait_ge(*DV2.at(0, "lamz"))
                link(nc.scalar.activation(sc[:, 288:292], sc[:, 284:288], ACT.Abs))
                nc.scalar.activation(sc[:, 292:296], sc[:, 288:292], ACT.Exp, scale=-1.0).then_inc(*AC2.sig(0, "spe"))
                act.wait_ge(lru_copy, 4)
                nc.scalar.activation(recb, lg, ACT.Square).then_inc(*AC2.sig(0, "lgsq"))
                for g in range(5):
                    n = 4 if g < 4 else 2
                    for i in range(n):
                        split(AT["dil_in"] + 4 * g + i + AHEAD)
                    act.wait_ge(unit_used, AT["dil_in"] + 4 * g + n)
                    b, w = (4, 6, 0, 2, 4)[g], 128 * n
                    nc.scalar.activation(qkv[:, :, 512 * g:512 * g + w], ps[:, b:b + 2, 0:w], ACT.Copy).then_inc(dil_copy, 1)
                act.wait_ge(*PE2.at(0, "r"))
                for i in range(4):
                    q = nc.scalar.activation(thr[:, i, :], bank(6 + i // 2, (i % 2) * TOK, (i % 2 + 1) * TOK), ACT.Tanh,
                                             scale=0.5, bias=half("lru_ba", i))
                q.then_inc(*AC2.sig(0, "rth"))
                act.wait_ge(*PE2.at(0, "i"))
                for i in range(4):
                    q = nc.scalar.activation(thi[:, i, :], bank(i // 2, (i % 2) * TOK, (i % 2 + 1) * TOK), ACT.Tanh,
                                             scale=0.5, bias=half("lru_bx", i))
                q.then_inc(*AC2.sig(0, "ith"))
                act.wait_ge(*AC2.at(0, "rth"))
                act.wait_ge(*DV2.at(0, "sp4"))
                for i in range(4):
                    k = sc[:, 296 + i:297 + i]
                    q = nc.scalar.activation(aa[:, i, :], thr[:, i, :], ACT.Exp, scale=k, bias=k)
                q.then_inc(*AC2.sig(0, "a"))
                for i in range(4):
                    k = sc[:, 296 + i:297 + i]
                    q = nc.scalar.activation(tqb[:, i, :], thr[:, i, :], ACT.Tanh, scale=k, bias=k)
                q.then_inc(*AC2.sig(0, "tq"))
                act.wait_ge(*DV2.at(0, "m2"))
                nc.scalar.activation(thr, recb, ACT.Sqrt).then_inc(*AC2.sig(0, "mult"))
                act.wait_ge(*DV2.at(0, "gin"))
                nc.scalar.activation(tqb, recb, ACT.Tanh, scale=0.7978845608028654).then_inc(*AC2.sig(0, "gth"))
                act.wait_ge(*DV2.at(0, "ylru"))
                nc.scalar.activation(a_hi[:, 8:12, :], thi, ACT.Copy).then_inc(*AC2.sig(0, "ylru_hi"))
                act.wait_ge(dil_copy, 5)
                nc.scalar.activation(dsq, qkv[:, :, 0:2 * DW], ACT.Square).then_inc(*AC2.sig(0, "dsq"))
                act.wait_ge(*PE2.at(0, "dilT"))
                nc.scalar.activation(flat(qTd), ps[:, 0:3, :], ACT.Copy)
                nc.scalar.activation(flat(kTd), ps[:, 3:6, :], ACT.Copy).then_inc(*AC2.sig(0, "dilT"))
                for h in range(DH):
                    p = h % 2
                    act.wait_ge(d_nmax, h + 1)
                    s = sc[:, 304 + 16 * p:320 + 16 * p]
                    for g in range(DG):
                        nc.scalar.activation(Pd[p][:, g, 0:128], bank(3 * p + g, 0, 128), ACT.Exp, bias=s[:, 0:1],
                                             scale=DD ** -0.5, accum_out=s[:, 2 + g:3 + g])
                        q = nc.scalar.activation(Pd[p][:, g, 128:384], bank(3 * p + g, 128, 384), ACT.Exp, bias=s[:, 1:2],
                                                 scale=DD ** -0.5, accum_out=s[:, 5 + g:6 + g])
                    q.then_inc(d_exp, 1)
                    if h:
                        d_turned(h - 1)
                    if h == 3:
                        d_high(0)
                d_turned(3)
                d_high(1)
                for k in range(6):
                    split(AT["od_out"] + k + AHEAD)

            def d_turned(h):
                act.wait_ge(d_ptps, h + 1)
                nc.scalar.activation(PTd[h % 2], ps[:, 3 * (h % 2):3 * (h % 2) + 3, 0:384], ACT.Copy).then_inc(d_pt, 1)

            def d_high(pair):
                act.wait_ge(d_o, pair + 1)
                nc.scalar.activation(a_hi[:, 12 + pair, :], bank(6 + pair, 0, TOK), ACT.Copy).then_inc(d_hi, 1)

            for u in range(AHEAD):
                split(u)
            t, F = 0, 0
            for l in range(DEPTH):
                norm(t, 0); t += 1
                ffn(AT["ffa", l], F, gating); F += FT
                norm(t, 0); t += 1
                mixer(l)
                norm(t, 0); t += 1
                ffn(AT["ffb", l], F, gating); F += FT

            act.wait_ge(x_ready, 8 * (t - 1) + 8)
            act.dma_start(late, late_in).then_inc(late_loaded, 16)
            for i, mix in enumerate((even, odd)):
                norm(t, 0); t += 1
                mix()
                norm(t, 0); t += 1
                ffn(AT["ffn", i], F, gating2); F += FT

        @block.gpsimd
        def _(pool):
            chain = [0]
            nc.gpsimd.memset(nhalf[:], -0.5).then_inc(pool_chain, 1)
            pool.wait_ge(pool_chain, 1)

            def rsqrt(o, i):
                n = i.shape[1]
                return nc.gpsimd.tensor_tensor(o, i, nhalf[:, 0:n], ALU.pow)

            def norm(t):
                pool.wait_ge(var_ready, t + 1)
                rsqrt(sc[:, 4:6], sc[:, 2:4]).then_inc(rs_ready, 1)

            def mixer(l):
                pool.wait_ge(*DV.at(l, "gvar"))
                rsqrt(sc[:, 112:128], sc[:, 128:144]).then_inc(*PO.sig(l, "grs"))
                pool.wait_ge(*AC.at(l, "AT"))
                for m in range(1, LEVELS):
                    if m >= 3:
                        pool.wait_ge(*PE.at(l, ("U", m - 2, 1)))
                    nc.gpsimd.tensor_tensor(ATM[m % 2], ATr, each(const("mt", (m - 1) * 128, 128), 8), ALU.mult
                                            ).then_inc(*PO.sig(l, ("ATM", m)))
                pool.wait_ge(*DV.at(l, "ovar"))
                rsqrt(sc[:, 152:160], sc[:, 144:152]).then_inc(*PO.sig(l, "ors"))
                pool.wait_ge(*DV.at(l, "mobavar"))
                rsqrt(sc[:, 192:224], sc[:, 160:192]).then_inc(*PO.sig(l, "mobars"))
                pool.wait_ge(*DV.at(l, "cvar"))
                rsqrt(sc[:, 228:232], sc[:, 224:228]).then_inc(*PO.sig(l, "crs"))
                pool.wait_ge(*DV.at(l, "mlavar"))
                rsqrt(sc[:, 192:224], sc[:, 160:192]).then_inc(*PO.sig(l, "mlars"))

            t = 0
            for l in range(DEPTH):
                norm(t); t += 1
                norm(t); t += 1
                mixer(l)
                norm(t); t += 1

            norm(t); t += 1
            pool.wait_ge(*DV2.at(0, "lnvar"))
            rsqrt(sc[:, 276:278], sc[:, 278:280]).then_inc(*PO2.sig(0, "lnrs"))
            norm(t); t += 1
            norm(t); t += 1
            pool.wait_ge(*DV2.at(0, "dvar"))
            rsqrt(sc[:, 400:448], sc[:, 352:400]).then_inc(*PO2.sig(0, "drs"))
            norm(t); t += 1

        @block.vector
        def _(dve):
            chain = [0]
            V = nc.vector

            def tick(ins):
                chain[0] += 1
                ins.then_inc(dve_chain, 1)
                return chain[0]

            def need(n):
                dve.wait_ge(dve_chain, n)

            def link(ins):
                need(tick(ins))

            V.memset(ones[:], 1.0).then_inc(consts_set, 1)
            dve.wait_ge(params_loaded, 32)
            V.tensor_scalar(par[:, 0:N_HALVED], par[:, 0:N_HALVED], 0.5, None, ALU.mult).then_inc(halved, 1)
            dve.wait_ge(halved, 1)

            def split(u, j=0):
                if u >= UNITS:
                    return
                dve.wait_ge(hi_ready, u + 1 + 6 * j)
                V.tensor_tensor(w_lo[:, u % SLOTS, :], raw[:, u % RAW, :], w_hi[:, u % SLOTS, :], ALU.subtract
                                ).then_inc(split_ready, 1)

            def update(t, units, factor):
                dve.wait_ge(unit_used, units)
                for c in range(KC):
                    V.scalar_tensor_tensor(x[:, c, :], bank(c // 2, (c % 2) * TOK, (c % 2 + 1) * TOK), factor, x[:, c, :],
                                           ALU.mult, ALU.add).then_inc(x_ready, 1)

            def norm(t, gain):
                dve.wait_ge(stat_ready, t + 1)
                V.tensor_scalar(sc[:, 2:4], bank(6, 0, 2), 1.0 / DM, EPS, ALU.mult, ALU.add).then_inc(var_ready, 1)
                dve.wait_ge(rs_ready, t + 1)
                V.tensor_scalar(diag[:, 0:128], ident, sc[:, 4:5], None, ALU.mult)
                V.tensor_scalar(diag[:, 128:256], ident, sc[:, 5:6], None, ALU.mult).then_inc(diag_ready, 1)
                dve.wait_ge(bc_ready, t + 1)
                def low(c):
                    dve.wait_ge(h_hi_ready, 8 * t + c + 1)
                    V.tensor_tensor(a_lo[:, c, :], tmp[:, c, :], a_hi[:, c, :], ALU.subtract).then_inc(h_ready, 1)
                for c in range(KC):
                    V.scalar_tensor_tensor(tmp[:, c, :], x[:, c, :], whole(gain, c), bank(7, 0, TOK), ALU.mult, ALU.mult
                                           ).then_inc(hn_ready, 1)
                    if c >= 2:
                        low(c - 2)
                low(KC - 2)
                low(KC - 1)

            def gating(F, p, n, j=0):
                dve.wait_ge(gate_act, F + 1 + 2 * j)
                V.scalar_tensor_tensor(a2[:, p, :], th2[:, p, :], 1.0, bank(4 + p, 0, TOK), ALU.add, ALU.mult
                                       ).then_inc(loop_chain, 1)
                dve.wait_ge(loop_chain, F + 1 + 2 * j)
                V.scalar_tensor_tensor(gu2[:, p, :], a2[:, p, :], 0.25, bank(4 + p, TOK, 512), ALU.mult, ALU.mult
                                       ).then_inc(gu_ready, 1)

            def gu_low(F, p, j=0):
                dve.wait_ge(gu_hi_ready, F + 1 + 2 * j)
                V.tensor_tensor(a_lo[:, 8 + p, :], gu2[:, p, :], a_hi[:, 8 + p, :], ALU.subtract).then_inc(gu_split, 1)

            def ffn(n0, F0, gate):
                split(n0 + AHEAD); split(n0 + 1 + AHEAD)
                gate(F0, 0, 0)
                gu_low(F0, 0)
                def tile(f, u, j=0):
                    split(u + AHEAD, j); split(u + 1 + AHEAD, j)
                    gate(F0 + f, f % 2, f, j)
                    split(u + 2 + AHEAD, j)
                    gu_low(F0 + f, f % 2, j)
                last = int(n0 + 3 * FT == UNITS)
                with dve.Fori(0, (FT - 2) // 2 - last) as j:
                    tile(1, n0 + 2, j)
                    tile(2, n0 + 5, j)
                for f in range(FT - 1 - 2 * last, FT):
                    tile(f, n0 + 3 * f - 1)
                split(n0 + 3 * FT - 1 + AHEAD)

            def rope_norm(v, heads, d, off, half_, rs, gain, cos, sin, m1, m2, done=None):
                H = 2 * heads
                link(V.tensor_tensor(v, v, over(rs, d), ALU.mult))
                link(V.tensor_tensor(v, v, each(gain, H), ALU.mult))
                w = H * 2 * half_
                m1v = m1[:, 0:w].rearrange("p (a b) -> p a b", b=2 * half_)
                m2v = m2[:, 0:w].rearrange("p (a b) -> p a b", b=2 * half_)
                for j in range(TT):
                    r = v[:, heads * j:heads * (j + 1), off:off + 2 * half_]
                    for s in range(2):
                        rs_ = r[:, :, s * half_:(s + 1) * half_]
                        for m, tab in ((m1v, cos), (m2v, sin)):
                            last = tick(V.tensor_tensor(m[:, heads * j:heads * (j + 1), s * half_:(s + 1) * half_], rs_,
                                                        each(const(tab, j * half_, half_), heads), ALU.mult))
                need(last)
                V.tensor_tensor(v[:, :, off:off + half_], m1v[:, :, 0:half_], m2v[:, :, half_:], ALU.subtract)
                i = V.tensor_tensor(v[:, :, off + half_:off + 2 * half_], m1v[:, :, half_:], m2v[:, :, 0:half_], ALU.add)
                if done is None:
                    tick(i)
                else:
                    i.then_inc(*done)

            def score_max(n, scale):
                p = n % 2
                dve.wait_ge(scores_ready, n + 1)
                s = sc[:, 8 + 4 * p:12 + 4 * p]
                v = bank(p, 0, 384).rearrange("p (a b) -> p a b", b=128)[:, 0:3:2, :]
                link(V.tensor_tensor(v, v, each(const("causal"), 2), ALU.add))
                mx = sc[:, 16 + 2 * p:18 + 2 * p]
                V.tensor_reduce(mx[:, 0:1], bank(p, 0, 128), AX.X, ALU.max)
                link(V.tensor_reduce(mx[:, 1:2], bank(p, 128, 384), AX.X, ALU.max))
                V.tensor_scalar(s[:, 0:2], mx, -scale, None, ALU.mult).then_inc(nmax_ready, 1)

            def normalise(n):
                p = n % 2
                dve.wait_ge(exp_done, n + 1)
                s = sc[:, 8 + 4 * p:12 + 4 * p]
                rec = sc[:, 20 + 2 * p:22 + 2 * p]
                link(V.reciprocal(rec, s[:, 2:4]))
                V.tensor_scalar(Pb[p][:, 0:128], Pb[p][:, 0:128], rec[:, 0:1], None, ALU.mult)
                V.tensor_scalar(Pb[p][:, 128:384], Pb[p][:, 128:384], rec[:, 1:2], None, ALU.mult).then_inc(p_ready, 1)

            def o_low(pair, chunk):
                dve.wait_ge(o_hi, pair + 1)
                V.tensor_tensor(a_lo[:, chunk, :], bank(4 + pair % 2, 0, TOK), a_hi[:, chunk, :], ALU.subtract
                                ).then_inc(o_split, 1)

            def attention(l, kind, g0, scale, chunk):
                n0 = 16 * l + 8 * kind
                score_max(n0, scale)
                for n in range(8):
                    split(AT["gates_" + "abc"[g0 // 8], l] + n + AHEAD)
                    normalise(n0 + n)
                    if n < 7:
                        score_max(n0 + n + 1, scale)
                    if n % 2 == 0 and n:
                        o_low(8 * l + 4 * kind + n // 2 - 1, chunk + n // 2 - 1)
                o_low(8 * l + 4 * kind + 3, chunk + 3)

            def log1p(e, o, w, w2, q):
                link(V.tensor_scalar(o, e, 2.0, None, ALU.add))
                link(V.reciprocal(q, o))
                link(V.tensor_tensor(w, e, q, ALU.mult))
                link(V.tensor_tensor(w2, w, w, ALU.mult))
                link(V.tensor_scalar(q, w2, 1.0 / 17, None, ALU.mult))
                for k in range(7, 0, -1):
                    link(V.scalar_tensor_tensor(q, q, 1.0 / (2 * k + 1), w2, ALU.add, ALU.mult))
                link(V.scalar_tensor_tensor(o, q, 1.0, w, ALU.add, ALU.mult))
                link(V.tensor_scalar(o, o, 2.0, None, ALU.mult))

            def mixer(l):
                for i in range(4):
                    split(AT["small", l] + i + AHEAD)
                link(V.memset(cb[:, :, 0:3], 0.0))
                dve.wait_ge(*AC.at(l, "sm"))
                for j in range(TT):
                    i = V.tensor_tensor(sc[:, 32 + 4 * j:36 + 4 * j], small[:, j, 420:424], whole(("dtb", l), 0, 4), ALU.add)
                    if j == 0:
                        tick(i)
                i.then_inc(*DV.sig(l, "z0"))

                def conv(p):
                    dve.wait_ge(cb_ready, 6 * l + p + 1)
                    c = (2 * p, 2 * p + 1)
                    w = [[half(("gconv", l), GK * i + k) for k in range(GK)] for i in c]
                    n = [tick(V.tensor_scalar(y[:, c[q], :], cb[:, c[q], 0:TOK], w[q][0], None, ALU.mult)) for q in range(2)]
                    for k in range(1, GK):
                        for q in range(2):
                            need(n[q])
                            i = V.scalar_tensor_tensor(y[:, c[q], :], cb[:, c[q], k:k + TOK], w[q][k], y[:, c[q], :],
                                                       ALU.mult, ALU.add)
                            if k < GK - 1:
                                n[q] = tick(i)
                            elif q == 0:
                                tick(i)
                    i.then_inc(conv_ready, 1)

                def silu(p):
                    dve.wait_ge(silu_th, 6 * l + p + 1)
                    v = y[:, 2 * p:2 * p + 2, :]
                    i = V.scalar_tensor_tensor(v, yth[:, 2 * p:2 * p + 2, :], 1.0, v, ALU.add, ALU.mult)
                    if p == 5:
                        i.then_inc(*DV.sig(l, "silu"))
                    else:
                        tick(i)
                for p in range(6):
                    u = AT["gdn", l] + 2 * p
                    split(u + AHEAD); split(u + 1 + AHEAD)
                    conv(p)
                    if p:
                        silu(p - 1)
                for q in range(2):
                    u = AT["z", l] + 2 * q
                    split(u + AHEAD); split(u + 1 + AHEAD)
                    if q == 0:
                        silu(5)
                    dve.wait_ge(z_th, 2 * l + q + 1)
                    v = flat(zs[:, 2 * q:2 * q + 2, :])
                    V.scalar_tensor_tensor(v, v, 1.0, bank(6 + q), ALU.add, ALU.mult).then_inc(zs_ready, 1)
                beta, sp, g = sc[:, 104:112], sc[:, 232:240], sc[:, 240:248]
                dve.wait_ge(*AC.at(l, "spe"))
                link(V.tensor_scalar(beta, sc[:, 40:48], 0.5, 0.5, ALU.mult, ALU.add))
                log1p(sc[:, 64:72], sp, sc[:, 248:256], sc[:, 256:264], sc[:, 264:272])
                link(V.scalar_tensor_tensor(sp, sc[:, 32:40], 0.0, sp, ALU.max, ALU.add))
                ea = sc[:, 56:60]
                tick(V.scalar_tensor_tensor(g[:, 0:4], sp[:, 0:4], -1.0, ea, ALU.mult, ALU.mult))
                V.scalar_tensor_tensor(g[:, 4:8], sp[:, 4:8], -1.0, ea, ALU.mult, ALU.mult).then_inc(*DV.sig(l, "g"))
                dve.wait_ge(*DV.at(l, "g"))
                V.tensor_tensor(tg, each(const("tri"), 8), over(g, 128), ALU.mult).then_inc(*DV.sig(l, "tg"))
                for i in range(12):
                    split(AT["moba", l] + i + AHEAD)
                dve.wait_ge(*PE.at(l, "cums"))
                V.tensor_copy(sc[:, 72:84], bank(3, 0, 12)).then_inc(*DV.sig(l, "cumcp"))
                dve.wait_ge(*DV.at(l, "cumcp"))
                V.tensor_tensor(sc[:, 96:100], sc[:, 80:84], sc[:, 72:76], ALU.subtract).then_inc(*DV.sig(l, "gld"))
                dve.wait_ge(*PE.at(l, "R"))
                for t in range(2):
                    i = V.scalar_tensor_tensor(E[:, 4 * t:4 * t + 4, :], bank(4 + t).rearrange("p (a b) -> p a b", b=128), -1.0,
                                               each(const("causal"), 4), ALU.mult, ALU.add)
                    if t == 0:
                        tick(i)
                i.then_inc(*DV.sig(l, "Et"))
                dve.wait_ge(*PE.at(l, "stat"))
                V.tensor_scalar(sc[:, 128:144], bank(2, 0, 16), EPS, None, ALU.add).then_inc(*DV.sig(l, "gvar"))
                dve.wait_ge(*PO.at(l, "grs"))
                link(V.tensor_scalar(sc[:, 112:120], sc[:, 112:120], GD ** -0.5, None, ALU.mult))
                V.tensor_tensor(diag16, each(ident, 16), over(sc[:, 112:128], 128), ALU.mult).then_inc(*DV.sig(l, "diag"))
                dve.wait_ge(*PE.at(l, "bc"))
                for qk in range(2):
                    for t in range(2):
                        v = y[:, 4 * qk:4 * qk + 4, 128 * t:128 * t + 128]
                        i = V.tensor_tensor(v, v, bank(2 * qk + t).rearrange("p (a b) -> p a b", b=128), ALU.mult)
                        if t == 0:
                            tick(i)
                    i.then_inc(*DV.sig(l, ("qn", "kn")[qk]))
                split(AT["gates_a", l] + AHEAD)
                dve.wait_ge(*AC.at(l, "kds"))
                link(V.tensor_tensor(sc[:, 272:276], beta[:, 4:8], sc[:, 92:96], ALU.mult))
                dve.wait_ge(*PE.at(l, "ktok"))
                tick(V.tensor_tensor(kgd[:, 0:4, :], bank(4).rearrange("p (a b) -> p a b", b=128), over(sc[:, 100:104], 128), ALU.mult))
                V.tensor_tensor(kgd[:, 4:8, :], bank(5).rearrange("p (a b) -> p a b", b=128), over(sc[:, 272:276], 128), ALU.mult
                                ).then_inc(*DV.sig(l, "kgd"))
                dve.wait_ge(*PE.at(l, "vtok"))
                tick(V.tensor_tensor(vb[:, 0:4, :], bank(0).rearrange("p (a b) -> p a b", b=128), over(beta[:, 0:4], 128), ALU.mult))
                V.tensor_tensor(vb[:, 4:8, :], bank(1).rearrange("p (a b) -> p a b", b=128), over(beta[:, 4:8], 128), ALU.mult
                                ).then_inc(*DV.sig(l, "vb"))
                split(AT["gates_a", l] + 1 + AHEAD)
                dve.wait_ge(*AC.at(l, "E"))
                dve.wait_ge(*PE.at(l, "G"))
                for b in range(8):
                    i = V.scalar_tensor_tensor(A[:, b, :], bank(2 + b // 4, (b % 4) * 128, (b % 4 + 1) * 128), beta[:, b:b + 1],
                                               E[:, b, :], ALU.mult, ALU.mult)
                i.then_inc(*DV.sig(l, "A"))
                dve.wait_ge(*PE.at(l, "QK"))
                for t in range(2):
                    i = V.tensor_tensor(QK[:, 4 * t:4 * t + 4, :], bank(4 + t).rearrange("p (a b) -> p a b", b=128),
                                        E[:, 4 * t:4 * t + 4, :], ALU.mult)
                i.then_inc(*DV.sig(l, "QK"))
                dve.wait_ge(*DV.at(l, "A"))
                link(V.tensor_tensor(X, A, each(const("m0"), 8), ALU.mult))
                V.tensor_tensor(X, each(ident, 8), X, ALU.subtract).then_inc(*DV.sig(l, "X0"))
                dve.wait_ge(*AC.at(l, "AT"))
                link(V.tensor_tensor(XT, ATr, each(const("m0t"), 8), ALU.mult))
                V.tensor_tensor(XT, each(ident, 8), XT, ALU.subtract).then_inc(*DV.sig(l, "XT0"))
                for m in range(1, LEVELS):
                    split(AT["gates_a", l] + 1 + m + AHEAD)
                    dve.wait_ge(*(DV.at(l, "XT0") if m == 1 else DV.at(l, ("T", m - 1, 1))))
                    for t in range(2):
                        for k, M, b in (("X", X, 2), ("T", XT, 4)):
                            if (k, m, t) not in DV.steps:
                                continue
                            dve.wait_ge(*PE.at(l, (k, m, t)))
                            v = M[:, 4 * t:4 * t + 4, :]
                            V.tensor_tensor(v, v, bank(b + t).rearrange("p (a b) -> p a b", b=128), ALU.subtract
                                            ).then_inc(*DV.sig(l, (k, m, t)))
                dve.wait_ge(*PE.at(l, "u"))
                V.tensor_copy(VN[:, 0:4, :], bank(0).rearrange("p (a b) -> p a b", b=128)).then_inc(*DV.sig(l, "vn0"))
                dve.wait_ge(*PE.at(l, "S1"))
                V.tensor_copy(S1, bank(3)).then_inc(*DV.sig(l, "S1"))
                tq = reg(9216, 4, 128)
                dve.wait_ge(*PE.at(l, "oa"))
                V.tensor_tensor(tq, bank(5).rearrange("p (a b) -> p a b", b=128), over(sc[:, 92:96], 128), ALU.mult
                                ).then_inc(*DV.sig(l, "tq"))
                dve.wait_ge(*AC.at(l, "u1"))
                V.tensor_tensor(VN[:, 4:8, :], O[:, 4:8, :], bank(4).rearrange("p (a b) -> p a b", b=128), ALU.subtract
                                ).then_inc(*DV.sig(l, "vn1"))
                dve.wait_ge(*PE.at(l, "ob1"))
                dve.wait_ge(*DV.at(l, "vn1"))
                V.tensor_tensor(O[:, 4:8, :], tq, bank(0).rearrange("p (a b) -> p a b", b=128), ALU.add).then_inc(*DV.sig(l, "O1"))
                dve.wait_ge(*AC.at(l, "osq"))
                link(V.tensor_reduce(sc[:, 144:152], ATM[0], AX.X, ALU.add))
                V.tensor_scalar(sc[:, 144:152], sc[:, 144:152], 1.0 / GD, EPS, ALU.mult, ALU.add).then_inc(*DV.sig(l, "ovar"))
                dve.wait_ge(*PO.at(l, "ors"))
                V.tensor_tensor(O, O, over(sc[:, 152:160], 128), ALU.mult).then_inc(*DV.sig(l, "on"))
                dve.wait_ge(*PE.at(l, "oT"))
                oz = reg(8192, 4, TOK)
                for q in range(2):
                    i = V.scalar_tensor_tensor(flat(oz[:, 2 * q:2 * q + 2, :]), bank(4 + q), half(("gout", l)),
                                               flat(zs[:, 2 * q:2 * q + 2, :]), ALU.mult, ALU.mult)
                i.then_inc(*DV.sig(l, "oz"))
                dve.wait_ge(*AC.at(l, "oz_hi"))
                V.tensor_tensor(a_lo[:, 12:16, :], oz, a_hi[:, 12:16, :], ALU.subtract).then_inc(*DV.sig(l, "oz_lo"))
                dve.wait_ge(*AC.at(l, "mobasq"))
                for q, r in enumerate((rA, rB)):
                    link(V.tensor_reduce(sc[:, 160 + 16 * q:176 + 16 * q], r[:, 0:1024].rearrange("p (a b) -> p a b", b=MD),
                                         AX.X, ALU.add))
                V.tensor_scalar(sc[:, 160:192], sc[:, 160:192], 1.0 / MD, EPS, ALU.mult, ALU.add).then_inc(*DV.sig(l, "mobavar"))
                dve.wait_ge(*PO.at(l, "mobars"))
                for q, name in enumerate(("mobaq", "mobak")):
                    v = flat(mqkv[:, 2 * q:2 * q + 2, :]).rearrange("p (a b) -> p a b", b=MD)
                    rope_norm(v, MH, MD, 0, 32, sc[:, 192 + 16 * q:208 + 16 * q], whole((name, l), 0, MD), "cosm", "sinm",
                              rA, rB, DV.sig(l, "mobaqk") if q else None)
                attention(l, 0, 8, MD ** -0.5, 16)
                dve.wait_ge(*AC.at(l, "csq"))
                cs = rA[:, 0:768].rearrange("p (a b) -> p a b", b=384)
                cv = sc[:, 224:228]
                tick(V.tensor_reduce(cv[:, 0:2], cs[:, :, 0:QR], AX.X, ALU.add))
                link(V.tensor_reduce(cv[:, 2:4], cs[:, :, QR:384], AX.X, ALU.add))
                tick(V.tensor_scalar(cv[:, 0:2], cv[:, 0:2], 1.0 / QR, EPS, ALU.mult, ALU.add))
                V.tensor_scalar(cv[:, 2:4], cv[:, 2:4], 1.0 / KVR, EPS, ALU.mult, ALU.add).then_inc(*DV.sig(l, "cvar"))
                dve.wait_ge(*PO.at(l, "crs"))
                tick(V.tensor_tensor(cn[:, :, 0:QR], small[:, :, 0:QR], over(sc[:, 228:230], QR), ALU.mult))
                V.tensor_tensor(cn[:, :, QR:384], small[:, :, QR:384], over(sc[:, 230:232], KVR), ALU.mult
                                ).then_inc(*DV.sig(l, "cn"))
                dve.wait_ge(*PE.at(l, "cT"))
                for f in range(3):
                    i = V.tensor_scalar(c32[:, f, :], bank(f // 2, (f % 2) * TOK, (f % 2 + 1) * TOK), whole(("cgain", l), f),
                                        None, ALU.mult)
                    if f < 2:
                        tick(i)
                i.then_inc(*DV.sig(l, "c32"))
                dve.wait_ge(*AC.at(l, "c_hi"))
                V.tensor_tensor(a_lo[:, 8:11, :], c32, a_hi[:, 8:11, :], ALU.subtract).then_inc(*DV.sig(l, "c_lo"))
                tick(V.tensor_copy(kl[:, 0:8, LN:LD], each(small[:, 0, 384:416], LH)))
                for i in range(3):
                    split(AT["up", l] + i + AHEAD)
                dve.wait_ge(*AC.at(l, "up"))
                V.tensor_copy(kl[:, 8:16, LN:LD], each(small[:, 1, 384:416], LH)).then_inc(*DV.sig(l, "kr"))
                dve.wait_ge(*AC.at(l, "mlasq"))
                for q, r in enumerate((rA, rB)):
                    link(V.tensor_reduce(sc[:, 160 + 16 * q:176 + 16 * q], r.rearrange("p (a b) -> p a b", b=LD), AX.X, ALU.add))
                V.tensor_scalar(sc[:, 160:192], sc[:, 160:192], 1.0 / LD, EPS, ALU.mult, ALU.add).then_inc(*DV.sig(l, "mlavar"))
                dve.wait_ge(*PO.at(l, "mlars"))
                for q, (v, name) in enumerate(((ql, "mlaq"), (kl, "mlak"))):
                    rope_norm(v, LH, LD, LN, 16, sc[:, 192 + 16 * q:208 + 16 * q], whole((name, l), 0, LD), "cosl", "sinl",
                              rA, rB, DV.sig(l, "mlaqk") if q else None)
                attention(l, 1, 16, LD ** -0.5, 8)
                for dp in range(4):
                    m = mA[:, dp % 2, :]
                    for n in range(3):
                        i = 3 * dp + n
                        split(AT["branch", l] + i + AHEAD)
                        dve.wait_ge(unit_used, AT["branch", l] + i + 1)
                        th = flat(gates[:, 8 * n + 2 * dp:8 * n + 2 * dp + 2, :])
                        V.scalar_tensor_tensor(mB if n else m, th, 1.0, bank(4 + i % 4), ALU.add, ALU.mult
                                               ).then_inc(merge_read, 1)
                        if n:
                            dve.wait_ge(merge_read, 12 * l + i + 1)
                            a = V.tensor_tensor(m, m, mB, ALU.add)
                            if n == 2:
                                a.then_inc(mix_ready, 1)
                            else:
                                link(a)
                    dve.wait_ge(mix_hi, 4 * l + dp + 1)
                    V.tensor_tensor(flat(a_lo[:, 2 * dp:2 * dp + 2, :]), m, flat(a_hi[:, 2 * dp:2 * dp + 2, :]), ALU.subtract
                                    ).then_inc(mix_split, 1)
                for k in range(KC):
                    split(AT["out", l] + k + AHEAD)

            def gating2(F, p, n, j=0):
                lo = HALVED["fconv", (F - F2) // FT][0] + 4 * ((F - F2) % FT)
                w = [par[:, lo + k:lo + k + 1] if isinstance(j, int) else par[:, bass.ds(lo + k + 8 * j, 1)] for k in range(2)]
                dve.wait_ge(conv_in, F - F2 + 1 + 2 * j)
                V.scalar_tensor_tensor(gh2[:, p, 1:], bank(4 + p, 0, TOK - 1), w[1], gh2[:, p, 1:], ALU.mult, ALU.add
                                       ).then_inc(loop_chain2, 1)
                dve.wait_ge(loop_chain2, F - F2 + 1 + 2 * j)
                V.scalar_tensor_tensor(gh2[:, p, 2:], bank(4 + p, 0, TOK - 2), w[0], gh2[:, p, 2:], ALU.mult, ALU.add
                                       ).then_inc(conv_used, 1)
                dve.wait_ge(gate_act, F + 1 + 2 * j)
                V.scalar_tensor_tensor(a2[:, p, :], th2[:, p, :], 1.0, gh2[:, p, :], ALU.add, ALU.mult
                                       ).then_inc(loop_chain, 1)
                dve.wait_ge(loop_chain, F + 1 + 2 * j)
                V.tensor_tensor(gu2[:, p, :], a2[:, p, :], bank(4 + p, TOK, 512), ALU.mult).then_inc(gu_ready, 1)

            def even():
                n0 = AT["ev_in"]
                tick(V.memset(ub[:, :, 0:CFK - 1], 0.0))
                link(V.memset(cx[:, :, 0:SCK - 1], 0.0))
                for i in range(4):
                    split(n0 + 2 * i + AHEAD); split(n0 + 2 * i + 1 + AHEAD)
                    dve.wait_ge(cf_th, i + 1)
                    V.scalar_tensor_tensor(ub[:, i, CFK - 1:], lnth[:, i, :], 1.0, bank(i, 0, TOK), ALU.add, ALU.mult
                                           ).then_inc(pair_read, 1)

                last = [0, 0]
                def taps(lo, hi):
                    for n in range(lo, min(hi, 4 * CFK)):
                        pair, k, q = n // (2 * CFK), n % (2 * CFK) // 2, n % 2
                        i = 2 * pair + q
                        w = half("cfconv", CFK * i + k)
                        if k == 0:
                            dve.wait_ge(pair_read, i + 1)
                            last[q] = tick(V.tensor_scalar(cf[:, i, :], ub[:, i, 0:TOK], w, whole("cfbias", i), ALU.mult, ALU.add))
                        else:
                            need(last[q])
                            e = V.scalar_tensor_tensor(cf[:, i, :], ub[:, i, k:k + TOK], w, cf[:, i, :], ALU.mult, ALU.add)
                            if n == 4 * CFK - 1:
                                e.then_inc(*DV2.sig(0, "cf"))
                            else:
                                last[q] = tick(e)
                step = 0
                for i in range(4):
                    u = n0 + 8 + 2 * i
                    for _ in range(2):
                        split(u + AHEAD)
                        u += 1
                        taps(step, step + 9)
                        step += 9
                    dve.wait_ge(sc_copy, i + 1)
                    V.tensor_tensor(cx[:, i, SCK - 1:], csb[:, i, :], bank((4, 5, 0, 1)[i], TOK, 512), ALU.mult
                                    ).then_inc(pair_read, 1)
                n = [0] * 4
                for k in range(SCK):
                    for i in range(4):
                        w = whole("scconv", SCK * i + k)
                        if k == 0:
                            dve.wait_ge(pair_read, 5 + i)
                            n[i] = tick(V.tensor_scalar(ysc[:, i, :], cx[:, i, 0:TOK], w, None, ALU.mult))
                        else:
                            need(n[i])
                            n[i] = tick(V.scalar_tensor_tensor(ysc[:, i, :], cx[:, i, k:k + TOK], w, ysc[:, i, :], ALU.mult, ALU.add))
                for q in range(2):
                    for i in range(2):
                        split(n0 + 16 + 2 * q + i + AHEAD)
                        taps(step, step + 9)
                        step += 9
                    dve.wait_ge(unit_used, n0 + 18 + 2 * q)
                    need(n[2 * q + 1])
                    V.tensor_tensor(flat(o2[:, 2 * q:2 * q + 2, :]), flat(ysc[:, 2 * q:2 * q + 2, :]), bank(6 + q), ALU.mult
                                    ).then_inc(b_read, 1)
                assert step < 4 * CFK - 1
                taps(step, 4 * CFK)
                dve.wait_ge(*PE2.at(0, "mean"))
                dve.wait_ge(*DV2.at(0, "cf"))
                for i in range(4):
                    e = V.scalar_tensor_tensor(cf[:, i, :], bank(0, 0, TOK), -1.0 / 512, cf[:, i, :], ALU.mult, ALU.add)
                    if i < 3:
                        tick(e)
                e.then_inc(*DV2.sig(0, "cen"))
                dve.wait_ge(*PE2.at(0, "lnstat"))
                V.tensor_scalar(sc[:, 278:280], bank(1, 0, 2), 1.0 / 512, EPS, ALU.mult, ALU.add).then_inc(*DV2.sig(0, "lnvar"))
                dve.wait_ge(*PO2.at(0, "lnrs"))
                tick(V.tensor_scalar(diag[:, 0:128], ident, sc[:, 276:277], None, ALU.mult))
                V.tensor_scalar(diag[:, 128:256], ident, sc[:, 277:278], None, ALU.mult).then_inc(*DV2.sig(0, "lndiag"))
                dve.wait_ge(*PE2.at(0, "lnbc"))
                for i in range(4):
                    n[i] = tick(V.scalar_tensor_tensor(cf[:, i, :], cf[:, i, :], half("lng", i), bank(2, 0, TOK), ALU.mult, ALU.mult))
                for i in range(4):
                    need(n[i])
                    e = V.tensor_scalar(cf[:, i, :], cf[:, i, :], half("lnb", i), None, ALU.add)
                    if i < 3:
                        tick(e)
                e.then_inc(*DV2.sig(0, "yb"))
                dve.wait_ge(*AC2.at(0, "lnth"))
                V.scalar_tensor_tensor(flat(o2[:, 4:8, :]), flat(lnth), 1.0, flat(cf), ALU.add, ALU.mult).then_inc(*DV2.sig(0, "o2"))
                dve.wait_ge(*AC2.at(0, "o2_hi"))
                V.tensor_tensor(a_lo[:, 8:16, :], o2, a_hi[:, 8:16, :], ALU.subtract).then_inc(*DV2.sig(0, "o2_lo"))
                for k in range(8):
                    split(AT["ev_out"] + k + AHEAD)

            def odd():
                n0 = AT["lru_in"]
                link(V.memset(lx[:, :, 0:LK - 1], 0.0))
                V.tensor_scalar(sc[:, 284:288], whole("lam", 0, 4), -1.0, None, ALU.mult).then_inc(*DV2.sig(0, "lamz"))
                n = [0] * 4
                for q in range(4):
                    split(n0 + 2 * q + AHEAD); split(n0 + 2 * q + 1 + AHEAD)
                    if q < 2:
                        dve.wait_ge(lru_copy, q + 1)
                        for k in range(LK):
                            for i in (2 * q, 2 * q + 1):
                                w = whole("lruconv", LK * i + k)
                                if k == 0:
                                    n[i] = tick(V.tensor_scalar(xc[:, i, :], lx[:, i, 0:TOK], w, whole("lrubias", i), ALU.mult, ALU.add))
                                    continue
                                need(n[i])
                                e = V.scalar_tensor_tensor(xc[:, i, :], lx[:, i, k:k + TOK], w, xc[:, i, :], ALU.mult, ALU.add)
                                if (k, i) == (LK - 1, 3):
                                    e.then_inc(*DV2.sig(0, "xc"))
                                else:
                                    n[i] = tick(e)
                dve.wait_ge(*AC2.at(0, "spe"))
                sp = sc[:, 296:300]
                log1p(sc[:, 292:296], sp, sc[:, 248:252], sc[:, 256:260], sc[:, 264:268])
                link(V.scalar_tensor_tensor(sp, sc[:, 284:288], 0.0, sp, ALU.max, ALU.add))
                V.tensor_scalar(sp, sp, -4.0, None, ALU.mult).then_inc(*DV2.sig(0, "sp4"))
                dve.wait_ge(*AC2.at(0, "lgsq"))
                for i in range(18):
                    split(AT["dil_in"] + i + AHEAD)
                link(V.tensor_scalar(flat(recb), flat(recb), 0.044715, 1.0, ALU.mult, ALU.add))
                gin = reg(7696, 4, TOK)
                link(V.tensor_tensor(flat(gin), flat(recb), flat(lg), ALU.mult))
                dve.wait_ge(*AC2.at(0, "tq"))
                m2 = reg(8720, 4, TOK)
                link(V.tensor_scalar(flat(m2), flat(tqb), -1.0, 1.0, ALU.mult, ALU.add))
                link(V.reciprocal(flat(m2), flat(m2)))
                link(V.scalar_tensor_tensor(flat(m2), flat(tqb), -2.0, flat(m2), ALU.mult, ALU.mult))
                V.tensor_scalar(flat(recb), flat(m2), 2.0 ** -100, None, ALU.max).then_inc(*DV2.sig(0, "m2"))
                dve.wait_ge(*AC2.at(0, "ith"))
                link(V.scalar_tensor_tensor(flat(thi), flat(thi), 1.0, flat(xc), ALU.add, ALU.mult))
                dve.wait_ge(*AC2.at(0, "mult"))
                link(V.scalar_tensor_tensor(flat(m2), flat(m2), 2.0 ** -100, flat(thr), ALU.is_ge, ALU.mult))
                link(V.scalar_tensor_tensor(flat(thi), flat(thi), 0.5, flat(m2), ALU.mult, ALU.mult))
                V.tensor_copy(flat(recb), flat(gin)).then_inc(*DV2.sig(0, "gin"))
                for i in range(4):
                    e = tick(V.tensor_tensor_scan(m2[:, i, :], aa[:, i, :], thi[:, i, :], 0.0, ALU.mult, ALU.add))
                need(e)
                dve.wait_ge(*AC2.at(0, "gth"))
                link(V.scalar_tensor_tensor(flat(tqb), flat(tqb), 1.0, flat(lg), ALU.add, ALU.mult))
                V.scalar_tensor_tensor(flat(thi), flat(tqb), 0.5, flat(m2), ALU.mult, ALU.mult).then_inc(*DV2.sig(0, "ylru"))
                dve.wait_ge(*AC2.at(0, "ylru_hi"))
                V.tensor_tensor(a_lo[:, 8:12, :], thi, a_hi[:, 8:12, :], ALU.subtract).then_inc(*DV2.sig(0, "ylru_lo"))
                dve.wait_ge(*AC2.at(0, "dsq"))
                v = sc[:, 352:400].rearrange("p (a b) -> p a b", b=24)
                link(V.tensor_reduce(sc[:, 352:400], flat(dsq).rearrange("p (a b) -> p a b", b=DD), AX.X, ALU.add))
                V.tensor_scalar(sc[:, 352:400], sc[:, 352:400], 1.0 / DD, EPS, ALU.mult, ALU.add).then_inc(*DV2.sig(0, "dvar"))
                dve.wait_ge(*PO2.at(0, "drs"))
                for j in range(TT):
                    r = qkv[:, j, 0:2 * DW].rearrange("p (a b) -> p a b", b=DD)
                    n[j] = tick(V.tensor_tensor(r, r, over(sc[:, 400 + 24 * j:424 + 24 * j], DD), ALU.mult))
                for j in range(TT):
                    need(n[j])
                    for q, name in enumerate(("dilq", "dilk")):
                        r = qkv[:, j, DW * q:DW * q + DW].rearrange("p (a b) -> p a b", b=DD)
                        e = V.tensor_tensor(r, r, each(whole(name, 0, DD), 12), ALU.mult)
                        if (j, q) == (1, 1):
                            e.then_inc(*DV2.sig(0, "dqk"))
                        else:
                            tick(e)

                def dmax(h):
                    p = h % 2
                    dve.wait_ge(d_scores, h + 1)
                    s, mx = sc[:, 304 + 16 * p:320 + 16 * p], sc[:, 336 + 8 * p:344 + 8 * p]
                    v = ps[:, 3 * p:3 * p + 3, 0:384]
                    link(V.tensor_tensor(v, v, dneg, ALU.add))
                    V.tensor_reduce(mx[:, 0:3], v[:, :, 0:128], AX.X, ALU.max)
                    link(V.tensor_reduce(mx[:, 3:6], v[:, :, 128:384], AX.X, ALU.max))
                    link(V.tensor_reduce(mx[:, 6:8], mx[:, 0:6].rearrange("p (a b) -> p a b", b=3), AX.X, ALU.max))
                    V.tensor_scalar(s[:, 0:2], mx[:, 6:8], -(DD ** -0.5), None, ALU.mult).then_inc(d_nmax, 1)
                dve.wait_ge(late_loaded, 16)
                dmax(0)
                for h in range(DH):
                    p = h % 2
                    dve.wait_ge(d_exp, h + 1)
                    s, rec = sc[:, 304 + 16 * p:320 + 16 * p], sc[:, 312 + 16 * p:316 + 16 * p]
                    link(V.tensor_reduce(rec[:, 0:2], s[:, 2:8].rearrange("p (a b) -> p a b", b=3), AX.X, ALU.add))
                    link(V.reciprocal(rec[:, 2:4], rec[:, 0:2]))
                    tick(V.tensor_scalar(Pd[p][:, :, 0:128], Pd[p][:, :, 0:128], rec[:, 2:3], None, ALU.mult))
                    V.tensor_scalar(Pd[p][:, :, 128:384], Pd[p][:, :, 128:384], rec[:, 3:4], None, ALU.mult).then_inc(d_p, 1)
                    if h < 3:
                        dmax(h + 1)
                    if h == 3:
                        d_low(0)
                d_low(1)
                for k in range(6):
                    split(AT["od_out"] + k + AHEAD)

            def d_low(pair):
                dve.wait_ge(d_hi, pair + 1)
                V.tensor_tensor(a_lo[:, 12 + pair, :], bank(6 + pair, 0, TOK), a_hi[:, 12 + pair, :], ALU.subtract).then_inc(d_lo, 1)

            for u in range(AHEAD):
                split(u)
            dve.wait_ge(x_loaded, 16)
            t, F = 0, 0
            for l in range(DEPTH):
                norm(t, ("ffa", l)); t += 1
                ffn(AT["ffa", l], F, gating); F += FT
                update(t, AT["ffa", l] + 3 * FT, 1.0)
                norm(t, ("mix", l)); t += 1
                mixer(l)
                update(t, AT["out", l] + 8, 0.5)
                norm(t, ("ffb", l)); t += 1
                ffn(AT["ffb", l], F, gating); F += FT
                update(t, AT["ffb", l] + 3 * FT, 1.0)

            for i, (mix, end) in enumerate(((even, AT["ev_out"] + 8), (odd, AT["od_out"] + 6))):
                norm(t, ("mix2", i)); t += 1
                mix()
                update(t, end, 1.0)
                norm(t, ("ffn2", i)); t += 1
                ffn(AT["ffn", i], F, gating2); F += FT
                update(t, AT["ffn", i] + 3 * FT, 1.0)

        @block.tensor
        def _(pe):
            def mm(o, a, b, start=True, stop=True, **k):
                return nc.tensor.matmul(o, a, b, start=start, stop=stop, **k)

            def norm(t):
                if t == 0:
                    pe.wait_ge(consts_set, 1)
                    pe.wait_ge(params_loaded, 32)
                for c in range(KC):
                    pe.wait_ge(sq_ready, 8 * t + c + 1)
                    for j in range(TT):
                        i = mm(bank(6, j, j + 1), tmp[:, c, 128 * j:128 * j + 128], ones[:, 0:1], start=(c == 0 and j == 0),
                               stop=(c == KC - 1), skip_group_check=True)
                i.then_inc(stat_ready, 1)
                pe.wait_ge(diag_ready, t + 1)
                mm(bank(7, 0, TOK), ones[:], diag[:]).then_inc(bc_ready, 1)

            def fm(u, o, j=0, t=None):
                s = u % SLOTS
                pe.wait_ge(split_ready, u + 1 + 6 * j)
                for k in range(KC):
                    if t is not None:
                        pe.wait_ge(h_ready, 8 * t + k + 1)
                    w = slice(k * 128, (k + 1) * 128)
                    mm(o, w_hi[:, s, w], a_hi[:, k, :], start=(k == 0), stop=False)
                    mm(o, w_hi[:, s, w], a_lo[:, k, :], start=False, stop=False)
                    i = mm(o, w_lo[:, s, w], a_hi[:, k, :], start=False, stop=(k == KC - 1))
                i.then_inc(unit_used, 1)

            def km(u, chunk, first, last, j=0):
                s = u % SLOTS
                pe.wait_ge(split_ready, u + 1 + 6 * j)
                for n in range(KC):
                    o = bank(n // 2, (n % 2) * TOK, (n % 2 + 1) * TOK)
                    w = slice(n * 128, (n + 1) * 128)
                    mm(o, w_hi[:, s, w], a_hi[:, chunk, :], start=(first and n % 2 == 0), stop=False, skip_group_check=True)
                    mm(o, w_hi[:, s, w], a_lo[:, chunk, :], start=False, stop=False, skip_group_check=True)
                    i = mm(o, w_lo[:, s, w], a_hi[:, chunk, :], start=False, stop=last, skip_group_check=True)
                i.then_inc(unit_used, 1)

            def tm(u, b, cols, kts, k0, first, last, t=None, banks=None, c0=0):
                s = u % SLOTS
                pe.wait_ge(split_ready, u + 1)
                step = UC // kts
                for i in range(kts):
                    k = k0 + i
                    if t is not None:
                        pe.wait_ge(h_ready, 8 * t + k + 1)
                    w = slice(i * step, i * step + cols)
                    for j in range(TT):
                        o = bank(b + j, 0, cols)
                        tk = slice(128 * j, 128 * j + 128)
                        st, sp_ = first and i == 0, last and i == kts - 1
                        mm(o, a_hi[:, c0 + k, tk], w_hi[:, s, w], start=st, stop=False)
                        mm(o, a_hi[:, c0 + k, tk], w_lo[:, s, w], start=False, stop=False)
                        q = mm(o, a_lo[:, c0 + k, tk], w_hi[:, s, w], start=False, stop=sp_)
                q.then_inc(unit_used, 1)

            def ffn(n0, F0, t):
                def gate_up(f, u, j=0, t=None):
                    if F0 + f >= 2:
                        pe.wait_ge(gu_ready, F0 + f - 1 + 2 * j)
                    p = f % 2
                    fm(u, bank(4 + p, 0, TOK), j, t)
                    fm(u + 1, bank(4 + p, TOK, 512), j)
                def down(f, u, first, last, j=0):
                    pe.wait_ge(gu_split, F0 + f + 1 + 2 * j)
                    km(u, 8 + f % 2, first, last, j)
                gate_up(0, n0, 0, t)
                gate_up(1, n0 + 2)
                down(0, n0 + 4, True, False)
                with pe.Fori(0, (FT - 2) // 2) as j:
                    gate_up(2, n0 + 5, j)
                    down(1, n0 + 7, False, False, j)
                    gate_up(3, n0 + 8, j)
                    down(2, n0 + 10, False, False, j)
                down(FT - 1, n0 + 3 * FT - 1, False, True)

            def gate_unit(l, i):
                u = AT["gates_" + "abc"[i // 8], l] + i % 8
                if 24 * l + i >= 2:
                    pe.wait_ge(gate_evac, 24 * l + i - 1)
                fm(u, bank(6 + i % 2, 0, TOK))

            def attention(l, kind, g0, q, k, v):
                n0 = 16 * l + 8 * kind
                def scores(n):
                    g = n0 + n
                    if g >= 2:
                        pe.wait_ge(exp_done, g - 1)
                    qh, kh = q(n), k(n)
                    mm(bank(g % 2, 0, 128), qh[:, 0:128], kh[:, 0:128])
                    mm(bank(g % 2, 128, 384), qh[:, 128:256], kh).then_inc(scores_ready, 1)
                def turn(n):
                    g = n0 + n
                    pe.wait_ge(p_ready, g + 1)
                    for b in range(3):
                        i = nc.tensor.transpose(bank(2 + g % 2, 128 * b, 128 * b + 128), Pb[g % 2][:, 128 * b:128 * b + 128], ident)
                    i.then_inc(pt_ps, 1)
                def pv(n):
                    g = n0 + n
                    pair = g // 2
                    pe.wait_ge(pt_ready, g + 1)
                    if pair >= 2:
                        pe.wait_ge(o_split, pair - 1)
                    pt, r = PTb[g % 2], 64 * (n % 2)
                    o = ps[r:r + 64, 4 + pair % 2, 0:TOK]
                    mm(o, v(0, n), pt[:, 0:256], start=True, stop=False)
                    i = mm(o[:, 128:256], v(1, n), pt[:, 256:384], start=False, stop=True)
                    if n % 2:
                        i.then_inc(o_ready, 1)
                scores(0)
                for n in range(8):
                    if n < 7:
                        scores(n + 1)
                    gate_unit(l, g0 + n)
                    turn(n)
                    if n:
                        pv(n - 1)
                pv(7)

            def mixer(l, t):
                ev = lambda s, st: pe.wait_ge(*s.at(l, st))
                for i in range(4):
                    tm(AT["small", l] + i, 0, SMALL, 2, 2 * i, i == 0, i == 3, t)
                for i in range(12):
                    if i == 8:
                        ev(AC, "sm")
                    p = i // 2
                    fm(AT["gdn", l] + i, bank((2 + p) % 6, (i % 2) * TOK, (i % 2 + 1) * TOK))
                for i in range(4):
                    fm(AT["z", l] + i, bank(6 + i // 2, (i % 2) * TOK, (i % 2 + 1) * TOK))
                for g in range(3):
                    pe.wait_ge(cb_ready, 6 * l + 2 * g + 2)
                    for i in range(4):
                        tm(AT["moba", l] + 4 * g + i, (2, 4, 0)[g], 512, 2, 2 * i, i == 0, i == 3)
                ev(DV, "g")
                pe.wait_ge(m_ready, 3 * l + 2)
                g8 = sc[:, 240:248]
                mm(bank(3, 0, 8), const("tri"), g8)
                mm(bank(3, 8, 12), ones[:], g8[:, 0:4]).then_inc(*PE.sig(l, "cums"))
                ev(DV, "tg")
                for b in range(2):
                    i = mm(bank(4 + b), ones[:], flat(tg[:, 4 * b:4 * b + 4, :]))
                i.then_inc(*PE.sig(l, "R"))
                ev(AC, "gsq")
                for qk in range(2):
                    for tt in range(2):
                        for h in range(4):
                            c = qk * 8 + tt * 4 + h
                            i = mm(bank(2, c, c + 1), tmp[:, qk * 4 + h, 128 * tt:128 * tt + 128], ones[:, 0:1])
                i.then_inc(*PE.sig(l, "stat"))
                pe.wait_ge(zs_ready, 2 * l + 2)
                gate_unit(l, 0)
                ev(DV, "diag")
                pe.wait_ge(m_ready, 3 * l + 3)
                for b in range(4):
                    i = mm(bank(b), ones[:], flat(diag16[:, 4 * b:4 * b + 4, :]))
                i.then_inc(*PE.sig(l, "bc"))
                gate_unit(l, 1)
                kT = lambda tt, h: y[:, 4 + h, 128 * tt:128 * tt + 128]
                qT = lambda tt, h: y[:, h, 128 * tt:128 * tt + 128]
                vT = lambda tt, h: y[:, 8 + h, 128 * tt:128 * tt + 128]
                def blocks(b, f, step):
                    for tt in range(2):
                        for h in range(4):
                            i = f(bank(b + tt, 128 * h, 128 * h + 128), tt, h)
                    i.then_inc(*PE.sig(l, step))
                ev(DV, "kn")
                ev(DV, "Et")
                blocks(4, lambda o, tt, h: nc.tensor.transpose(o, kT(tt, h), ident), "ktok")
                blocks(0, lambda o, tt, h: nc.tensor.transpose(o, vT(tt, h), ident), "vtok")
                blocks(2, lambda o, tt, h: mm(o, kT(tt, h), kT(tt, h)), "G")
                ev(DV, "kgd")
                blocks(4, lambda o, tt, h: mm(o, qT(tt, h), kT(tt, h)), "QK")
                ev(DV, "vb")
                ev(DV, "A")
                blocks(0, lambda o, tt, h: nc.tensor.transpose(o, A[:, 4 * tt + h, :], ident), "AT")
                ev(DV, "QK")
                blocks(2, lambda o, tt, h: nc.tensor.transpose(o, QK[:, 4 * tt + h, :], ident), "QKT")
                ev(DV, "XT0")
                ev(AC, "QKT")
                for m in range(1, LEVELS):
                    ev(PO, ("ATM", m))
                    for tt in range(2):
                        if m > 1:
                            ev(DV, ("X", m - 1, tt))
                        for h in range(4):
                            b = 4 * tt + h
                            i = mm(bank(tt, 128 * h, 128 * h + 128), ATM[m % 2][:, b, :], X[:, b, :])
                        i.then_inc(*PE.sig(l, ("U", m, tt)))
                    gate_unit(l, 1 + m)
                    for tt in range(2):
                        ev(AC, ("U", m, tt))
                        if m > 1:
                            ev(DV, ("T", m - 1, tt))
                        if m < LEVELS - 1:
                            for h in range(4):
                                b = 4 * tt + h
                                i = mm(bank(2 + tt, 128 * h, 128 * h + 128), XT[:, b, :], U[:, b, :])
                            i.then_inc(*PE.sig(l, ("X", m, tt)))
                        for h in range(4):
                            b = 4 * tt + h
                            i = mm(bank(4 + tt, 128 * h, 128 * h + 128), U[:, b, :], XT[:, b, :])
                        i.then_inc(*PE.sig(l, ("T", m, tt)))
                ev(DV, ("T", LEVELS - 1, 1))
                four = lambda b, f, step: [f(bank(b, 128 * h, 128 * h + 128), h) for h in range(4)][-1].then_inc(*PE.sig(l, step))
                blocks(0, lambda o, tt, h: mm(o, XT[:, 4 * tt + h, :], vb[:, 4 * tt + h, :]), "u")
                four(2, lambda o, h: mm(o, kgd[:, 4 + h, :], XT[:, 4 + h, :]), "wT")
                ev(DV, "vn0")
                four(3, lambda o, h: mm(o, kgd[:, h, :], VN[:, h, :]), "S1")
                ev(AC, "wT")
                four(2, lambda o, h: mm(o, QKT[:, h, :], VN[:, h, :]), "ob0")
                ev(DV, "S1")
                four(4, lambda o, h: mm(o, wT[:, 128 * h:128 * h + 128], S1[:, 128 * h:128 * h + 128]), "wS")
                four(5, lambda o, h: mm(o, qT(1, h), S1[:, 128 * h:128 * h + 128]), "oa")
                ev(DV, "vn1")
                four(0, lambda o, h: mm(o, QKT[:, 4 + h, :], VN[:, 4 + h, :]), "ob1")
                ev(DV, "on")
                for h in range(4):
                    for tt in range(2):
                        i = nc.tensor.transpose(bank(4 + h // 2, (h % 2) * TOK + 128 * tt, (h % 2) * TOK + 128 * tt + 128),
                                                O[:, 4 * tt + h, :], ident)
                i.then_inc(*PE.sig(l, "oT"))
                ev(DV, "mobaqk")
                for qk in range(2):
                    for c in range(4):
                        for tt in range(2):
                            i = nc.tensor.transpose(bank(2 * qk + c // 2, (c % 2) * TOK + 128 * tt, (c % 2) * TOK + 128 * tt + 128),
                                                    mqkv[:, 2 * qk + tt, 128 * c:128 * c + 128], ident)
                i.then_inc(*PE.sig(l, "mobaT"))
                ev(AC, "mobaT")
                ev(DV, "oz_lo")
                hp = lambda n: slice(64 * (n % 2), 64 * (n % 2) + 64)
                attention(l, 0, 8, lambda n: qTm[hp(n), n // 2, :], lambda n: kTm[hp(n), n // 2, :],
                          lambda tt, n: mqkv[:, 4 + tt, 64 * n:64 * n + 64])
                ev(DV, "cn")
                pe.wait_ge(exp_done, 16 * l + 8)
                for f in range(3):
                    for tt in range(2):
                        i = nc.tensor.transpose(bank(f // 2, (f % 2) * TOK + 128 * tt, (f % 2) * TOK + 128 * tt + 128),
                                                cn[:, tt, 128 * f:128 * f + 128], ident)
                i.then_inc(*PE.sig(l, "cT"))
                ev(DV, "c_lo")
                pe.wait_ge(o_split, 8 * l + 4)
                pe.wait_ge(gate_evac, 24 * l + 16)
                u = AT["up", l]
                s = u % SLOTS
                tm(u, 0, 512, 2, 0, True, True, c0=8)
                s = (u + 1) % SLOTS
                pe.wait_ge(split_ready, u + 2)
                for j in range(TT):
                    tk = slice(128 * j, 128 * j + 128)
                    for k in range(2):
                        o, w = bank(2, TOK * j, TOK * j + TOK), slice(512 * k, 512 * k + 256)
                        mm(o, a_hi[:, 8 + k, tk], w_hi[:, s, w], start=(k == 0), stop=False)
                        mm(o, a_hi[:, 8 + k, tk], w_lo[:, s, w], start=False, stop=False)
                        i = mm(o, a_lo[:, 8 + k, tk], w_hi[:, s, w], start=False, stop=(k == 1))
                i.then_inc(unit_used, 1)
                s = (u + 2) % SLOTS
                pe.wait_ge(split_ready, u + 3)
                for n in range(2):
                    for j in range(TT):
                        tk = slice(128 * j, 128 * j + 128)
                        o, w = bank(3 + 2 * n + j), slice(512 * n, 512 * n + 512)
                        mm(o, a_hi[:, 10, tk], w_hi[:, s, w], start=True, stop=False)
                        mm(o, a_hi[:, 10, tk], w_lo[:, s, w], start=False, stop=False)
                        i = mm(o, a_lo[:, 10, tk], w_hi[:, s, w], start=False, stop=True)
                i.then_inc(unit_used, 1)
                ev(DV, "mlaqk")
                for m, name in ((ql, "mlaTq"), (kl, "mlaTk")):
                    if name == "mlaTk":
                        ev(AC, "mlaTq")
                    for h in range(LH):
                        for tt in range(2):
                            c = (h % 2) * TOK + 128 * tt
                            i = nc.tensor.transpose(ps[0:LD, h // 2, c:c + 128], m[:, 8 * tt + h, :], ident)
                    i.then_inc(*PE.sig(l, name))
                ev(AC, "mlaTk")
                attention(l, 1, 16, lambda n: qTl[:, n, :], lambda n: kTl[:, n, :], lambda tt, n: vl[:, tt, 64 * n:64 * n + 64])
                pe.wait_ge(o_split, 8 * l + 8)
                pe.wait_ge(gate_evac, 24 * l + 24)
                for i in range(12):
                    if 12 * l + i >= 4:
                        pe.wait_ge(merge_read, 12 * l + i - 3)
                    u, n = AT["branch", l] + i, i % 3
                    s = u % SLOTS
                    pe.wait_ge(split_ready, u + 1)
                    for d in range(2):
                        o = bank(4 + i % 4, d * TOK, (d + 1) * TOK)
                        for k in range(4):
                            w, c = slice(k * 256 + d * 128, k * 256 + d * 128 + 128), 8 + 4 * n + k
                            mm(o, w_hi[:, s, w], a_hi[:, c, :], start=(k == 0), stop=False)
                            mm(o, w_hi[:, s, w], a_lo[:, c, :], start=False, stop=False)
                            q = mm(o, w_lo[:, s, w], a_hi[:, c, :], start=False, stop=(k == 3))
                    q.then_inc(unit_used, 1)
                for k in range(KC):
                    pe.wait_ge(mix_split, 4 * l + k // 2 + 1)
                    km(AT["out", l] + k, k, k == 0, k == KC - 1)

            def even(t):
                n0 = AT["ev_in"]
                for i in range(8):
                    b = (0, 1, 2, 3, 4, 5, 0, 1)[i]
                    if i >= 6:
                        pe.wait_ge(pair_read, i - 5)
                    for q in range(2):
                        fm(n0 + 2 * i + q, bank(b, q * TOK, (q + 1) * TOK), 0, t if i == 0 and q == 0 else None)
                for i in range(4):
                    fm(n0 + 16 + i, bank(6 + i // 2, (i % 2) * TOK, (i % 2 + 1) * TOK))
                pe.wait_ge(*DV2.at(0, "cf"))
                for i in range(4):
                    e = mm(bank(0, 0, TOK), ones[:], cf[:, i, :], start=(i == 0), stop=(i == 3))
                e.then_inc(*PE2.sig(0, "mean"))
                pe.wait_ge(*AC2.at(0, "lnsq"))
                for c in range(4):
                    for j in range(TT):
                        e = mm(bank(1, j, j + 1), tmp[:, c, 128 * j:128 * j + 128], ones[:, 0:1], start=(c == 0 and j == 0),
                               stop=(c == 3), skip_group_check=True)
                e.then_inc(*PE2.sig(0, "lnstat"))
                pe.wait_ge(*DV2.at(0, "lndiag"))
                mm(bank(2, 0, TOK), ones[:], diag[:]).then_inc(*PE2.sig(0, "lnbc"))
                pe.wait_ge(*DV2.at(0, "o2_lo"))
                for k in range(8):
                    km(AT["ev_out"] + k, 8 + k, k == 0, k == 7)

            def odd(t):
                n0 = AT["lru_in"]
                for i in range(8):
                    fm(n0 + i, bank(i // 2, (i % 2) * TOK, (i % 2 + 1) * TOK), 0, t if i == 0 else None)
                for g in range(5):
                    if g >= 2:
                        pe.wait_ge(*((lru_copy, 2 * g - 2) if g < 4 else (dil_copy, 1)))
                    b = (4, 6, 0, 2, 4)[g]
                    if g < 4:
                        for i in range(4):
                            tm(AT["dil_in"] + 4 * g + i, b, 512, 2, 2 * i, i == 0, i == 3)
                    else:
                        for i in range(2):
                            tm(AT["dil_in"] + 16 + i, b, 256, 4, 4 * i, i == 0, i == 1)
                pe.wait_ge(*DV2.at(0, "xc"))
                pe.wait_ge(late_loaded, 16)
                pe.wait_ge(dil_copy, 3)
                for name, b, step in (("wa", 6, "r"), ("wx", 0, "i")):
                    lo = LATE[name][0]
                    for i in range(4):
                        e = mm(bank(b + i // 2, (i % 2) * TOK, (i % 2 + 1) * TOK), late[:, lo + 128 * i:lo + 128 * i + 128], xc[:, i, :])
                    e.then_inc(*PE2.sig(0, step))
                pe.wait_ge(*DV2.at(0, "dqk"))
                pe.wait_ge(dil_copy, 5)
                for qk in range(2):
                    for c in range(6):
                        for tt in range(2):
                            o = (c % 2) * TOK + 128 * tt
                            e = nc.tensor.transpose(bank(3 * qk + c // 2, o, o + 128),
                                                    qkv[:, tt, DW * qk + 128 * c:DW * qk + 128 * c + 128], ident)
                e.then_inc(*PE2.sig(0, "dilT"))
                pe.wait_ge(*AC2.at(0, "dilT"))

                def scores(h):
                    if h >= 2:
                        pe.wait_ge(d_pt, h - 1)
                    r = slice(64 * (h % 2), 64 * (h % 2) + 64)
                    for g in range(DG):
                        q, k, b = qTd[r, 2 * g + h // 2, :], kTd[r, 2 * g + h // 2, :], 3 * (h % 2) + g
                        mm(bank(b, 0, 128), q[:, 0:128], k[:, 0:128])
                        e = mm(bank(b, 128, 384), q[:, 128:256], k)
                    e.then_inc(d_scores, 1)

                def turn(h):
                    pe.wait_ge(d_p, h + 1)
                    for g in range(DG):
                        for b in range(3):
                            e = nc.tensor.transpose(bank(3 * (h % 2) + g, 128 * b, 128 * b + 128),
                                                    Pd[h % 2][:, g, 128 * b:128 * b + 128], ident)
                    e.then_inc(d_ptps, 1)

                def pv(h):
                    pe.wait_ge(d_pt, h + 1)
                    r = 64 * (h % 2)
                    o = ps[r:r + 64, 6 + h // 2, 0:TOK]
                    for g in range(DG):
                        vd = [qkv[:, tt, 2 * DW + 64 * (4 * g + h):2 * DW + 64 * (4 * g + h) + 64] for tt in range(2)]
                        mm(o, vd[0], PTd[h % 2][:, g, 0:256], start=(g == 0), stop=False, skip_group_check=True)
                        e = mm(o[:, 128:256], vd[1], PTd[h % 2][:, g, 256:384], start=False, stop=(g == DG - 1),
                               skip_group_check=True)
                    if h % 2:
                        e.then_inc(d_o, 1)
                scores(0)
                for h in range(DH):
                    if h < 3:
                        scores(h + 1)
                    turn(h)
                    if h:
                        pv(h - 1)
                pv(3)
                pe.wait_ge(*DV2.at(0, "ylru_lo"))
                for k in range(6):
                    if k >= 4:
                        pe.wait_ge(d_lo, k - 3)
                    km(AT["od_out"] + k, 8 + k, k == 0, k == 5)

            t, F = 0, 0
            for l in range(DEPTH):
                norm(t)
                ffn(AT["ffa", l], F, t); F += FT; t += 1
                norm(t)
                mixer(l, t); t += 1
                norm(t)
                ffn(AT["ffb", l], F, t); F += FT; t += 1

            for i, mix in enumerate((even, odd)):
                norm(t)
                mix(t); t += 1
                norm(t)
                ffn(AT["ffn", i], F, t); F += FT; t += 1


def kernel(**inputs):
    import concourse.bacc as bacc
    from concourse.bass_utils import run_bass_kernel_spmd as run

    a = {k: np.asarray(v) for k, v in inputs.items()}
    stream = np.zeros((UNITS, PART, UC), np.float32)

    def fm(u, w):
        n = w.shape[1] // 128
        stream[u:u + n] = w.reshape(8, 128, n, 128).transpose(2, 1, 0, 3).reshape(n, 128, UC)

    def tm(u, w, kts=2):
        n, c = w.shape[0] // (128 * kts), w.shape[1]
        stream[u:u + n].reshape(n, 128, kts, UC // kts)[:, :, :, :c] = w.reshape(n, kts, 128, c).transpose(0, 2, 1, 3)

    def km(u, w):
        stream[u:u + w.shape[0] // 128] = w.reshape(-1, 128, DM)

    def ffn(u, gate, up, down):
        g = np.empty((3 * FT, 128, UC), np.float32)
        gt, ut = (w.reshape(8, 128, FT, 128).transpose(2, 1, 0, 3).reshape(FT, 128, UC) for w in (gate, up))
        dt = down.reshape(FT, 128, DM)
        g[0], g[1] = gt[0], ut[0]
        g[2:3 * FT - 1:3], g[3:3 * FT - 1:3], g[4:3 * FT - 1:3], g[3 * FT - 1] = gt[1:], ut[1:], dt[:-1], dt[-1]
        stream[u:u + 3 * FT] = g

    for l in range(DEPTH):
        for n in ("ffa", "ffb"):
            w = a[n + "_w_in"][l]
            ffn(AT[n, l], w[:, :FF], w[:, FF:], a[n + "_w_out"][l])
        cuts = np.cumsum([QR, KVR, LR, 512, 512, 512, GH, GH, 512, 1536])
        cq, ckv, kr, gq, gk, gv, gb, ga, gz, m, gl = np.split(a["w_in"][l], cuts, axis=1)
        tm(AT["small", l], np.concatenate([cq, ckv, kr, gb, ga], 1))
        fm(AT["gdn", l], np.concatenate([gq, gk, gv], 1))
        fm(AT["z", l], gz)
        for i in range(3):
            tm(AT["moba", l] + 4 * i, m[:, 512 * i:512 * i + 512])
        for i in range(3):
            fm(AT["gates_" + "abc"[i], l], gl[:, 1024 * i:1024 * i + 1024])
        uq, ukv = a["mla_w_uq"][l], a["mla_w_ukv"][l]
        tm(AT["up", l], uq[:, :512])
        tm(AT["up", l] + 1, uq[:, 512:])
        stream[AT["up", l] + 2] = ukv.reshape(128, LH, 2, 64).transpose(0, 2, 1, 3).reshape(128, UC)
        b = a["w_branch"][l].reshape(3, 4, 128, 4, 256).transpose(3, 0, 2, 1, 4).reshape(12, 128, UC)
        stream[AT["branch", l]:AT["branch", l] + 12] = b
        km(AT["out", l], a["w_out"][l])
        ffn(AT["ffn", l], a["ffn_w_gate_2"][l], a["ffn_w_up_2"][l], a["ffn_w_down_2"][l])
    scb, scc, scx, cfa, cfg = (w.reshape(DM, 4, 128) for w in np.split(a["ev_w_in_2"][0], 5, axis=1))
    fm(AT["ev_in"], np.stack([cfa, cfg], 2).reshape(DM, 1024))
    fm(AT["ev_in"] + 8, np.stack([scc, scx], 2).reshape(DM, 1024))
    fm(AT["ev_in"] + 16, scb.reshape(DM, 512))
    km(AT["ev_out"], a["ev_w_out_2"][0])
    od = a["od_w_in_2"][0]
    fm(AT["lru_in"], od[:, :1024])
    for i in range(4):
        tm(AT["dil_in"] + 4 * i, od[:, 1024 + 512 * i:1536 + 512 * i])
    tm(AT["dil_in"] + 16, od[:, 3072:], 4)
    km(AT["od_out"], a["od_w_out_2"][0])

    params = np.zeros((PART, N_HALVED + N_WHOLE), np.float32)

    def put(name, v, where=WHOLE, base=N_HALVED):
        lo, hi = where[name]
        params[:, base + lo:base + hi] = v

    def feat(v):
        return np.moveaxis(v.reshape(*v.shape[:-1], -1, 128), -1, 0)

    halved = lambda name, v: put(name, v, HALVED, 0)
    taps = lambda v: np.swapaxes(feat(v), 1, 2).reshape(128, -1)
    for l in range(DEPTH):
        halved(("gconv", l), taps(a["gdn_conv"][l]))
        halved(("gout", l), a["gdn_out_norm"][l][:, None])
        halved(("fconv", l), taps(np.concatenate([a["ffn_conv_w_2"][l], a["ffn_conv_b_2"][l][None]])))
        for n, k in (("ffa", "ffa_norm"), ("mix", "mix_norm"), ("ffb", "ffb_norm"), ("mix2", "mix_norm_g_2"),
                     ("ffn2", "ffn_norm_g_2")):
            put((n, l), feat(a[k][l]))
        put(("cgain", l), feat(np.concatenate([a["mla_cq_norm"][l], a["mla_ckv_norm"][l]])))
        for n, k in (("mlaq", "mla_q_norm"), ("mlak", "mla_k_norm"), ("mobaq", "moba_q_norm"), ("mobak", "moba_k_norm"),
                     ("alog", "gdn_a_log"), ("dtb", "gdn_dt_bias")):
            put((n, l), a[k][l][None])
    halved("cfconv", taps(a["ev_cf_conv_w_2"][0]))
    halved("lng", feat(a["ev_cf_ln_g_2"][0]))
    halved("lnb", feat(a["ev_cf_ln_b_2"][0]))
    halved("lru_ba", feat(a["od_lru_ba_2"][0]))
    halved("lru_bx", feat(a["od_lru_bx_2"][0]))
    put("scconv", taps(a["ev_sc_conv_w_2"][0]))
    put("cfbias", feat(a["ev_cf_conv_b_2"][0]))
    put("lruconv", taps(a["od_lru_conv_w_2"][0]))
    put("lrubias", feat(a["od_lru_conv_b_2"][0]))
    put("lam", feat(a["od_lru_lam_2"][0]))
    put("dilq", a["od_q_norm_g_2"][0][None])
    put("dilk", a["od_k_norm_g_2"][0][None])

    con, late = constants()
    for name, k in (("wa", "od_lru_wa_2"), ("wx", "od_lru_wx_2")):
        lo, _ = LATE[name]
        for h in range(8):
            r, c = 64 * (h % 2), lo + 128 * (h // 2) + 64 * (h % 2)
            late[r:r + 64, c:c + 64] = a[k][0][h]

    xt = np.ascontiguousarray(a["x"][0].reshape(TOK, KC, 128).transpose(2, 1, 0))
    nc = bacc.Bacc("TRN2", target_bir_lowering=False, num_devices=1)
    arrays = {"stream": stream, "params": params, "consts": con, "late": late, "x_in": xt}
    args = [nc.dram_tensor(k, v.shape, F32, kind="ExternalInput").ap() for k, v in arrays.items()]
    args.append(nc.dram_tensor("out", (PART, KC, TOK), F32, kind="ExternalOutput").ap())
    build(nc, *args)
    r = run(nc, [arrays], core_ids=[0])
    return r.results[0]["out"].transpose(2, 1, 0).reshape(1, TOK, DM)
```

```python
from contextlib import ExitStack

import numpy as np

import concourse.bass as bass
from concourse import mybir

F32 = mybir.dt.float32
F32R = mybir.dt.float32r
ACT = mybir.ActivationFunctionType
ALU = mybir.AluOpType
AX = mybir.AxisListType

PART = 128
TOK = 256
TT = TOK // PART
DM = 1024
KC = DM // PART
FF = 2816
FT = FF // PART
DEPTH = 2
EPS = 1e-6
NEG = -1e30
UC = 1024
RAW = 3
SLOTS = 6
AHEAD = SLOTS - 1

MH, MD = 8, 64
LH, LN, LR, LV = 8, 64, 32, 64
LD = LN + LR
QR, KVR = 256, 128
GH, GD, GK = 4, 128, 4
CFK, SCK = 31, 3
POOL_TAPS = 10
DG, DH, DD = 3, 4, 64
DW = DG * DH * DD
LK = 4
SMALL = QR + KVR + LR + 2 * GH
LEVELS = 7
FFN_NORMS = (0, 2, 3, 5, 7, 9)


def plan():
    at, n = {}, 0
    def run(name, count):
        nonlocal n
        at[name] = n
        n += count
    for l in range(DEPTH):
        run(("ffa", l), 3 * FT)
        run(("small", l), 4)
        run(("gdn", l), 12)
        run(("z", l), 4)
        run(("moba", l), 12)
        run(("gates_a", l), 8)
        run(("gates_b", l), 8)
        run(("up", l), 3)
        run(("gates_c", l), 8)
        run(("branch", l), 12)
        run(("out", l), 8)
        run(("ffb", l), 3 * FT)
    run("ev_in", 20)
    run("ev_out", 8)
    run(("ffn", 0), 3 * FT)
    run("lru_in", 8)
    run("dil_in", 18)
    run("od_out", 6)
    run(("ffn", 1), 3 * FT)
    at["end"] = n
    return at


AT = plan()
UNITS = AT["end"]
NORMS = 5 * DEPTH


def columns(items):
    at, n = {}, 0
    for name, width in items:
        at[name] = (n, n + width)
        n += width
    return at, n


HALVED, N_HALVED = columns(
    [(("gconv", l), 48) for l in range(DEPTH)] + [(("gout", l), 1) for l in range(DEPTH)]
    + [("cfconv", 4 * CFK), ("lng", 4), ("lnb", 4), ("lru_ba", 4), ("lru_bx", 4)]
    + [(("fconv", i), 4 * FT) for i in range(DEPTH)])
WHOLE, N_WHOLE = columns(
    [((n, l), 8) for n in ("ffa", "mix", "ffb", "mix2", "ffn2") for l in range(DEPTH)]
    + [(("cgain", l), 3) for l in range(DEPTH)]
    + [((n, l), w) for n, w in (("mlaq", LD), ("mlak", LD), ("mobaq", MD), ("mobak", MD), ("alog", GH), ("dtb", GH))
       for l in range(DEPTH)]
    + [("scconv", 12), ("cfbias", 4), ("lruconv", 16), ("lrubias", 4), ("lam", 4), ("dilq", DD), ("dilk", DD)])
CONST, N_CONST = columns(
    [("ident", 128), ("tri", 128), ("m0", 128), ("m0t", 128), ("mt", (LEVELS - 1) * 128), ("causal", 128),
     ("cosm", TT * 32), ("sinm", TT * 32), ("cosl", TT * 16), ("sinl", TT * 16)])
LATE, N_LATE = columns([("dneg", 9 * 128), ("wa", 512), ("wx", 512)])


def constants():
    out, late = np.zeros((PART, N_CONST), np.float32), np.zeros((PART, N_LATE), np.float32)
    i, j = np.arange(128)[:, None], np.arange(128)[None, :]

    def put(name, a):
        lo, hi = CONST[name]
        out[:, lo:hi] = a.reshape(128, hi - lo)

    put("ident", (i == j).astype(np.float32))
    put("tri", (i <= j).astype(np.float32))
    masks = []
    for m in range(LEVELS):
        s = 1 << m
        masks.append(((i // (2 * s) == j // (2 * s)) & ((i // s) % 2 == 1) & ((j // s) % 2 == 0)).astype(np.float32))
    put("m0", masks[0])
    put("m0t", masks[0].T)
    put("mt", np.stack([m.T for m in masks[1:]], 1))
    causal = j <= i
    neg = []
    for step, band in ((1, j >= i), (4, (i - j) % 4 == 0), (16, (i - j) % 16 == 0)):
        same = causal & ((i - j) % step == 0)
        neg += [same, band, same]
    put("causal", np.where(causal, 0.0, NEG).astype(np.float32))
    lo, hi = LATE["dneg"]
    late[:, lo:hi] = np.stack([np.where(m, 0.0, NEG).astype(np.float32) for m in neg], 1).reshape(128, hi - lo)
    for half, c, s in ((32, "cosm", "sinm"), (16, "cosl", "sinl")):
        inv = np.float32(10000.0) ** (-np.arange(half, dtype=np.float32) * np.float32(2.0) / np.float32(2 * half))
        ang = np.arange(TOK, dtype=np.float32)[:, None] * inv[None].astype(np.float32)
        for name, f in ((c, np.cos), (s, np.sin)):
            put(name, f(ang).astype(np.float32).reshape(TT, 128, half).transpose(1, 0, 2))
    return out, late


class Events:

    def __init__(self, sem, steps):
        self.sem, self.steps, self.done = sem, {s: n for n, s in enumerate(steps)}, 0

    def at(self, l, step):
        return self.sem, l * len(self.steps) + self.steps[step] + 1

    def sig(self, l, step):
        self.done += 1
        assert self.at(l, step)[1] == self.done, (l, step)
        return self.sem, 1


LV_STEPS = [(k, m, t) for m in range(1, LEVELS) for k, t in (("U", 0), ("U", 1), ("X", 0), ("T", 0), ("X", 1), ("T", 1))
            if not (m == LEVELS - 1 and k == "X")]
PE_STEPS = (["cT", "cums", "R", "stat", "bc", "ktok", "vtok", "G", "QK", "AT", "QKT"] + LV_STEPS
            + ["u", "wT", "S1", "ob0", "wS", "oa", "ob1", "mobaT", "oT", "mlaTq", "mlaTk"])
DVE_STEPS = (["z0", "cvar", "cn", "c32", "c_lo", "silu", "g", "tg", "cumcp", "gld", "Et", "gvar", "diag", "qn", "kn", "kgd", "vb", "A", "QK", "X0", "XT0", "mobavar"]
             + [s for s in LV_STEPS if s[0] != "U" and s[1] < LEVELS - 1] + ["mobaqk"]
             + [s for s in LV_STEPS if s[0] != "U" and s[1] == LEVELS - 1]
             + ["vn0", "S1", "tq", "vn1", "O1", "ovar", "on", "oz", "oz_lo",
                "kr", "mlavark", "mlavarq", "mlaqk"])
ACT_STEPS = (["sm", "spe", "csq", "c_hi", "gsq", "egc", "kds", "E", "AT", "QKT", "mobasq"] + [s for s in LV_STEPS if s[0] == "U"]
             + ["u1", "wT", "O0", "osq", "mobaT", "oz_hi", "up", "mlasq", "mlaTq", "mlaTk"])
POOL_STEPS = (["crs", "grs"] + [("ATM", m) for m in range(1, 4)] + ["mobars"] + [("ATM", m) for m in range(4, LEVELS)]
              + ["ors", "mlarsk", "mlarsq"])
PREP = 4

PE2_STEPS = ["mean", "lnstat", "lnbc", "r", "i", "dilT"]
DVE2_STEPS = ["ysc_lo", "cf", "cen", "lnvar", "lndiag", "yb", "o2", "o2_lo", "lamz", "xc", "sp4", "gin", "dvar0", "dvar1", "dqk", "xin", "m2",
              "ylru", "ylru_lo"]
ACT2_STEPS = ["ysc_hi", "lnsq", "lnth", "o2_hi", "spe", "lgsq", "gth", "dsq", "rth", "ith", "a", "tq", "dilT", "mult", "ylru_hi"]
POOL2_STEPS = ["lnrs", "drs0", "drs1"]


def build(nc, stream, params, consts, late_in, x_in, out):
    with ExitStack() as ctx:
        def sb(name, shape, dt=F32):
            return ctx.enter_context(nc.sbuf_tensor(name, shape, dt))

        def sem(name):
            return ctx.enter_context(nc.semaphore(name))

        raw = sb("raw", [PART, RAW, UC])
        w_hi = sb("w_hi", [PART, SLOTS, UC], F32R)
        w_lo = sb("w_lo", [PART, SLOTS, UC], F32R)
        x = sb("x", [PART, KC, TOK])
        tmp = sb("tmp", [PART, KC, TOK])
        a_hi = sb("a_hi", [PART, 20, TOK], F32R)
        a_lo = sb("a_lo", [PART, 20, TOK], F32R)
        par = sb("par", [PART, N_HALVED + N_WHOLE])
        con = sb("con", [PART, N_CONST])
        ones = sb("ones", [PART, PART])
        nhalf = sb("nhalf", [PART, 64])
        sc = sb("sc", [PART, 512])
        diag = sb("diag", [PART, TOK])
        gates = sb("gates", [PART, 24, TOK])
        arena = sb("arena", [PART, 13184])
        ps = ctx.enter_context(nc.psum_tensor("ps", [PART, 8, 512], F32))

        raw_loaded = [sem(f"raw_loaded{i}") for i in range(RAW)]
        params_loaded, x_loaded, stored = sem("params_loaded"), sem("x_loaded"), sem("stored")
        consts_set, halved = sem("consts_set"), sem("halved")
        hi_ready, split_ready, unit_used = sem("hi_ready"), sem("split_ready"), sem("unit_used")
        consts_loaded = sem("consts_loaded")
        sq_sum, rrow_ready, gs_ready = sem("sq_sum"), sem("rrow_ready"), sem("gs_ready")
        x_ready, sq_ready, stat_ready, var_ready = sem("x_ready"), sem("sq_ready"), sem("stat_ready"), sem("var_ready")
        rs_ready, diag_ready, bc_ready = sem("rs_ready"), sem("diag_ready"), sem("bc_ready")
        hn_ready, h_hi_ready, h_ready = sem("hn_ready"), sem("h_hi_ready"), sem("h_ready")
        gate_act, gu_ready, gu_hi_ready, gu_split = sem("gate_act"), sem("gu_ready"), sem("gu_hi_ready"), sem("gu_split")
        conv_in, conv_used = sem("conv_in"), sem("conv_used")
        dve_chain, act_chain, pool_chain = sem("dve_chain"), sem("act_chain"), sem("pool_chain")
        loop_chain = sem("loop_chain")
        cb_ready, conv_ready, silu_th = sem("cb_ready"), sem("conv_ready"), sem("silu_th")
        z_th, zs_ready, m_ready, gate_evac = sem("z_th"), sem("zs_ready"), sem("m_ready"), sem("gate_evac")
        scores_ready, nmax_ready, exp_done, p_ready = sem("scores_ready"), sem("nmax_ready"), sem("exp_done"), sem("p_ready")
        pt_ps, pt_ready, o_ready, o_hi, o_split = sem("pt_ps"), sem("pt_ready"), sem("o_ready"), sem("o_hi"), sem("o_split")
        merge_read, mix_ready, mix_hi, mix_split = sem("merge_read"), sem("mix_ready"), sem("mix_hi"), sem("mix_split")
        pe_ev = [Events(sem("pe_step"), PE_STEPS)]
        dve_ev = [Events(sem("dve_step"), DVE_STEPS)]
        act_ev = [Events(sem("act_step"), ACT_STEPS)]
        pool_ev = [Events(sem("pool_step"), POOL_STEPS)]
        PE, DV, AC, PO = pe_ev[0], dve_ev[0], act_ev[0], pool_ev[0]
        PE2, DV2 = Events(sem("pe_step2"), PE2_STEPS), Events(sem("dve_step2"), DVE2_STEPS)
        AC2, PO2 = Events(sem("act_step2"), ACT2_STEPS), Events(sem("pool_step2"), POOL2_STEPS)
        late_loaded, loop_chain2 = sem("late_loaded"), sem("loop_chain2")
        part_sum, tap_ready = sem("part_sum"), sem("tap_ready")
        cf_th, sc_copy, pair_read, b_read = sem("cf_th"), sem("sc_copy"), sem("pair_read"), sem("b_read")
        lru_copy, dil_copy = sem("lru_copy"), sem("dil_copy")
        d_scores, d_nmax, d_exp, d_p = sem("d_scores"), sem("d_nmax"), sem("d_exp"), sem("d_p")
        d_ptps, d_pt, d_o, d_hi, d_lo = sem("d_ptps"), sem("d_pt"), sem("d_o"), sem("d_hi"), sem("d_lo")

        def before(t):
            return t - sum(n < t for n in FFN_NORMS)

        def gate_at(l, i):
            return AT["gates_" + "abc"[i // 8], l] + i % 8

        MOBA_FILL = {n: 8 + n for n in range(8)}
        MLA_FILL = {2 * n: 16 + PREP + n for n in range(8 - PREP)}

        def half(name, i=0, n=1):
            lo, _ = HALVED[name]
            return par[:, lo + i:lo + i + n]

        def whole(name, i=0, n=1):
            lo, _ = WHOLE[name]
            return par[:, N_HALVED + lo + i:N_HALVED + lo + i + n]

        def const(name, i=0, n=None):
            lo, hi = CONST[name]
            return con[:, lo + i:(hi if n is None else lo + i + n)]

        ident = const("ident")

        def bank(b, lo=0, hi=512):
            return ps[:, b, lo:hi]

        def flat(ap):
            return ap.rearrange("p a b -> p (a b)")

        def over(ap, n):
            return ap.unsqueeze(2).broadcast_to([PART, ap.shape[1], n])

        def each(ap, n):
            return ap.unsqueeze(1).broadcast_to([PART, n, ap.shape[1]])

        def reg(lo, *dims):
            n = int(np.prod(dims))
            v = arena[:, lo:lo + n]
            return v if len(dims) == 1 else v.rearrange("p (a b) -> p a b", b=dims[-1])

        gup = gates[:, 8:24, :].rearrange("p a b -> p (a b)")
        mqkv = reg(0, 6, 512)
        zs = reg(3072, 4, TOK)
        y = reg(4096, 12, TOK)
        yth = reg(7168, 12, TOK)
        X = reg(7168, 8, 128)
        XT = reg(8192, 8, 128)
        tg = reg(7168, 8, 128)
        vb = reg(9216, 8, 128)
        kgd = reg(10240, 8, 128)
        O = reg(11264, 8, 128)
        small = reg(12288, TT, SMALL)
        cb = gup[:, 0:12 * (TOK + 3)].rearrange("p (a b) -> p a b", b=TOK + 3)
        E = gup[:, 0:1024].rearrange("p (a b) -> p a b", b=128)
        QKT = E
        A = gup[:, 1024:2048].rearrange("p (a b) -> p a b", b=128)
        U = A
        QK = gup[:, 2048:3072].rearrange("p (a b) -> p a b", b=128)
        VN = QK
        ATr = gup[:, 3072:4096].rearrange("p (a b) -> p a b", b=128)
        S1 = gup[:, 1024:1536]
        wT = gup[:, 1536:2048]
        tmpf = flat(tmp[:, :, :])
        ATM = [tmpf[:, 0:1024].rearrange("p (a b) -> p a b", b=128), tmpf[:, 1024:2048].rearrange("p (a b) -> p a b", b=128)]
        diag16 = tmpf.rearrange("p (a b) -> p a b", b=128)
        qTm, kTm = reg(3072, 4, TOK), reg(4096, 4, TOK)
        rA, rB = reg(6144, 1536), reg(7680, 1536)
        Pb = [reg(9216, 384), reg(9600, 384)]
        PTb = [reg(9984, 384), reg(10368, 384)]
        ql, kl = reg(0, 16, LD), reg(1536, 16, LD)
        vl = reg(3072, TT, 512)
        csq = tmpf[:, 0:768].rearrange("p (a b) -> p a b", b=QR + KVR)
        cn = tmpf[:, 768:1536].rearrange("p (a b) -> p a b", b=QR + KVR)
        c32 = tmp[:, 0:3, :]
        sA, sB = reg(6144, 1024), gup[:, 2048:3072]
        qTl = arena[0:LD, 6144:8192].rearrange("p (a b) -> p a b", b=TOK)
        kTl = tmp[0:LD, :, :]
        th2, a2, gu2 = reg(0, 2, TOK), reg(512, 2, TOK), reg(1024, 2, TOK)
        mA, mB = reg(0, 2, 512), reg(1024, 512)
        gh2 = reg(1536, 2, TOK)
        gus = reg(2048, 2, 512)
        rrow = reg(3072, TOK)
        F2 = 2 * DEPTH * FT
        gflat = gates[:, :, :].rearrange("p a b -> p (a b)")
        late = gflat[:, 0:N_LATE]
        dneg = late[:, 0:9 * 128].rearrange("p (a b) -> p a b", b=3 * 128)
        gr = lambda lo, *d: (gflat[:, lo:lo + int(np.prod(d))] if len(d) == 1 else
                             gflat[:, lo:lo + int(np.prod(d))].rearrange("p (a b) -> p a b", b=d[-1]))
        ub = reg(0, 4, TOK + CFK - 1)
        cf = reg(1152, 4, TOK)
        cx = reg(2304, 4, TOK + SCK - 1)
        csb = reg(3400, 4, TOK)
        ysc = reg(4500, 4, TOK)
        o2 = reg(5600, 8, TOK)
        lnth = reg(7700, 4, TOK)
        cfp = reg(8724, 4, TOK)
        tapped = reg(9748, 8, TOK)
        lx = reg(0, 4, TOK + LK - 1)
        lg = reg(1040, 4, TOK)
        xc = reg(2064, 4, TOK)
        qkv = reg(3088, TT, 3 * DW)
        Pd = [reg(7696, 3, 384), reg(8848, 3, 384)]
        PTd = [reg(10000, 3, 384), reg(11152, 3, 384)]
        dsq = arena[:, 10000:10000 + 2 * 2 * DW].rearrange("p (a b) -> p a b", b=2 * DW)
        qTd, kTd = reg(0, 6, TOK), reg(1536, 6, TOK)
        thr, thi, aa = gr(2200, 4, TOK), gr(3224, 4, TOK), gr(4248, 4, TOK)
        tqb, gin = tmp[:, 0:4, :], tmp[:, 4:8, :]

        block = ctx.enter_context(nc.Block())

        @block.sync
        def _(sp):
            sp.dma_start(x[:], x_in).then_inc(x_loaded, 16)
            sp.dma_start(par[:], params).then_inc(params_loaded, 16)
            for b in range(RAW):
                sp.dma_start(raw[:, b, :], stream[b]).then_inc(raw_loaded[b], 16)
            sp.dma_start(con[:], consts).then_inc(consts_loaded, 16)
            rounds = (UNITS - RAW) // RAW
            with sp.Fori(0, rounds) as r:
                for b in range(RAW):
                    sp.wait_ge(split_ready, RAW * r + b + 1)
                    sp.dma_start(raw[:, b, :], stream[bass.ds(RAW * r + RAW + b, 1)].rearrange("o p n -> (o p) n")
                                 ).then_inc(raw_loaded[b], 16)
            for u in range(RAW + rounds * RAW, UNITS):
                sp.wait_ge(split_ready, u - RAW + 1)
                sp.dma_start(raw[:, u % RAW, :], stream[u]).then_inc(raw_loaded[u % RAW], 16)
            for c in range(KC):
                sp.wait_ge(x_ready, 8 * (NORMS - 1) + c + 1)
                sp.dma_start(out[:, c, :], x[:, c, :]).then_inc(stored, 16)
            sp.wait_ge(stored, 16 * KC)
            sp.wait_ge(late_loaded, 16)

        @block.scalar
        def _(act):
            chain = [0]

            def link(ins):
                chain[0] += 1
                ins.then_inc(act_chain, 1)
                act.wait_ge(act_chain, chain[0])

            def split(u, j=0):
                if u >= UNITS:
                    return
                act.wait_ge(raw_loaded[u % RAW], 16 * (u // RAW + 1 + 2 * j))
                if u >= SLOTS:
                    act.wait_ge(unit_used, u - SLOTS + 1 + 6 * j)
                nc.scalar.activation(w_hi[:, u % SLOTS, :], raw[:, u % RAW, :], ACT.Copy).then_inc(hi_ready, 1)

            def norm(t):
                for c in range(KC):
                    act.wait_ge(x_ready, 8 * (t - 1) + c + 1)
                    nc.scalar.activation(tmp[:, c, :], x[:, c, :], ACT.Square).then_inc(sq_ready, 1)
                for c in range(KC):
                    act.wait_ge(hn_ready, 8 * before(t) + c + 1)
                    nc.scalar.activation(a_hi[:, c, :], tmp[:, c, :], ACT.Copy).then_inc(h_hi_ready, 1)

            def ffn_norm(t, gain):
                def high(c):
                    nc.scalar.activation(a_hi[:, c, :], x[:, c, :], ACT.Copy, scale=whole(gain, c)).then_inc(h_hi_ready, 1)

                def square(c):
                    nc.scalar.activation(tmp[:, c, :], x[:, c, :], ACT.Square).then_inc(sq_ready, 1)

                if t == 0:
                    act.wait_ge(x_loaded, 16)
                    act.wait_ge(params_loaded, 16)
                    for c in range(KC):
                        high(c)
                    split(0)
                    for c in range(KC):
                        square(c)
                    for u in range(1, AHEAD):
                        split(u)
                    return
                for c in range(KC):
                    act.wait_ge(x_ready, 8 * (t - 1) + c + 1)
                    high(c)
                    square(c)

            def gating(F, p, j=0):
                act.wait_ge(gs_ready, F + 1 + 2 * j)
                nc.scalar.activation(th2[:, p, :], gus[:, p, 0:TOK], ACT.Tanh, scale=0.5).then_inc(gate_act, 1)

            def gu_high(F, p, j=0):
                act.wait_ge(gu_ready, F + 1 + 2 * j)
                nc.scalar.activation(a_hi[:, 8 + p, :], gu2[:, p, :], ACT.Copy).then_inc(gu_hi_ready, 1)

            def ffn(n0, F0, conv=False):
                def gate(f, between=(), j=0):
                    F, p = F0 + f, f % 2
                    if conv:
                        current_tap(F, p, j)
                        for u in between[:1]:
                            split(u, j)
                        act.wait_ge(conv_used, F - F2 + 1 + 2 * j)
                        nc.scalar.activation(th2[:, p, :], gh2[:, p, :], ACT.Tanh).then_inc(gate_act, 1)
                        for u in between[1:]:
                            split(u, j)
                    else:
                        gating(F, p, j)
                        for u in between:
                            split(u, j)
                    gu_high(F, p, j)

                if n0 == AT["ffa", 1]:
                    split(n0 - 1 + AHEAD)
                split(n0 + AHEAD); split(n0 + 1 + AHEAD)
                gate(0)
                def tile(f, u, j=0):
                    split(u + AHEAD, j)
                    gate(f, (u + 1 + AHEAD, u + 2 + AHEAD), j)
                last = int(n0 + 3 * FT == UNITS)
                with act.Fori(0, (FT - 2) // 2 - last) as j:
                    tile(1, n0 + 2, j)
                    tile(2, n0 + 5, j)
                for f in range(FT - 1 - 2 * last, FT - 1):
                    tile(f, n0 + 3 * f - 1)
                split(n0 + 3 * FT - 4 + AHEAD)
                gate(FT - 1)
                for u in range(n0 + 3 * FT - 3, n0 + 3 * FT - 1):
                    split(u + AHEAD)

            def gate_tile(l, i):
                act.wait_ge(unit_used, gate_at(l, i) + 1)
                nc.scalar.activation(gates[:, i, :], bank(6 + i % 2, 0, TOK), ACT.Tanh, scale=0.5).then_inc(gate_evac, 1)

            def exp_scores(n, scale):
                p = n % 2
                act.wait_ge(nmax_ready, n + 1)
                s = sc[:, 8 + 4 * p:12 + 4 * p]
                nc.scalar.activation(Pb[p][:, 0:128], bank(p, 0, 128), ACT.Exp, bias=s[:, 0:1], scale=scale,
                                     accum_out=s[:, 2:3])
                nc.scalar.activation(Pb[p][:, 128:384], bank(p, 128, 384), ACT.Exp, bias=s[:, 1:2], scale=scale,
                                     accum_out=s[:, 3:4]).then_inc(exp_done, 1)

            def evac_pt(n):
                act.wait_ge(pt_ps, n + 1)
                nc.scalar.activation(PTb[n % 2], bank(2 + n % 2, 0, 384), ACT.Copy).then_inc(pt_ready, 1)

            def o_high(pair, chunk):
                act.wait_ge(o_ready, pair + 1)
                nc.scalar.activation(a_hi[:, chunk, :], bank(4 + pair % 2, 0, TOK), ACT.Copy).then_inc(o_hi, 1)

            def attention(l, kind, fill, scale, chunk):
                n0 = 16 * l + 8 * kind
                for n in range(8):
                    if n in fill:
                        split(gate_at(l, fill[n]) + AHEAD)
                    exp_scores(n0 + n, scale)
                    if n in fill:
                        gate_tile(l, fill[n])
                    evac_pt(n0 + n)
                    if n % 2 == 0 and n:
                        o_high(8 * l + 4 * kind + n // 2 - 1, chunk + n // 2 - 1)
                o_high(8 * l + 4 * kind + 3, chunk + 3)

            def mixer(l):
                a = sc[:, 32:40].rearrange("p (a b) -> p a b", b=4)
                for i in range(-1, 4):
                    split(AT["small", l] + i + AHEAD)
                act.wait_ge(unit_used, AT["small", l] + 4)
                nc.scalar.activation(small, ps[:, 0:2, 0:SMALL], ACT.Copy).then_inc(*AC.sig(l, "sm"))
                act.wait_ge(*AC.at(l, "sm"))
                nc.scalar.activation(sc[:, 40:48].rearrange("p (a b) -> p a b", b=4), small[:, :, 416:420], ACT.Tanh, scale=0.5)
                act.wait_ge(*DV.at(l, "z0"))
                link(nc.scalar.activation(sc[:, 48:56], sc[:, 32:40], ACT.Abs))
                nc.scalar.activation(sc[:, 56:60], whole(("alog", l), 0, 4), ACT.Exp)
                nc.scalar.activation(sc[:, 64:72], sc[:, 48:56], ACT.Exp, scale=-1.0).then_inc(*AC.sig(l, "spe"))
                nc.scalar.activation(csq, small[:, :, 0:384], ACT.Square).then_inc(*AC.sig(l, "csq"))
                def th(p):
                    act.wait_ge(conv_ready, 6 * l + p + 1)
                    nc.scalar.activation(yth[:, 2 * p:2 * p + 2, :], y[:, 2 * p:2 * p + 2, :], ACT.Tanh).then_inc(silu_th, 1)
                for p in range(6):
                    u = AT["gdn", l] + 2 * p
                    split(u + AHEAD); split(u + 1 + AHEAD)
                    act.wait_ge(unit_used, u + 2)
                    nc.scalar.activation(cb[:, 2 * p:2 * p + 2, 3:], bank((2 + p) % 6).rearrange("p (a b) -> p a b", b=TOK),
                                         ACT.Copy).then_inc(cb_ready, 1)
                    if p:
                        th(p - 1)
                    if p == 5:
                        act.wait_ge(*DV.at(l, "c32"))
                        nc.scalar.activation(a_hi[:, 8:11, :], c32, ACT.Copy).then_inc(*AC.sig(l, "c_hi"))
                for q in range(2):
                    u = AT["z", l] + 2 * q
                    split(u + AHEAD); split(u + 1 + AHEAD)
                    if q == 0:
                        th(5)
                    act.wait_ge(unit_used, u + 2)
                    nc.scalar.activation(flat(zs[:, 2 * q:2 * q + 2, :]), bank(6 + q), ACT.Tanh, scale=0.5).then_inc(z_th, 1)
                act.wait_ge(*DV.at(l, "silu"))
                nc.scalar.activation(flat(tmp[:, :, :]), flat(y[:, 0:8, :]), ACT.Square).then_inc(*AC.sig(l, "gsq"))
                for g in range(3):
                    for i in range(4):
                        split(AT["moba", l] + 4 * g + i + AHEAD)
                    act.wait_ge(unit_used, AT["moba", l] + 4 * g + 4)
                    b = (2, 4, 0)[g]
                    nc.scalar.activation(mqkv[:, 2 * g:2 * g + 2, :], ps[:, b:b + 2, :], ACT.Copy).then_inc(m_ready, 1)
                act.wait_ge(*DV.at(l, "cumcp"))
                nc.scalar.activation(sc[:, 88:96], sc[:, 72:80], ACT.Exp).then_inc(*AC.sig(l, "egc"))
                act.wait_ge(*DV.at(l, "gld"))
                nc.scalar.activation(sc[:, 100:104], sc[:, 96:100], ACT.Exp).then_inc(*AC.sig(l, "kds"))
                act.wait_ge(*DV.at(l, "Et"))
                for b in range(8):
                    e = nc.scalar.activation(E[:, b, :], E[:, b, :], ACT.Exp, bias=sc[:, 72 + b:73 + b])
                e.then_inc(*AC.sig(l, "E"))
                split(AT["gates_a", l] + AHEAD); gate_tile(l, 0)
                split(AT["gates_a", l] + 1 + AHEAD); gate_tile(l, 1)
                act.wait_ge(*PE.at(l, "AT"))
                nc.scalar.activation(ATr, ps[:, 0:2, :], ACT.Copy).then_inc(*AC.sig(l, "AT"))
                act.wait_ge(*PE.at(l, "QKT"))
                nc.scalar.activation(QKT, ps[:, 2:4, :], ACT.Copy).then_inc(*AC.sig(l, "QKT"))
                act.wait_ge(m_ready, 3 * l + 3)
                nc.scalar.activation(sA, flat(mqkv[:, 0:2, :]), ACT.Square)
                nc.scalar.activation(sB, flat(mqkv[:, 2:4, :]), ACT.Square).then_inc(*AC.sig(l, "mobasq"))
                for m in range(1, LEVELS):
                    split(AT["gates_a", l] + 1 + m + AHEAD)
                    for t in range(2):
                        act.wait_ge(*PE.at(l, ("U", m, t)))
                        nc.scalar.activation(U[:, 4 * t:4 * t + 4, :], bank(t).rearrange("p (a b) -> p a b", b=128),
                                             ACT.Copy).then_inc(*AC.sig(l, ("U", m, t)))
                    gate_tile(l, 1 + m)
                act.wait_ge(*PE.at(l, "u"))
                nc.scalar.activation(O[:, 4:8, :], bank(1).rearrange("p (a b) -> p a b", b=128), ACT.Copy).then_inc(*AC.sig(l, "u1"))
                act.wait_ge(*PE.at(l, "wT"))
                nc.scalar.activation(wT, bank(2), ACT.Copy).then_inc(*AC.sig(l, "wT"))
                act.wait_ge(*PE.at(l, "ob0"))
                nc.scalar.activation(O[:, 0:4, :], bank(2).rearrange("p (a b) -> p a b", b=128), ACT.Copy).then_inc(*AC.sig(l, "O0"))
                act.wait_ge(*AC.at(l, "O0"))
                act.wait_ge(*DV.at(l, "O1"))
                nc.scalar.activation(ATM[0], O, ACT.Square).then_inc(*AC.sig(l, "osq"))
                act.wait_ge(*PE.at(l, "mobaT"))
                nc.scalar.activation(flat(kTm), ps[:, 2:4, :], ACT.Copy)
                act.wait_ge(*DV.at(l, "oz"))
                nc.scalar.activation(flat(qTm), ps[:, 0:2, :], ACT.Copy).then_inc(*AC.sig(l, "mobaT"))
                nc.scalar.activation(a_hi[:, 12:16, :], reg(8192, 4, TOK), ACT.Copy).then_inc(*AC.sig(l, "oz_hi"))
                attention(l, 0, MOBA_FILL, MD ** -0.5, 16)
                for i in range(3):
                    split(AT["up", l] + i + AHEAD)
                act.wait_ge(unit_used, AT["up", l] + 3)
                qv = ql.rearrange("p (j h) d -> p j (h d)", j=TT)
                for j in range(TT):
                    nc.scalar.activation(qv[:, j, 0:512], bank(j), ACT.Copy)
                nc.scalar.activation(qv[:, :, 512:768], bank(2).rearrange("p (j n) -> p j n", j=TT), ACT.Copy)
                for j in range(TT):
                    nc.scalar.activation(kl[:, 8 * j:8 * j + 8, 0:LN], bank(3 + j).rearrange("p (h d) -> p h d", d=LN), ACT.Copy)
                nc.scalar.activation(vl, ps[:, 5:7, :], ACT.Copy).then_inc(*AC.sig(l, "up"))
                act.wait_ge(*DV.at(l, "kr"))
                nc.scalar.activation(rB, flat(kl), ACT.Square)
                nc.scalar.activation(rA, flat(ql), ACT.Square).then_inc(*AC.sig(l, "mlasq"))
                for n in range(PREP):
                    split(AT["gates_c", l] + n + AHEAD)
                    gate_tile(l, 16 + n)
                act.wait_ge(*PE.at(l, "mlaTq"))
                nc.scalar.activation(qTl, ps[0:LD, 0:4, :], ACT.Copy).then_inc(*AC.sig(l, "mlaTq"))
                act.wait_ge(*PE.at(l, "mlaTk"))
                nc.scalar.activation(kTl, ps[0:LD, 4:8, :], ACT.Copy).then_inc(*AC.sig(l, "mlaTk"))
                attention(l, 1, MLA_FILL, LD ** -0.5, 8)
                for i in range(12):
                    split(AT["branch", l] + i + AHEAD)
                    if i % 3 == 0 and i:
                        mix_high(l, i // 3 - 1)
                mix_high(l, 3)
                for k in range(KC):
                    split(AT["out", l] + k + AHEAD)

            def mix_high(l, dp):
                act.wait_ge(mix_ready, 4 * l + dp + 1)
                nc.scalar.activation(flat(a_hi[:, 2 * dp:2 * dp + 2, :]), mA[:, dp % 2, :], ACT.Copy).then_inc(mix_hi, 1)

            def current_tap(F, p, j=0):
                lo = HALVED["fconv", (F - F2) // FT][0] + 4 * ((F - F2) % FT)
                w = par[:, lo + 2:lo + 3] if isinstance(j, int) else par[:, bass.ds(lo + 2 + 8 * j, 1)]
                b = par[:, lo + 3:lo + 4] if isinstance(j, int) else par[:, bass.ds(lo + 3 + 8 * j, 1)]
                act.wait_ge(gs_ready, F + 1 + 2 * j)
                nc.scalar.activation(gh2[:, p, :], gus[:, p, 0:TOK], ACT.Identity, scale=w, bias=b).then_inc(conv_in, 1)

            def even():
                n0 = AT["ev_in"]
                split(n0 - 1 + AHEAD)
                tap = [0]

                def products(count):
                    for n in range(tap[0], min(tap[0] + count, 4 * POOL_TAPS)):
                        i, k = 2 * (n // (2 * POOL_TAPS)) + n % 2, CFK - POOL_TAPS + n % (2 * POOL_TAPS) // 2
                        act.wait_ge(pair_read, i + 1)
                        if n >= 8:
                            act.wait_ge(part_sum, n - 7)
                        nc.scalar.activation(tapped[:, n % 8, :], ub[:, i, k:k + TOK], ACT.Copy,
                                             scale=half("cfconv", CFK * i + k)).then_inc(tap_ready, 1)
                    tap[0] += count
                for i in range(4):
                    split(n0 + 2 * i + AHEAD); split(n0 + 2 * i + 1 + AHEAD)
                    act.wait_ge(unit_used, n0 + 2 * i + 2)
                    nc.scalar.activation(lnth[:, i, :], bank(i, TOK, 512), ACT.Tanh, scale=0.5).then_inc(cf_th, 1)
                    if i > 1:
                        products(3)
                for i in range(4):
                    u = n0 + 8 + 2 * i
                    split(u + AHEAD); split(u + 1 + AHEAD)
                    act.wait_ge(unit_used, u + 2)
                    nc.scalar.activation(csb[:, i, :], bank((4, 5, 0, 1)[i], 0, TOK), ACT.Copy).then_inc(sc_copy, 1)
                    products(6)
                for i in range(4):
                    split(n0 + 16 + i + AHEAD)
                    products(4)
                act.wait_ge(b_read, 2)
                nc.scalar.activation(a_hi[:, 8:12, :], o2[:, 0:4, :], ACT.Copy).then_inc(*AC2.sig(0, "ysc_hi"))
                for k in range(4):
                    split(AT["ev_out"] + k + AHEAD)
                act.wait_ge(*DV2.at(0, "cen"))
                nc.scalar.activation(flat(tmp[:, 0:4, :]), flat(cf), ACT.Square).then_inc(*AC2.sig(0, "lnsq"))
                act.wait_ge(*DV2.at(0, "yb"))
                nc.scalar.activation(flat(lnth), flat(cf), ACT.Tanh).then_inc(*AC2.sig(0, "lnth"))
                act.wait_ge(*DV2.at(0, "o2"))
                nc.scalar.activation(a_hi[:, 12:16, :], o2[:, 4:8, :], ACT.Copy).then_inc(*AC2.sig(0, "o2_hi"))
                for k in range(4, 8):
                    split(AT["ev_out"] + k + AHEAD)

            def odd():
                n0 = AT["lru_in"]
                split(n0 - 1 + AHEAD)
                for q in range(4):
                    split(n0 + 2 * q + AHEAD); split(n0 + 2 * q + 1 + AHEAD)
                    act.wait_ge(unit_used, n0 + 2 * q + 2)
                    o = lx[:, 2 * q:2 * q + 2, LK - 1:] if q < 2 else lg[:, 2 * q - 4:2 * q - 2, :]
                    nc.scalar.activation(o, bank(q).rearrange("p (a b) -> p a b", b=TOK), ACT.Copy).then_inc(lru_copy, 1)
                act.wait_ge(*DV2.at(0, "lamz"))
                link(nc.scalar.activation(sc[:, 288:292], sc[:, 284:288], ACT.Abs))
                nc.scalar.activation(sc[:, 292:296], sc[:, 288:292], ACT.Exp, scale=-1.0).then_inc(*AC2.sig(0, "spe"))
                act.wait_ge(lru_copy, 4)
                nc.scalar.activation(gin, lg, ACT.Square).then_inc(*AC2.sig(0, "lgsq"))
                def group(g):
                    n = 4 if g < 4 else 2
                    for i in range(n):
                        split(AT["dil_in"] + 4 * g + i + AHEAD)
                    act.wait_ge(unit_used, AT["dil_in"] + 4 * g + n)
                    b, w = (4, 6, 0, 2, 4)[g], 128 * n
                    nc.scalar.activation(qkv[:, :, 512 * g:512 * g + w], ps[:, b:b + 2, 0:w], ACT.Copy).then_inc(dil_copy, 1)

                group(0)
                act.wait_ge(*DV2.at(0, "gin"))
                nc.scalar.activation(gin, gin, ACT.Tanh, scale=0.7978845608028654).then_inc(*AC2.sig(0, "gth"))
                group(1)
                group(2)
                act.wait_ge(dil_copy, 3)
                nc.scalar.activation(dsq, qkv[:, :, 0:2 * DW], ACT.Square).then_inc(*AC2.sig(0, "dsq"))
                act.wait_ge(*PE2.at(0, "r"))
                for i in range(4):
                    q = nc.scalar.activation(thr[:, i, :], bank(6 + i // 2, (i % 2) * TOK, (i % 2 + 1) * TOK), ACT.Tanh,
                                             scale=0.5, bias=half("lru_ba", i))
                q.then_inc(*AC2.sig(0, "rth"))
                act.wait_ge(*PE2.at(0, "i"))
                for i in range(4):
                    q = nc.scalar.activation(thi[:, i, :], bank(4 + i // 2, (i % 2) * TOK, (i % 2 + 1) * TOK), ACT.Tanh,
                                             scale=0.5, bias=half("lru_bx", i))
                q.then_inc(*AC2.sig(0, "ith"))
                act.wait_ge(*AC2.at(0, "rth"))
                act.wait_ge(*DV2.at(0, "sp4"))
                for i in range(4):
                    k = sc[:, 296 + i:297 + i]
                    q = nc.scalar.activation(aa[:, i, :], thr[:, i, :], ACT.Exp, scale=k, bias=k)
                q.then_inc(*AC2.sig(0, "a"))
                for i in range(4):
                    k = sc[:, 296 + i:297 + i]
                    q = nc.scalar.activation(tqb[:, i, :], thr[:, i, :], ACT.Tanh, scale=k, bias=k)
                q.then_inc(*AC2.sig(0, "tq"))
                group(3)
                group(4)
                act.wait_ge(*PE2.at(0, "dilT"))
                nc.scalar.activation(flat(qTd), ps[:, 0:3, :], ACT.Copy)
                act.wait_ge(*DV2.at(0, "xin"))
                nc.scalar.activation(flat(kTd), ps[:, 3:6, :], ACT.Copy).then_inc(*AC2.sig(0, "dilT"))
                act.wait_ge(*DV2.at(0, "m2"))
                nc.scalar.activation(thr, thr, ACT.Sqrt).then_inc(*AC2.sig(0, "mult"))
                for h in range(DH):
                    p = h % 2
                    act.wait_ge(d_nmax, h + 1)
                    s = sc[:, 304 + 16 * p:320 + 16 * p]
                    for g in range(DG):
                        nc.scalar.activation(Pd[p][:, g, 0:128], bank(3 * p + g, 0, 128), ACT.Exp, bias=s[:, 0:1],
                                             scale=DD ** -0.5, accum_out=s[:, 2 + g:3 + g])
                        q = nc.scalar.activation(Pd[p][:, g, 128:384], bank(3 * p + g, 128, 384), ACT.Exp, bias=s[:, 1:2],
                                                 scale=DD ** -0.5, accum_out=s[:, 5 + g:6 + g])
                    q.then_inc(d_exp, 1)
                    if h:
                        d_turned(h - 1)
                    if h == 1:
                        act.wait_ge(*DV2.at(0, "ylru"))
                        nc.scalar.activation(a_hi[:, 8:12, :], thi, ACT.Copy).then_inc(*AC2.sig(0, "ylru_hi"))
                    if h == 3:
                        d_high(0)
                d_turned(3)
                d_high(1)
                for k in range(6):
                    split(AT["od_out"] + k + AHEAD)

            def d_turned(h):
                act.wait_ge(d_ptps, h + 1)
                nc.scalar.activation(PTd[h % 2], ps[:, 3 * (h % 2):3 * (h % 2) + 3, 0:384], ACT.Copy).then_inc(d_pt, 1)

            def d_high(pair):
                act.wait_ge(d_o, pair + 1)
                nc.scalar.activation(a_hi[:, 12 + pair, :], bank(6 + pair, 0, TOK), ACT.Copy).then_inc(d_hi, 1)

            t, F = 0, 0
            for l in range(DEPTH):
                ffn_norm(t, ("ffa", l)); t += 1
                ffn(AT["ffa", l], F); F += FT
                norm(t); t += 1
                mixer(l)
                ffn_norm(t, ("ffb", l)); t += 1
                ffn(AT["ffb", l], F); F += FT

            act.wait_ge(x_ready, 8 * (t - 1) + 8)
            act.dma_start(late, late_in).then_inc(late_loaded, 16)
            for i, mix in enumerate((even, odd)):
                norm(t); t += 1
                mix()
                ffn_norm(t, ("ffn2", i)); t += 1
                ffn(AT["ffn", i], F, conv=True); F += FT

        @block.gpsimd
        def _(pool):
            chain = [0]
            nc.gpsimd.memset(nhalf[:], -0.5).then_inc(pool_chain, 1)
            pool.wait_ge(pool_chain, 1)

            def rsqrt(o, i):
                n = i.shape[1]
                return nc.gpsimd.tensor_tensor(o, i, nhalf[:, 0:n], ALU.pow)

            def ffn_norm(t, f):
                acc = tmp[:, 0, :]
                for c in range(1, KC):
                    pool.wait_ge(sq_ready, 8 * t + c + 1)
                    if c > 1:
                        pool.wait_ge(sq_sum, (KC - 1) * f + c - 1)
                    nc.gpsimd.tensor_tensor(acc, acc, tmp[:, c, :], ALU.add).then_inc(sq_sum, 1)
                norm(t)

            def norm(t):
                pool.wait_ge(var_ready, t + 1)
                rsqrt(sc[:, 4:6], sc[:, 2:4]).then_inc(rs_ready, 1)

            def mixer(l):
                pool.wait_ge(*DV.at(l, "cvar"))
                rsqrt(sc[:, 228:232], sc[:, 224:228]).then_inc(*PO.sig(l, "crs"))
                pool.wait_ge(*DV.at(l, "gvar"))
                rsqrt(sc[:, 112:128], sc[:, 128:144]).then_inc(*PO.sig(l, "grs"))
                pool.wait_ge(*AC.at(l, "AT"))
                for m in range(1, LEVELS):
                    if m >= 3:
                        pool.wait_ge(*PE.at(l, ("U", m - 2, 1)))
                    nc.gpsimd.tensor_tensor(ATM[m % 2], ATr, each(const("mt", (m - 1) * 128, 128), 8), ALU.mult
                                            ).then_inc(*PO.sig(l, ("ATM", m)))
                    if m == 3:
                        pool.wait_ge(*DV.at(l, "mobavar"))
                        rsqrt(sc[:, 192:224], sc[:, 160:192]).then_inc(*PO.sig(l, "mobars"))
                pool.wait_ge(*DV.at(l, "ovar"))
                rsqrt(sc[:, 152:160], sc[:, 144:152]).then_inc(*PO.sig(l, "ors"))
                pool.wait_ge(*DV.at(l, "mlavark"))
                rsqrt(sc[:, 208:224], sc[:, 176:192]).then_inc(*PO.sig(l, "mlarsk"))
                pool.wait_ge(*DV.at(l, "mlavarq"))
                rsqrt(sc[:, 192:208], sc[:, 160:176]).then_inc(*PO.sig(l, "mlarsq"))

            t = 0
            for l in range(DEPTH):
                ffn_norm(t, 2 * l); t += 1
                norm(t); t += 1
                mixer(l)
                ffn_norm(t, 2 * l + 1); t += 1

            norm(t); t += 1
            done, n = [0, 0], 0
            for pair in range(2):
                for k in range(CFK - POOL_TAPS, CFK):
                    for q in range(2):
                        i = 2 * pair + q
                        pool.wait_ge(tap_ready, n + 1)
                        if k == CFK - POOL_TAPS:
                            e = nc.gpsimd.tensor_copy(cfp[:, i, :], tapped[:, n % 8, :])
                        else:
                            pool.wait_ge(part_sum, done[q])
                            e = nc.gpsimd.tensor_tensor(cfp[:, i, :], cfp[:, i, :], tapped[:, n % 8, :], ALU.add)
                        e.then_inc(part_sum, 1)
                        n += 1
                        done[q] = n
            pool.wait_ge(*DV2.at(0, "lnvar"))
            rsqrt(sc[:, 276:278], sc[:, 278:280]).then_inc(*PO2.sig(0, "lnrs"))
            ffn_norm(t, 4); t += 1
            norm(t); t += 1
            for j in range(TT):
                pool.wait_ge(*DV2.at(0, f"dvar{j}"))
                rsqrt(sc[:, 400 + 24 * j:424 + 24 * j], sc[:, 352 + 24 * j:376 + 24 * j]).then_inc(*PO2.sig(0, f"drs{j}"))
            ffn_norm(t, 5)

        @block.vector
        def _(dve):
            chain = [0]
            V = nc.vector

            def tick(ins):
                chain[0] += 1
                ins.then_inc(dve_chain, 1)
                return chain[0]

            def need(n):
                dve.wait_ge(dve_chain, n)

            def link(ins):
                need(tick(ins))

            V.memset(ones[:], 1.0).then_inc(consts_set, 1)
            dve.wait_ge(params_loaded, 16)
            V.tensor_scalar(par[:, 0:N_HALVED], par[:, 0:N_HALVED], 0.5, None, ALU.mult).then_inc(halved, 1)
            dve.wait_ge(halved, 1)

            def split(u, j=0):
                if u >= UNITS:
                    return
                dve.wait_ge(hi_ready, u + 1 + 6 * j)
                V.tensor_tensor(w_lo[:, u % SLOTS, :], raw[:, u % RAW, :], w_hi[:, u % SLOTS, :], ALU.subtract
                                ).then_inc(split_ready, 1)

            def update(t, units, factor, gain=None):
                dve.wait_ge(unit_used, units)
                for c in range(KC + 2):
                    if c < KC:
                        V.scalar_tensor_tensor(x[:, c, :], bank(c // 2, (c % 2) * TOK, (c % 2 + 1) * TOK), factor, x[:, c, :],
                                               ALU.mult, ALU.add).then_inc(x_ready, 1)
                    if gain and c >= 2:
                        gained_low(t, c - 2, gain)

            def scales(t):
                dve.wait_ge(stat_ready, t + 1)
                V.tensor_scalar(sc[:, 2:4], bank(6, 0, 2), 1.0 / DM, EPS, ALU.mult, ALU.add).then_inc(var_ready, 1)
                dve.wait_ge(rs_ready, t + 1)
                V.tensor_scalar(diag[:, 0:128], ident, sc[:, 4:5], None, ALU.mult)
                V.tensor_scalar(diag[:, 128:256], ident, sc[:, 5:6], None, ALU.mult).then_inc(diag_ready, 1)
                dve.wait_ge(bc_ready, t + 1)

            def gained_low(t, c, gain):
                dve.wait_ge(h_hi_ready, 8 * t + c + 1)
                dve.wait_ge(x_loaded if t == 0 else x_ready, 16 if t == 0 else 8 * (t - 1) + c + 1)
                V.scalar_tensor_tensor(a_lo[:, c, :], x[:, c, :], whole(gain, c), a_hi[:, c, :], ALU.mult, ALU.subtract
                                       ).then_inc(h_ready, 1)

            def norm(t, gain):
                scales(t)
                def low(c):
                    dve.wait_ge(h_hi_ready, 8 * t + c + 1)
                    V.tensor_tensor(a_lo[:, c, :], tmp[:, c, :], a_hi[:, c, :], ALU.subtract).then_inc(h_ready, 1)
                for c in range(KC):
                    V.scalar_tensor_tensor(tmp[:, c, :], x[:, c, :], whole(gain, c), bank(7, 0, TOK), ALU.mult, ALU.mult
                                           ).then_inc(hn_ready, 1)
                    if c >= 2:
                        low(c - 2)
                low(KC - 2)
                low(KC - 1)

            def scaled(F, p, u_end, j=0):
                dve.wait_ge(unit_used, u_end + 6 * j)
                V.tensor_tensor(gus[:, p, :].rearrange("p (a b) -> p a b", b=TOK), bank(4 + p).rearrange("p (a b) -> p a b", b=TOK),
                                each(rrow, 2), ALU.mult).then_inc(gs_ready, 1)

            def gating(F, p, j=0):
                dve.wait_ge(gate_act, F + 1 + 2 * j)
                V.scalar_tensor_tensor(a2[:, p, :], th2[:, p, :], 1.0, gus[:, p, 0:TOK], ALU.add, ALU.mult
                                       ).then_inc(loop_chain, 1)
                dve.wait_ge(loop_chain, F + 1 + 2 * j)
                V.scalar_tensor_tensor(gu2[:, p, :], a2[:, p, :], 0.25, gus[:, p, TOK:512], ALU.mult, ALU.mult
                                       ).then_inc(gu_ready, 1)

            def gu_low(F, p, j=0):
                dve.wait_ge(gu_hi_ready, F + 1 + 2 * j)
                V.tensor_tensor(a_lo[:, 8 + p, :], gu2[:, p, :], a_hi[:, 8 + p, :], ALU.subtract).then_inc(gu_split, 1)

            def ffn(n0, F0, t, conv=False):
                def gate(f, between=(), j=0):
                    F, p = F0 + f, f % 2
                    scaled(F, p, n0 + 3 * f + (1 if f else 2), j)
                    if conv:
                        for u in between[:1]:
                            split(u, j)
                        taps2(F, p, j)
                        for u in between[1:2]:
                            split(u, j)
                        gating2(F, p, j)
                        for u in between[2:]:
                            split(u, j)
                    else:
                        for u in between[:2]:
                            split(u, j)
                        gating(F, p, j)
                        for u in between[2:]:
                            split(u, j)
                    gu_low(F, p, j)

                if n0 == AT["ffa", 1]:
                    split(n0 - 1 + AHEAD)
                split(n0 + AHEAD); split(n0 + 1 + AHEAD)
                scales(t)
                V.tensor_copy(rrow, bank(7, 0, TOK)).then_inc(rrow_ready, 1)
                dve.wait_ge(rrow_ready, FFN_NORMS.index(t) + 1)
                gate(0)
                def tile(f, u, j=0):
                    gate(f, (u + AHEAD, u + 1 + AHEAD, u + 2 + AHEAD), j)
                last = int(n0 + 3 * FT == UNITS)
                with dve.Fori(0, (FT - 2) // 2 - last) as j:
                    tile(1, n0 + 2, j)
                    tile(2, n0 + 5, j)
                for f in range(FT - 1 - 2 * last, FT - 1):
                    tile(f, n0 + 3 * f - 1)
                gate(FT - 1, (n0 + 3 * FT - 4 + AHEAD,))
                for u in range(n0 + 3 * FT - 3, n0 + 3 * FT - 1):
                    split(u + AHEAD)

            def rotate(v, heads, d, off, half_, cos, sin, m1, m2):
                H = 2 * heads
                w = H * 2 * half_
                m1v = m1[:, 0:w].rearrange("p (a b) -> p a b", b=2 * half_)
                m2v = m2[:, 0:w].rearrange("p (a b) -> p a b", b=2 * half_)

                def products(j):
                    for s in range(2):
                        r = v[:, heads * j:heads * (j + 1), off + s * half_:off + (s + 1) * half_]
                        for m, tab in ((m1v, cos), (m2v, sin)):
                            n = tick(V.tensor_tensor(m[:, heads * j:heads * (j + 1), s * half_:(s + 1) * half_], r,
                                                     each(const(tab, j * half_, half_), heads), ALU.mult))
                    return n

                def sums(n, done=None):
                    need(n)
                    V.tensor_tensor(v[:, :, off:off + half_], m1v[:, :, 0:half_], m2v[:, :, half_:], ALU.subtract)
                    i = V.tensor_tensor(v[:, :, off + half_:off + 2 * half_], m1v[:, :, half_:], m2v[:, :, 0:half_], ALU.add)
                    if done is None:
                        link(i)
                    else:
                        i.then_inc(*done)
                return products, sums

            def score_max(n, scale):
                p = n % 2
                dve.wait_ge(scores_ready, n + 1)
                s = sc[:, 8 + 4 * p:12 + 4 * p]
                v = bank(p, 0, 384).rearrange("p (a b) -> p a b", b=128)[:, 0:3:2, :]
                link(V.tensor_tensor(v, v, each(const("causal"), 2), ALU.add))
                mx = sc[:, 16 + 2 * p:18 + 2 * p]
                V.tensor_reduce(mx[:, 0:1], bank(p, 0, 128), AX.X, ALU.max)
                link(V.tensor_reduce(mx[:, 1:2], bank(p, 128, 384), AX.X, ALU.max))
                V.tensor_scalar(s[:, 0:2], mx, -scale, None, ALU.mult).then_inc(nmax_ready, 1)

            def normalise(n):
                p = n % 2
                dve.wait_ge(exp_done, n + 1)
                s = sc[:, 8 + 4 * p:12 + 4 * p]
                rec = sc[:, 20 + 2 * p:22 + 2 * p]
                link(V.reciprocal(rec, s[:, 2:4]))
                V.tensor_scalar(Pb[p][:, 0:128], Pb[p][:, 0:128], rec[:, 0:1], None, ALU.mult)
                V.tensor_scalar(Pb[p][:, 128:384], Pb[p][:, 128:384], rec[:, 1:2], None, ALU.mult).then_inc(p_ready, 1)

            def o_low(pair, chunk):
                dve.wait_ge(o_hi, pair + 1)
                V.tensor_tensor(a_lo[:, chunk, :], bank(4 + pair % 2, 0, TOK), a_hi[:, chunk, :], ALU.subtract
                                ).then_inc(o_split, 1)

            def attention(l, kind, fill, scale, chunk):
                n0 = 16 * l + 8 * kind
                score_max(n0, scale)
                if kind == 0:
                    dve.wait_ge(*AC.at(l, "oz_hi"))
                    V.tensor_tensor(a_lo[:, 12:16, :], reg(8192, 4, TOK), a_hi[:, 12:16, :], ALU.subtract
                                    ).then_inc(*DV.sig(l, "oz_lo"))
                for n in range(8):
                    if n in fill:
                        split(gate_at(l, fill[n]) + AHEAD)
                    normalise(n0 + n)
                    if n < 7:
                        score_max(n0 + n + 1, scale)
                    if n % 2 == 0 and n:
                        o_low(8 * l + 4 * kind + n // 2 - 1, chunk + n // 2 - 1)
                o_low(8 * l + 4 * kind + 3, chunk + 3)

            def log1p(e, o, w, w2, q):
                link(V.tensor_scalar(o, e, 2.0, None, ALU.add))
                link(V.reciprocal(q, o))
                link(V.tensor_tensor(w, e, q, ALU.mult))
                link(V.tensor_tensor(w2, w, w, ALU.mult))
                link(V.tensor_scalar(q, w2, 1.0 / 17, None, ALU.mult))
                for k in range(7, 0, -1):
                    link(V.scalar_tensor_tensor(q, q, 1.0 / (2 * k + 1), w2, ALU.add, ALU.mult))
                link(V.scalar_tensor_tensor(o, q, 1.0, w, ALU.add, ALU.mult))
                link(V.tensor_scalar(o, o, 2.0, None, ALU.mult))

            def mixer(l):
                for i in range(-1, 4):
                    split(AT["small", l] + i + AHEAD)
                link(V.memset(cb[:, :, 0:3], 0.0))
                dve.wait_ge(*AC.at(l, "sm"))
                for j in range(TT):
                    i = V.tensor_tensor(sc[:, 32 + 4 * j:36 + 4 * j], small[:, j, 420:424], whole(("dtb", l), 0, 4), ALU.add)
                    if j == 0:
                        tick(i)
                i.then_inc(*DV.sig(l, "z0"))
                dve.wait_ge(*AC.at(l, "csq"))
                cv = sc[:, 224:228]
                tick(V.tensor_reduce(cv[:, 0:2], csq[:, :, 0:QR], AX.X, ALU.add))
                link(V.tensor_reduce(cv[:, 2:4], csq[:, :, QR:384], AX.X, ALU.add))
                tick(V.tensor_scalar(cv[:, 0:2], cv[:, 0:2], 1.0 / QR, EPS, ALU.mult, ALU.add))
                V.tensor_scalar(cv[:, 2:4], cv[:, 2:4], 1.0 / KVR, EPS, ALU.mult, ALU.add).then_inc(*DV.sig(l, "cvar"))

                def latents(p):
                    if p == 1:
                        dve.wait_ge(*PO.at(l, "crs"))
                        tick(V.tensor_tensor(cn[:, :, 0:QR], small[:, :, 0:QR], over(sc[:, 228:230], QR), ALU.mult))
                        V.tensor_tensor(cn[:, :, QR:384], small[:, :, QR:384], over(sc[:, 230:232], KVR), ALU.mult
                                        ).then_inc(*DV.sig(l, "cn"))
                    if p == 4:
                        dve.wait_ge(*PE.at(l, "cT"))
                        for f in range(3):
                            i = V.tensor_scalar(c32[:, f, :], bank(6 + f // 2, (f % 2) * TOK, (f % 2 + 1) * TOK),
                                                whole(("cgain", l), f), None, ALU.mult)
                            if f < 2:
                                tick(i)
                        i.then_inc(*DV.sig(l, "c32"))
                    if p == 5:
                        dve.wait_ge(*AC.at(l, "c_hi"))
                        V.tensor_tensor(a_lo[:, 8:11, :], c32, a_hi[:, 8:11, :], ALU.subtract).then_inc(*DV.sig(l, "c_lo"))

                def conv(p):
                    dve.wait_ge(cb_ready, 6 * l + p + 1)
                    c = (2 * p, 2 * p + 1)
                    w = [[half(("gconv", l), GK * i + k) for k in range(GK)] for i in c]
                    n = [tick(V.tensor_scalar(y[:, c[q], :], cb[:, c[q], 0:TOK], w[q][0], None, ALU.mult)) for q in range(2)]
                    for k in range(1, GK):
                        for q in range(2):
                            need(n[q])
                            i = V.scalar_tensor_tensor(y[:, c[q], :], cb[:, c[q], k:k + TOK], w[q][k], y[:, c[q], :],
                                                       ALU.mult, ALU.add)
                            if k < GK - 1:
                                n[q] = tick(i)
                            elif q == 0:
                                tick(i)
                    i.then_inc(conv_ready, 1)

                def silu(p):
                    dve.wait_ge(silu_th, 6 * l + p + 1)
                    v = y[:, 2 * p:2 * p + 2, :]
                    i = V.scalar_tensor_tensor(v, yth[:, 2 * p:2 * p + 2, :], 1.0, v, ALU.add, ALU.mult)
                    if p == 5:
                        i.then_inc(*DV.sig(l, "silu"))
                    else:
                        tick(i)
                for p in range(6):
                    u = AT["gdn", l] + 2 * p
                    split(u + AHEAD); split(u + 1 + AHEAD)
                    conv(p)
                    if p:
                        silu(p - 1)
                    latents(p)
                for q in range(2):
                    u = AT["z", l] + 2 * q
                    split(u + AHEAD); split(u + 1 + AHEAD)
                    if q == 0:
                        silu(5)
                    dve.wait_ge(z_th, 2 * l + q + 1)
                    v = flat(zs[:, 2 * q:2 * q + 2, :])
                    V.scalar_tensor_tensor(v, v, 1.0, bank(6 + q), ALU.add, ALU.mult).then_inc(zs_ready, 1)
                beta, sp, g = sc[:, 104:112], sc[:, 232:240], sc[:, 240:248]
                dve.wait_ge(*AC.at(l, "spe"))
                link(V.tensor_scalar(beta, sc[:, 40:48], 0.5, 0.5, ALU.mult, ALU.add))
                log1p(sc[:, 64:72], sp, sc[:, 248:256], sc[:, 256:264], sc[:, 264:272])
                link(V.scalar_tensor_tensor(sp, sc[:, 32:40], 0.0, sp, ALU.max, ALU.add))
                ea = sc[:, 56:60]
                tick(V.scalar_tensor_tensor(g[:, 0:4], sp[:, 0:4], -1.0, ea, ALU.mult, ALU.mult))
                V.scalar_tensor_tensor(g[:, 4:8], sp[:, 4:8], -1.0, ea, ALU.mult, ALU.mult).then_inc(*DV.sig(l, "g"))
                dve.wait_ge(*DV.at(l, "g"))
                V.tensor_tensor(tg, each(const("tri"), 8), over(g, 128), ALU.mult).then_inc(*DV.sig(l, "tg"))
                for i in range(12):
                    split(AT["moba", l] + i + AHEAD)
                dve.wait_ge(*PE.at(l, "cums"))
                V.tensor_copy(sc[:, 72:84], bank(3, 0, 12)).then_inc(*DV.sig(l, "cumcp"))
                dve.wait_ge(*DV.at(l, "cumcp"))
                V.tensor_tensor(sc[:, 96:100], sc[:, 80:84], sc[:, 72:76], ALU.subtract).then_inc(*DV.sig(l, "gld"))
                dve.wait_ge(*PE.at(l, "R"))
                for t in range(2):
                    i = V.scalar_tensor_tensor(E[:, 4 * t:4 * t + 4, :], bank(4 + t).rearrange("p (a b) -> p a b", b=128), -1.0,
                                               each(const("causal"), 4), ALU.mult, ALU.add)
                    if t == 0:
                        tick(i)
                i.then_inc(*DV.sig(l, "Et"))
                dve.wait_ge(*PE.at(l, "stat"))
                V.tensor_scalar(sc[:, 128:144], bank(2, 0, 16), EPS, None, ALU.add).then_inc(*DV.sig(l, "gvar"))
                dve.wait_ge(*PO.at(l, "grs"))
                link(V.tensor_scalar(sc[:, 112:120], sc[:, 112:120], GD ** -0.5, None, ALU.mult))
                V.tensor_tensor(diag16, each(ident, 16), over(sc[:, 112:128], 128), ALU.mult).then_inc(*DV.sig(l, "diag"))
                dve.wait_ge(*PE.at(l, "bc"))
                for qk in range(2):
                    for t in range(2):
                        v = y[:, 4 * qk:4 * qk + 4, 128 * t:128 * t + 128]
                        i = V.tensor_tensor(v, v, bank(2 * qk + t).rearrange("p (a b) -> p a b", b=128), ALU.mult)
                        if t == 0:
                            tick(i)
                    i.then_inc(*DV.sig(l, ("qn", "kn")[qk]))
                split(AT["gates_a", l] + AHEAD)
                dve.wait_ge(*AC.at(l, "kds"))
                link(V.tensor_tensor(sc[:, 272:276], beta[:, 4:8], sc[:, 92:96], ALU.mult))
                dve.wait_ge(*PE.at(l, "ktok"))
                tick(V.tensor_tensor(kgd[:, 0:4, :], bank(4).rearrange("p (a b) -> p a b", b=128), over(sc[:, 100:104], 128), ALU.mult))
                V.tensor_tensor(kgd[:, 4:8, :], bank(5).rearrange("p (a b) -> p a b", b=128), over(sc[:, 272:276], 128), ALU.mult
                                ).then_inc(*DV.sig(l, "kgd"))
                dve.wait_ge(*PE.at(l, "vtok"))
                tick(V.tensor_tensor(vb[:, 0:4, :], bank(0).rearrange("p (a b) -> p a b", b=128), over(beta[:, 0:4], 128), ALU.mult))
                V.tensor_tensor(vb[:, 4:8, :], bank(1).rearrange("p (a b) -> p a b", b=128), over(beta[:, 4:8], 128), ALU.mult
                                ).then_inc(*DV.sig(l, "vb"))
                split(AT["gates_a", l] + 1 + AHEAD)
                dve.wait_ge(*AC.at(l, "E"))
                dve.wait_ge(*PE.at(l, "G"))
                for b in range(8):
                    i = V.scalar_tensor_tensor(A[:, b, :], bank(2 + b // 4, (b % 4) * 128, (b % 4 + 1) * 128), beta[:, b:b + 1],
                                               E[:, b, :], ALU.mult, ALU.mult)
                i.then_inc(*DV.sig(l, "A"))
                dve.wait_ge(*PE.at(l, "QK"))
                for t in range(2):
                    i = V.tensor_tensor(QK[:, 4 * t:4 * t + 4, :], bank(4 + t).rearrange("p (a b) -> p a b", b=128),
                                        E[:, 4 * t:4 * t + 4, :], ALU.mult)
                i.then_inc(*DV.sig(l, "QK"))
                dve.wait_ge(*DV.at(l, "A"))
                link(V.tensor_tensor(X, A, each(const("m0"), 8), ALU.mult))
                V.tensor_tensor(X, each(ident, 8), X, ALU.subtract).then_inc(*DV.sig(l, "X0"))
                dve.wait_ge(*AC.at(l, "AT"))
                link(V.tensor_tensor(XT, ATr, each(const("m0t"), 8), ALU.mult))
                V.tensor_tensor(XT, each(ident, 8), XT, ALU.subtract).then_inc(*DV.sig(l, "XT0"))
                mq, mk = (flat(mqkv[:, 2 * q:2 * q + 2, :]).rearrange("p (a b) -> p a b", b=MD) for q in range(2))
                q_products, q_sums = rotate(mq, MH, MD, 0, 32, "cosm", "sinm", sA, sB)
                k_products, k_sums = rotate(mk, MH, MD, 0, 32, "cosm", "sinm", sA, sB)

                def moba_step(m):
                    if m == 1:
                        dve.wait_ge(*AC.at(l, "mobasq"))
                        for q, r in enumerate((sA, sB)):
                            link(V.tensor_reduce(sc[:, 160 + 16 * q:176 + 16 * q], r.rearrange("p (a b) -> p a b", b=MD),
                                                 AX.X, ALU.add))
                        V.tensor_scalar(sc[:, 160:192], sc[:, 160:192], 1.0 / MD, EPS, ALU.mult, ALU.add
                                        ).then_inc(*DV.sig(l, "mobavar"))
                    if m == 2:
                        tick(V.tensor_tensor(mq, mq, each(whole(("mobaq", l), 0, MD), 2 * MH), ALU.mult))
                        link(V.tensor_tensor(mk, mk, each(whole(("mobak", l), 0, MD), 2 * MH), ALU.mult))
                    if m == 3:
                        dve.wait_ge(*PO.at(l, "mobars"))
                        tick(V.tensor_tensor(mq, mq, over(sc[:, 192:208], MD), ALU.mult))
                        link(V.tensor_tensor(mk, mk, over(sc[:, 208:224], MD), ALU.mult))
                    if m == 4:
                        q_products(0)
                        step[0] = q_products(1)
                    if m == 5:
                        q_sums(step[0])
                        k_products(0)
                    if m == 6:
                        k_sums(k_products(1), DV.sig(l, "mobaqk"))
                step = [0]
                for m in range(1, LEVELS):
                    split(AT["gates_a", l] + 1 + m + AHEAD)
                    moba_step(m)
                    dve.wait_ge(*(DV.at(l, "XT0") if m == 1 else DV.at(l, ("T", m - 1, 1))))
                    for t in range(2):
                        for k, M, b in (("X", X, 2), ("T", XT, 4)):
                            if (k, m, t) not in DV.steps:
                                continue
                            dve.wait_ge(*PE.at(l, (k, m, t)))
                            v = M[:, 4 * t:4 * t + 4, :]
                            V.tensor_tensor(v, v, bank(b + t).rearrange("p (a b) -> p a b", b=128), ALU.subtract
                                            ).then_inc(*DV.sig(l, (k, m, t)))
                dve.wait_ge(*PE.at(l, "u"))
                V.tensor_copy(VN[:, 0:4, :], bank(0).rearrange("p (a b) -> p a b", b=128)).then_inc(*DV.sig(l, "vn0"))
                dve.wait_ge(*PE.at(l, "S1"))
                V.tensor_copy(S1, bank(3)).then_inc(*DV.sig(l, "S1"))
                tq = reg(9216, 4, 128)
                dve.wait_ge(*PE.at(l, "oa"))
                V.tensor_tensor(tq, bank(5).rearrange("p (a b) -> p a b", b=128), over(sc[:, 92:96], 128), ALU.mult
                                ).then_inc(*DV.sig(l, "tq"))
                dve.wait_ge(*AC.at(l, "u1"))
                V.tensor_tensor(VN[:, 4:8, :], O[:, 4:8, :], bank(4).rearrange("p (a b) -> p a b", b=128), ALU.subtract
                                ).then_inc(*DV.sig(l, "vn1"))
                dve.wait_ge(*PE.at(l, "ob1"))
                dve.wait_ge(*DV.at(l, "vn1"))
                V.tensor_tensor(O[:, 4:8, :], tq, bank(0).rearrange("p (a b) -> p a b", b=128), ALU.add).then_inc(*DV.sig(l, "O1"))
                dve.wait_ge(*AC.at(l, "osq"))
                link(V.tensor_reduce(sc[:, 144:152], ATM[0], AX.X, ALU.add))
                V.tensor_scalar(sc[:, 144:152], sc[:, 144:152], 1.0 / GD, EPS, ALU.mult, ALU.add).then_inc(*DV.sig(l, "ovar"))
                dve.wait_ge(*PO.at(l, "ors"))
                V.tensor_tensor(O, O, over(sc[:, 152:160], 128), ALU.mult).then_inc(*DV.sig(l, "on"))
                dve.wait_ge(*PE.at(l, "oT"))
                oz = reg(8192, 4, TOK)
                for q in range(2):
                    i = V.scalar_tensor_tensor(flat(oz[:, 2 * q:2 * q + 2, :]), bank(4 + q), half(("gout", l)),
                                               flat(zs[:, 2 * q:2 * q + 2, :]), ALU.mult, ALU.mult)
                i.then_inc(*DV.sig(l, "oz"))
                attention(l, 0, MOBA_FILL, MD ** -0.5, 16)
                dve.wait_ge(unit_used, AT["up", l] + 1)
                tick(V.tensor_copy(kl[:, 0:8, LN:LD], each(small[:, 0, 384:416], LH)))
                for i in range(3):
                    split(AT["up", l] + i + AHEAD)
                dve.wait_ge(*AC.at(l, "up"))
                V.tensor_copy(kl[:, 8:16, LN:LD], each(small[:, 1, 384:416], LH)).then_inc(*DV.sig(l, "kr"))
                dve.wait_ge(*AC.at(l, "mlasq"))
                for q, r, name in ((1, rB, "mlavark"), (0, rA, "mlavarq")):
                    v = sc[:, 160 + 16 * q:176 + 16 * q]
                    link(V.tensor_reduce(v, r.rearrange("p (a b) -> p a b", b=LD), AX.X, ALU.add))
                    V.tensor_scalar(v, v, 1.0 / LD, EPS, ALU.mult, ALU.add).then_inc(*DV.sig(l, name))
                gc = AT["gates_c", l]
                split(gc + AHEAD)
                both = ((kl, "mlak", 208, "mlarsk"), (ql, "mlaq", 192, "mlarsq"))
                for v, name, _, _ in both:
                    n = tick(V.tensor_tensor(v, v, each(whole((name, l), 0, LD), 2 * LH), ALU.mult))
                split(gc + 1 + AHEAD)
                need(n)
                for v, _, c, rs in both:
                    dve.wait_ge(*PO.at(l, rs))
                    n = tick(V.tensor_tensor(v, v, over(sc[:, c:c + 16], LD), ALU.mult))
                need(n)
                for v, m in ((kl, 0), (ql, 1024)):
                    products, sums = rotate(v, LH, LD, LN, 16, "cosl", "sinl", rA[:, m // 2:m // 2 + 512], rB[:, m // 2:m // 2 + 512])
                    products(0)
                    sums(products(1), DV.sig(l, "mlaqk") if m else None)
                for n in range(2, PREP):
                    split(gc + n + AHEAD)
                attention(l, 1, MLA_FILL, LD ** -0.5, 8)
                for dp in range(4):
                    m = mA[:, dp % 2, :]
                    for n in range(3):
                        i = 3 * dp + n
                        split(AT["branch", l] + i + AHEAD)
                        dve.wait_ge(unit_used, AT["branch", l] + i + 1)
                        th = flat(gates[:, 8 * n + 2 * dp:8 * n + 2 * dp + 2, :])
                        V.scalar_tensor_tensor(mB if n else m, th, 1.0, bank(4 + i % 4), ALU.add, ALU.mult
                                               ).then_inc(merge_read, 1)
                        if n:
                            dve.wait_ge(merge_read, 12 * l + i + 1)
                            a = V.tensor_tensor(m, m, mB, ALU.add)
                            if n == 2:
                                a.then_inc(mix_ready, 1)
                            else:
                                link(a)
                    dve.wait_ge(mix_hi, 4 * l + dp + 1)
                    V.tensor_tensor(flat(a_lo[:, 2 * dp:2 * dp + 2, :]), m, flat(a_hi[:, 2 * dp:2 * dp + 2, :]), ALU.subtract
                                    ).then_inc(mix_split, 1)
                for k in range(KC):
                    split(AT["out", l] + k + AHEAD)

            def taps2(F, p, j=0):
                lo = HALVED["fconv", (F - F2) // FT][0] + 4 * ((F - F2) % FT)
                w = [par[:, lo + k:lo + k + 1] if isinstance(j, int) else par[:, bass.ds(lo + k + 8 * j, 1)] for k in range(2)]
                dve.wait_ge(conv_in, F - F2 + 1 + 2 * j)
                V.scalar_tensor_tensor(gh2[:, p, 1:], gus[:, p, 0:TOK - 1], w[1], gh2[:, p, 1:], ALU.mult, ALU.add
                                       ).then_inc(loop_chain2, 1)
                dve.wait_ge(loop_chain2, F - F2 + 1 + 2 * j)
                V.scalar_tensor_tensor(gh2[:, p, 2:], gus[:, p, 0:TOK - 2], w[0], gh2[:, p, 2:], ALU.mult, ALU.add
                                       ).then_inc(conv_used, 1)

            def gating2(F, p, j=0):
                dve.wait_ge(gate_act, F + 1 + 2 * j)
                V.scalar_tensor_tensor(a2[:, p, :], th2[:, p, :], 1.0, gh2[:, p, :], ALU.add, ALU.mult
                                       ).then_inc(loop_chain, 1)
                dve.wait_ge(loop_chain, F + 1 + 2 * j)
                V.tensor_tensor(gu2[:, p, :], a2[:, p, :], gus[:, p, TOK:512], ALU.mult).then_inc(gu_ready, 1)

            def even():
                n0 = AT["ev_in"]
                split(n0 - 1 + AHEAD)
                tick(V.memset(ub[:, :, 0:CFK - 1], 0.0))
                link(V.memset(cx[:, :, 0:SCK - 1], 0.0))
                last = [0, 0]
                KD = CFK - POOL_TAPS
                def taps(lo, hi):
                    for n in range(lo, min(hi, 4 * KD)):
                        pair, k, q = n // (2 * KD), n % (2 * KD) // 2, n % 2
                        i = 2 * pair + q
                        w = half("cfconv", CFK * i + k)
                        if k == 0:
                            dve.wait_ge(pair_read, i + 1)
                            last[q] = tick(V.tensor_scalar(cf[:, i, :], ub[:, i, 0:TOK], w, whole("cfbias", i), ALU.mult, ALU.add))
                        else:
                            need(last[q])
                            last[q] = tick(V.scalar_tensor_tensor(cf[:, i, :], ub[:, i, k:k + TOK], w, cf[:, i, :], ALU.mult, ALU.add))
                step, EARLY, MEAN, LATE_TAPS = 0, 5, 2, 12
                for i in range(4):
                    split(n0 + 2 * i + AHEAD); split(n0 + 2 * i + 1 + AHEAD)
                    dve.wait_ge(cf_th, i + 1)
                    V.scalar_tensor_tensor(ub[:, i, CFK - 1:], lnth[:, i, :], 1.0, bank(i, 0, TOK), ALU.add, ALU.mult
                                           ).then_inc(pair_read, 1)
                    if i >= 1:
                        taps(step, step + EARLY)
                        step += EARLY

                for i in range(4):
                    u = n0 + 8 + 2 * i
                    for _ in range(2):
                        split(u + AHEAD)
                        u += 1
                        taps(step, step + MEAN)
                        step += MEAN
                    dve.wait_ge(sc_copy, i + 1)
                    V.tensor_tensor(cx[:, i, SCK - 1:], csb[:, i, :], bank((4, 5, 0, 1)[i], TOK, 512), ALU.mult
                                    ).then_inc(pair_read, 1)
                n = [0] * 4
                for k in range(SCK):
                    for i in range(4):
                        w = whole("scconv", SCK * i + k)
                        if k == 0:
                            dve.wait_ge(pair_read, 5 + i)
                            n[i] = tick(V.tensor_scalar(ysc[:, i, :], cx[:, i, 0:TOK], w, None, ALU.mult))
                        else:
                            need(n[i])
                            n[i] = tick(V.scalar_tensor_tensor(ysc[:, i, :], cx[:, i, k:k + TOK], w, ysc[:, i, :], ALU.mult, ALU.add))
                for q in range(2):
                    for i in range(2):
                        split(n0 + 16 + 2 * q + i + AHEAD)
                        taps(step, step + MEAN)
                        step += MEAN
                    dve.wait_ge(unit_used, n0 + 18 + 2 * q)
                    need(n[2 * q + 1])
                    V.tensor_tensor(flat(o2[:, 2 * q:2 * q + 2, :]), flat(ysc[:, 2 * q:2 * q + 2, :]), bank(6 + q), ALU.mult
                                    ).then_inc(b_read, 1)
                dve.wait_ge(*AC2.at(0, "ysc_hi"))
                V.tensor_tensor(a_lo[:, 8:12, :], o2[:, 0:4, :], a_hi[:, 8:12, :], ALU.subtract).then_inc(*DV2.sig(0, "ysc_lo"))
                for k in range(4):
                    taps(step, step + LATE_TAPS)
                    step += LATE_TAPS
                    split(AT["ev_out"] + k + AHEAD)
                taps(step, 4 * KD)
                need(last[0])
                need(last[1])
                dve.wait_ge(part_sum, 4 * POOL_TAPS)
                V.tensor_tensor(flat(cf), flat(cf), flat(cfp), ALU.add).then_inc(*DV2.sig(0, "cf"))
                dve.wait_ge(*PE2.at(0, "mean"))
                dve.wait_ge(*DV2.at(0, "cf"))
                for i in range(4):
                    e = V.scalar_tensor_tensor(cf[:, i, :], bank(4, 0, TOK), -1.0 / 512, cf[:, i, :], ALU.mult, ALU.add)
                    if i < 3:
                        tick(e)
                e.then_inc(*DV2.sig(0, "cen"))
                dve.wait_ge(*PE2.at(0, "lnstat"))
                V.tensor_scalar(sc[:, 278:280], bank(5, 0, 2), 1.0 / 512, EPS, ALU.mult, ALU.add).then_inc(*DV2.sig(0, "lnvar"))
                dve.wait_ge(*PO2.at(0, "lnrs"))
                tick(V.tensor_scalar(diag[:, 0:128], ident, sc[:, 276:277], None, ALU.mult))
                V.tensor_scalar(diag[:, 128:256], ident, sc[:, 277:278], None, ALU.mult).then_inc(*DV2.sig(0, "lndiag"))
                dve.wait_ge(*PE2.at(0, "lnbc"))
                for i in range(4):
                    n[i] = tick(V.scalar_tensor_tensor(cf[:, i, :], cf[:, i, :], half("lng", i), bank(6, 0, TOK), ALU.mult, ALU.mult))
                for i in range(4):
                    need(n[i])
                    e = V.tensor_scalar(cf[:, i, :], cf[:, i, :], half("lnb", i), None, ALU.add)
                    if i < 3:
                        tick(e)
                e.then_inc(*DV2.sig(0, "yb"))
                dve.wait_ge(*AC2.at(0, "lnth"))
                V.scalar_tensor_tensor(flat(o2[:, 4:8, :]), flat(lnth), 1.0, flat(cf), ALU.add, ALU.mult).then_inc(*DV2.sig(0, "o2"))
                dve.wait_ge(*AC2.at(0, "o2_hi"))
                V.tensor_tensor(a_lo[:, 12:16, :], o2[:, 4:8, :], a_hi[:, 12:16, :], ALU.subtract).then_inc(*DV2.sig(0, "o2_lo"))
                for k in range(4, 8):
                    split(AT["ev_out"] + k + AHEAD)

            def odd():
                n0 = AT["lru_in"]
                split(n0 - 1 + AHEAD)
                link(V.memset(lx[:, :, 0:LK - 1], 0.0))
                V.tensor_scalar(sc[:, 284:288], whole("lam", 0, 4), -1.0, None, ALU.mult).then_inc(*DV2.sig(0, "lamz"))
                n = [0] * 4
                for q in range(4):
                    split(n0 + 2 * q + AHEAD); split(n0 + 2 * q + 1 + AHEAD)
                    if q < 2:
                        dve.wait_ge(lru_copy, q + 1)
                        for k in range(LK):
                            for i in (2 * q, 2 * q + 1):
                                w = whole("lruconv", LK * i + k)
                                if k == 0:
                                    n[i] = tick(V.tensor_scalar(xc[:, i, :], lx[:, i, 0:TOK], w, whole("lrubias", i), ALU.mult, ALU.add))
                                    continue
                                need(n[i])
                                e = V.scalar_tensor_tensor(xc[:, i, :], lx[:, i, k:k + TOK], w, xc[:, i, :], ALU.mult, ALU.add)
                                if (k, i) == (LK - 1, 3):
                                    e.then_inc(*DV2.sig(0, "xc"))
                                else:
                                    n[i] = tick(e)
                d0 = AT["dil_in"]
                split(d0 + AHEAD); split(d0 + 1 + AHEAD)
                dve.wait_ge(*AC2.at(0, "spe"))
                sp = sc[:, 296:300]
                log1p(sc[:, 292:296], sp, sc[:, 248:252], sc[:, 256:260], sc[:, 264:268])
                link(V.scalar_tensor_tensor(sp, sc[:, 284:288], 0.0, sp, ALU.max, ALU.add))
                V.tensor_scalar(sp, sp, -4.0, None, ALU.mult).then_inc(*DV2.sig(0, "sp4"))
                dve.wait_ge(*AC2.at(0, "lgsq"))
                link(V.tensor_scalar(flat(gin), flat(gin), 0.044715, 1.0, ALU.mult, ALU.add))
                V.tensor_tensor(flat(gin), flat(gin), flat(lg), ALU.mult).then_inc(*DV2.sig(0, "gin"))
                for i in range(2, 8):
                    split(d0 + i + AHEAD)
                dve.wait_ge(*AC2.at(0, "gth"))
                tick(V.scalar_tensor_tensor(flat(gin), flat(gin), 1.0, flat(lg), ALU.add, ALU.mult))
                for i in range(8, 12):
                    split(d0 + i + AHEAD)
                dve.wait_ge(*AC2.at(0, "dsq"))
                for j in range(TT):
                    v = sc[:, 352 + 24 * j:376 + 24 * j]
                    link(V.tensor_reduce(v, dsq[:, j, :].rearrange("p (a b) -> p a b", b=DD), AX.X, ALU.add))
                    V.tensor_scalar(v, v, 1.0 / DD, EPS, ALU.mult, ALU.add).then_inc(*DV2.sig(0, f"dvar{j}"))
                for j in range(TT):
                    for q, name in enumerate(("dilq", "dilk")):
                        r = qkv[:, j, DW * q:DW * q + DW].rearrange("p (a b) -> p a b", b=DD)
                        n[j] = tick(V.tensor_tensor(r, r, each(whole(name, 0, DD), 12), ALU.mult))
                for i in range(12, 15):
                    split(d0 + i + AHEAD)
                for j in range(TT):
                    dve.wait_ge(*PO2.at(0, f"drs{j}"))
                    r = qkv[:, j, 0:2 * DW].rearrange("p (a b) -> p a b", b=DD)
                    need(n[j])
                    e = V.tensor_tensor(r, r, over(sc[:, 400 + 24 * j:424 + 24 * j], DD), ALU.mult)
                    if j == 0:
                        tick(e)
                e.then_inc(*DV2.sig(0, "dqk"))
                split(d0 + 15 + AHEAD)
                dve.wait_ge(*AC2.at(0, "ith"))
                V.scalar_tensor_tensor(flat(thi), flat(thi), 1.0, flat(xc), ALU.add, ALU.mult).then_inc(*DV2.sig(0, "xin"))
                dve.wait_ge(*AC2.at(0, "tq"))
                m2 = reg(8720, 4, TOK)
                link(V.tensor_scalar(flat(m2), flat(tqb), -1.0, 1.0, ALU.mult, ALU.add))
                link(V.reciprocal(flat(m2), flat(m2)))
                link(V.scalar_tensor_tensor(flat(tqb), flat(tqb), -2.0, flat(m2), ALU.mult, ALU.mult))
                V.tensor_scalar(flat(thr), flat(tqb), 2.0 ** -100, None, ALU.max).then_inc(*DV2.sig(0, "m2"))
                split(d0 + 16 + AHEAD)
                split(d0 + 17 + AHEAD)

                def dmax(h):
                    p = h % 2
                    dve.wait_ge(d_scores, h + 1)
                    s, mx = sc[:, 304 + 16 * p:320 + 16 * p], sc[:, 336 + 8 * p:344 + 8 * p]
                    v = ps[:, 3 * p:3 * p + 3, 0:384]
                    link(V.tensor_tensor(v, v, dneg, ALU.add))
                    V.tensor_reduce(mx[:, 0:3], v[:, :, 0:128], AX.X, ALU.max)
                    link(V.tensor_reduce(mx[:, 3:6], v[:, :, 128:384], AX.X, ALU.max))
                    link(V.tensor_reduce(mx[:, 6:8], mx[:, 0:6].rearrange("p (a b) -> p a b", b=3), AX.X, ALU.max))
                    V.tensor_scalar(s[:, 0:2], mx[:, 6:8], -(DD ** -0.5), None, ALU.mult).then_inc(d_nmax, 1)
                dve.wait_ge(late_loaded, 16)
                dmax(0)
                dve.wait_ge(*AC2.at(0, "mult"))
                link(V.scalar_tensor_tensor(flat(tqb), flat(tqb), 2.0 ** -100, flat(thr), ALU.is_ge, ALU.mult))
                dve.wait_ge(*DV2.at(0, "xin"))
                link(V.scalar_tensor_tensor(flat(thi), flat(thi), 0.5, flat(tqb), ALU.mult, ALU.mult))
                for i in range(4):
                    e = tick(V.tensor_tensor_scan(tqb[:, i, :], aa[:, i, :], thi[:, i, :], 0.0, ALU.mult, ALU.add))
                need(e)
                V.scalar_tensor_tensor(flat(thi), flat(gin), 0.5, flat(tqb), ALU.mult, ALU.mult).then_inc(*DV2.sig(0, "ylru"))
                for h in range(DH):
                    p = h % 2
                    dve.wait_ge(d_exp, h + 1)
                    s, rec = sc[:, 304 + 16 * p:320 + 16 * p], sc[:, 312 + 16 * p:316 + 16 * p]
                    link(V.tensor_reduce(rec[:, 0:2], s[:, 2:8].rearrange("p (a b) -> p a b", b=3), AX.X, ALU.add))
                    link(V.reciprocal(rec[:, 2:4], rec[:, 0:2]))
                    tick(V.tensor_scalar(Pd[p][:, :, 0:128], Pd[p][:, :, 0:128], rec[:, 2:3], None, ALU.mult))
                    V.tensor_scalar(Pd[p][:, :, 128:384], Pd[p][:, :, 128:384], rec[:, 3:4], None, ALU.mult).then_inc(d_p, 1)
                    if h < 3:
                        dmax(h + 1)
                    if h == 1:
                        dve.wait_ge(*AC2.at(0, "ylru_hi"))
                        V.tensor_tensor(a_lo[:, 8:12, :], thi, a_hi[:, 8:12, :], ALU.subtract).then_inc(*DV2.sig(0, "ylru_lo"))
                    if h == 3:
                        d_low(0)
                d_low(1)
                for k in range(6):
                    split(AT["od_out"] + k + AHEAD)

            def d_low(pair):
                dve.wait_ge(d_hi, pair + 1)
                V.tensor_tensor(a_lo[:, 12 + pair, :], bank(6 + pair, 0, TOK), a_hi[:, 12 + pair, :], ALU.subtract).then_inc(d_lo, 1)

            for c in range(KC):
                gained_low(0, c, ("ffa", 0))
            for u in range(AHEAD):
                split(u)
            dve.wait_ge(consts_loaded, 16)
            t, F = 0, 0
            for l in range(DEPTH):
                t += 1
                ffn(AT["ffa", l], F, t - 1); F += FT
                update(t, AT["ffa", l] + 3 * FT, 1.0)
                norm(t, ("mix", l)); t += 1
                mixer(l)
                update(t, AT["out", l] + 8, 0.5, ("ffb", l))
                t += 1
                ffn(AT["ffb", l], F, t - 1); F += FT
                update(t, AT["ffb", l] + 3 * FT, 1.0, None if l else ("ffa", l + 1))

            for i, (mix, end) in enumerate(((even, AT["ev_out"] + 8), (odd, AT["od_out"] + 6))):
                norm(t, ("mix2", i)); t += 1
                mix()
                update(t, end, 1.0, ("ffn2", i))
                t += 1
                ffn(AT["ffn", i], F, t - 1, conv=True); F += FT
                update(t, AT["ffn", i] + 3 * FT, 1.0)

        @block.tensor
        def _(pe):
            def mm(o, a, b, start=True, stop=True, **k):
                return nc.tensor.matmul(o, a, b, start=start, stop=stop, **k)

            def ffn_stat(t):
                if t == 0:
                    pe.wait_ge(consts_set, 1)
                    pe.wait_ge(consts_loaded, 16)
                pe.wait_ge(sq_sum, (KC - 1) * (FFN_NORMS.index(t) + 1))
                for j in range(TT):
                    i = mm(bank(6, j, j + 1), tmp[:, 0, 128 * j:128 * j + 128], ones[:, 0:1])
                i.then_inc(stat_ready, 1)

            def ffn_spread(t):
                pe.wait_ge(diag_ready, t + 1)
                mm(bank(7, 0, TOK), ones[:], diag[:]).then_inc(bc_ready, 1)

            def norm(t):
                for c in range(KC):
                    pe.wait_ge(sq_ready, 8 * t + c + 1)
                    for j in range(TT):
                        i = mm(bank(6, j, j + 1), tmp[:, c, 128 * j:128 * j + 128], ones[:, 0:1], start=(c == 0 and j == 0),
                               stop=(c == KC - 1), skip_group_check=True)
                i.then_inc(stat_ready, 1)
                pe.wait_ge(diag_ready, t + 1)
                mm(bank(7, 0, TOK), ones[:], diag[:]).then_inc(bc_ready, 1)

            def fm(u, o, j=0, t=None):
                s = u % SLOTS
                pe.wait_ge(split_ready, u + 1 + 6 * j)
                for k in range(KC):
                    if t is not None:
                        pe.wait_ge(h_ready, 8 * t + k + 1)
                    w = slice(k * 128, (k + 1) * 128)
                    mm(o, w_hi[:, s, w], a_hi[:, k, :], start=(k == 0), stop=False)
                    mm(o, w_hi[:, s, w], a_lo[:, k, :], start=False, stop=False)
                    i = mm(o, w_lo[:, s, w], a_hi[:, k, :], start=False, stop=(k == KC - 1))
                i.then_inc(unit_used, 1)

            def km(u, chunk, first, last, j=0):
                s = u % SLOTS
                pe.wait_ge(split_ready, u + 1 + 6 * j)
                for n in range(KC):
                    o = bank(n // 2, (n % 2) * TOK, (n % 2 + 1) * TOK)
                    w = slice(n * 128, (n + 1) * 128)
                    mm(o, w_hi[:, s, w], a_hi[:, chunk, :], start=(first and n % 2 == 0), stop=False, skip_group_check=True)
                    mm(o, w_hi[:, s, w], a_lo[:, chunk, :], start=False, stop=False, skip_group_check=True)
                    i = mm(o, w_lo[:, s, w], a_hi[:, chunk, :], start=False, stop=last, skip_group_check=True)
                i.then_inc(unit_used, 1)

            def tm(u, b, cols, kts, k0, first, last, t=None, banks=None, c0=0):
                s = u % SLOTS
                pe.wait_ge(split_ready, u + 1)
                step = UC // kts
                for i in range(kts):
                    k = k0 + i
                    if t is not None:
                        pe.wait_ge(h_ready, 8 * t + k + 1)
                    w = slice(i * step, i * step + cols)
                    for j in range(TT):
                        o = bank(b + j, 0, cols)
                        tk = slice(128 * j, 128 * j + 128)
                        st, sp_ = first and i == 0, last and i == kts - 1
                        mm(o, a_hi[:, c0 + k, tk], w_hi[:, s, w], start=st, stop=False)
                        mm(o, a_hi[:, c0 + k, tk], w_lo[:, s, w], start=False, stop=False)
                        q = mm(o, a_lo[:, c0 + k, tk], w_hi[:, s, w], start=False, stop=sp_)
                q.then_inc(unit_used, 1)

            def ffn(n0, F0, t):
                def gate_up(f, u, j=0, t=None):
                    if F0 + f >= 2:
                        pe.wait_ge(gs_ready, F0 + f - 1 + 2 * j)
                    p = f % 2
                    fm(u, bank(4 + p, 0, TOK), j, t)
                    fm(u + 1, bank(4 + p, TOK, 512), j)
                def down(f, u, first, last, j=0):
                    pe.wait_ge(gu_split, F0 + f + 1 + 2 * j)
                    km(u, 8 + f % 2, first, last, j)
                gate_up(0, n0, 0, t)
                ffn_stat(t)
                if F0:
                    pe.wait_ge(gs_ready, F0)
                fm(n0 + 2, bank(5, 0, TOK))
                ffn_spread(t)
                fm(n0 + 3, bank(5, TOK, 512))
                down(0, n0 + 4, True, False)
                with pe.Fori(0, (FT - 2) // 2) as j:
                    gate_up(2, n0 + 5, j)
                    down(1, n0 + 7, False, False, j)
                    gate_up(3, n0 + 8, j)
                    down(2, n0 + 10, False, False, j)
                down(FT - 1, n0 + 3 * FT - 1, False, True)

            def gate_unit(l, i):
                if 24 * l + i >= 2:
                    pe.wait_ge(gate_evac, 24 * l + i - 1)
                fm(gate_at(l, i), bank(6 + i % 2, 0, TOK))

            def attention(l, kind, fill, q, k, v):
                n0 = 16 * l + 8 * kind
                def scores(n):
                    g = n0 + n
                    if g >= 2:
                        pe.wait_ge(exp_done, g - 1)
                    qh, kh = q(n), k(n)
                    mm(bank(g % 2, 0, 128), qh[:, 0:128], kh[:, 0:128])
                    mm(bank(g % 2, 128, 384), qh[:, 128:256], kh).then_inc(scores_ready, 1)
                def turn(n):
                    g = n0 + n
                    pe.wait_ge(p_ready, g + 1)
                    for b in range(3):
                        i = nc.tensor.transpose(bank(2 + g % 2, 128 * b, 128 * b + 128), Pb[g % 2][:, 128 * b:128 * b + 128], ident)
                    i.then_inc(pt_ps, 1)
                def pv(n):
                    g = n0 + n
                    pair = g // 2
                    pe.wait_ge(pt_ready, g + 1)
                    if pair >= 2:
                        pe.wait_ge(o_split, pair - 1)
                    pt, r = PTb[g % 2], 64 * (n % 2)
                    o = ps[r:r + 64, 4 + pair % 2, 0:TOK]
                    mm(o, v(0, n), pt[:, 0:256], start=True, stop=False)
                    i = mm(o[:, 128:256], v(1, n), pt[:, 256:384], start=False, stop=True)
                    if n % 2:
                        i.then_inc(o_ready, 1)
                scores(0)
                for n in range(8):
                    if n < 7:
                        scores(n + 1)
                    if n in fill:
                        gate_unit(l, fill[n])
                    turn(n)
                    if n:
                        pv(n - 1)
                pv(7)

            def mixer(l, t):
                ev = lambda s, st: pe.wait_ge(*s.at(l, st))
                for i in range(4):
                    tm(AT["small", l] + i, 0, SMALL, 2, 2 * i, i == 0, i == 3, t)
                for i in range(12):
                    if i == 8:
                        ev(AC, "sm")
                    if i == 8:
                        ev(DV, "cn")
                        for f in range(3):
                            for tt in range(2):
                                q = nc.tensor.transpose(bank(6 + f // 2, (f % 2) * TOK + 128 * tt, (f % 2) * TOK + 128 * tt + 128),
                                                        cn[:, tt, 128 * f:128 * f + 128], ident)
                        q.then_inc(*PE.sig(l, "cT"))
                    p = i // 2
                    fm(AT["gdn", l] + i, bank((2 + p) % 6, (i % 2) * TOK, (i % 2 + 1) * TOK))
                ev(DV, "c32")
                for i in range(4):
                    fm(AT["z", l] + i, bank(6 + i // 2, (i % 2) * TOK, (i % 2 + 1) * TOK))
                for g in range(3):
                    pe.wait_ge(cb_ready, 6 * l + 2 * g + 2)
                    for i in range(4):
                        tm(AT["moba", l] + 4 * g + i, (2, 4, 0)[g], 512, 2, 2 * i, i == 0, i == 3)
                ev(DV, "g")
                pe.wait_ge(m_ready, 3 * l + 2)
                g8 = sc[:, 240:248]
                mm(bank(3, 0, 8), const("tri"), g8)
                mm(bank(3, 8, 12), ones[:], g8[:, 0:4]).then_inc(*PE.sig(l, "cums"))
                ev(DV, "tg")
                for b in range(2):
                    i = mm(bank(4 + b), ones[:], flat(tg[:, 4 * b:4 * b + 4, :]))
                i.then_inc(*PE.sig(l, "R"))
                ev(AC, "gsq")
                for qk in range(2):
                    for tt in range(2):
                        for h in range(4):
                            c = qk * 8 + tt * 4 + h
                            i = mm(bank(2, c, c + 1), tmp[:, qk * 4 + h, 128 * tt:128 * tt + 128], ones[:, 0:1])
                i.then_inc(*PE.sig(l, "stat"))
                pe.wait_ge(zs_ready, 2 * l + 2)
                gate_unit(l, 0)
                ev(DV, "diag")
                pe.wait_ge(m_ready, 3 * l + 3)
                for b in range(4):
                    i = mm(bank(b), ones[:], flat(diag16[:, 4 * b:4 * b + 4, :]))
                i.then_inc(*PE.sig(l, "bc"))
                gate_unit(l, 1)
                kT = lambda tt, h: y[:, 4 + h, 128 * tt:128 * tt + 128]
                qT = lambda tt, h: y[:, h, 128 * tt:128 * tt + 128]
                vT = lambda tt, h: y[:, 8 + h, 128 * tt:128 * tt + 128]
                def blocks(b, f, step):
                    for tt in range(2):
                        for h in range(4):
                            i = f(bank(b + tt, 128 * h, 128 * h + 128), tt, h)
                    i.then_inc(*PE.sig(l, step))
                ev(DV, "kn")
                ev(DV, "Et")
                blocks(4, lambda o, tt, h: nc.tensor.transpose(o, kT(tt, h), ident), "ktok")
                blocks(0, lambda o, tt, h: nc.tensor.transpose(o, vT(tt, h), ident), "vtok")
                blocks(2, lambda o, tt, h: mm(o, kT(tt, h), kT(tt, h)), "G")
                ev(DV, "kgd")
                blocks(4, lambda o, tt, h: mm(o, qT(tt, h), kT(tt, h)), "QK")
                ev(DV, "vb")
                ev(DV, "A")
                blocks(0, lambda o, tt, h: nc.tensor.transpose(o, A[:, 4 * tt + h, :], ident), "AT")
                ev(DV, "QK")
                blocks(2, lambda o, tt, h: nc.tensor.transpose(o, QK[:, 4 * tt + h, :], ident), "QKT")
                ev(DV, "XT0")
                ev(AC, "QKT")
                for m in range(1, LEVELS):
                    ev(PO, ("ATM", m))
                    for tt in range(2):
                        if m > 1:
                            ev(DV, ("X", m - 1, tt))
                        for h in range(4):
                            b = 4 * tt + h
                            i = mm(bank(tt, 128 * h, 128 * h + 128), ATM[m % 2][:, b, :], X[:, b, :])
                        i.then_inc(*PE.sig(l, ("U", m, tt)))
                    gate_unit(l, 1 + m)
                    for tt in range(2):
                        ev(AC, ("U", m, tt))
                        if m > 1:
                            ev(DV, ("T", m - 1, tt))
                        if m < LEVELS - 1:
                            for h in range(4):
                                b = 4 * tt + h
                                i = mm(bank(2 + tt, 128 * h, 128 * h + 128), XT[:, b, :], U[:, b, :])
                            i.then_inc(*PE.sig(l, ("X", m, tt)))
                        for h in range(4):
                            b = 4 * tt + h
                            i = mm(bank(4 + tt, 128 * h, 128 * h + 128), U[:, b, :], XT[:, b, :])
                        i.then_inc(*PE.sig(l, ("T", m, tt)))
                ev(DV, ("T", LEVELS - 1, 1))
                four = lambda b, f, step: [f(bank(b, 128 * h, 128 * h + 128), h) for h in range(4)][-1].then_inc(*PE.sig(l, step))
                blocks(0, lambda o, tt, h: mm(o, XT[:, 4 * tt + h, :], vb[:, 4 * tt + h, :]), "u")
                four(2, lambda o, h: mm(o, kgd[:, 4 + h, :], XT[:, 4 + h, :]), "wT")
                ev(DV, "vn0")
                four(3, lambda o, h: mm(o, kgd[:, h, :], VN[:, h, :]), "S1")
                ev(AC, "wT")
                four(2, lambda o, h: mm(o, QKT[:, h, :], VN[:, h, :]), "ob0")
                ev(DV, "S1")
                four(4, lambda o, h: mm(o, wT[:, 128 * h:128 * h + 128], S1[:, 128 * h:128 * h + 128]), "wS")
                four(5, lambda o, h: mm(o, qT(1, h), S1[:, 128 * h:128 * h + 128]), "oa")
                ev(DV, "vn1")
                four(0, lambda o, h: mm(o, QKT[:, 4 + h, :], VN[:, 4 + h, :]), "ob1")
                ev(DV, "mobaqk")
                ev(AC, "O0")
                ev(DV, "O1")
                for qk in range(2):
                    for c in range(4):
                        for tt in range(2):
                            i = nc.tensor.transpose(bank(2 * qk + c // 2, (c % 2) * TOK + 128 * tt, (c % 2) * TOK + 128 * tt + 128),
                                                    mqkv[:, 2 * qk + tt, 128 * c:128 * c + 128], ident)
                i.then_inc(*PE.sig(l, "mobaT"))
                ev(DV, "on")
                for h in range(4):
                    for tt in range(2):
                        i = nc.tensor.transpose(bank(4 + h // 2, (h % 2) * TOK + 128 * tt, (h % 2) * TOK + 128 * tt + 128),
                                                O[:, 4 * tt + h, :], ident)
                i.then_inc(*PE.sig(l, "oT"))
                ev(AC, "mobaT")
                ev(DV, "oz")
                hp = lambda n: slice(64 * (n % 2), 64 * (n % 2) + 64)
                attention(l, 0, MOBA_FILL, lambda n: qTm[hp(n), n // 2, :], lambda n: kTm[hp(n), n // 2, :],
                          lambda tt, n: mqkv[:, 4 + tt, 64 * n:64 * n + 64])
                pe.wait_ge(exp_done, 16 * l + 8)
                ev(DV, "c_lo")
                pe.wait_ge(o_split, 8 * l + 4)
                pe.wait_ge(gate_evac, 24 * l + 16)
                u = AT["up", l]
                s = u % SLOTS
                tm(u, 0, 512, 2, 0, True, True, c0=8)
                s = (u + 1) % SLOTS
                pe.wait_ge(split_ready, u + 2)
                for j in range(TT):
                    tk = slice(128 * j, 128 * j + 128)
                    for k in range(2):
                        o, w = bank(2, TOK * j, TOK * j + TOK), slice(512 * k, 512 * k + 256)
                        mm(o, a_hi[:, 8 + k, tk], w_hi[:, s, w], start=(k == 0), stop=False)
                        mm(o, a_hi[:, 8 + k, tk], w_lo[:, s, w], start=False, stop=False)
                        i = mm(o, a_lo[:, 8 + k, tk], w_hi[:, s, w], start=False, stop=(k == 1))
                i.then_inc(unit_used, 1)
                s = (u + 2) % SLOTS
                pe.wait_ge(split_ready, u + 3)
                for n in range(2):
                    for j in range(TT):
                        tk = slice(128 * j, 128 * j + 128)
                        o, w = bank(3 + 2 * n + j), slice(512 * n, 512 * n + 512)
                        mm(o, a_hi[:, 10, tk], w_hi[:, s, w], start=True, stop=False)
                        mm(o, a_hi[:, 10, tk], w_lo[:, s, w], start=False, stop=False)
                        i = mm(o, a_lo[:, 10, tk], w_hi[:, s, w], start=False, stop=True)
                i.then_inc(unit_used, 1)
                ev(AC, "up")
                for n in range(PREP):
                    gate_unit(l, 16 + n)
                ev(DV, "mlaqk")
                pe.wait_ge(gate_evac, 24 * l + 16 + PREP)
                for m, b, name in ((ql, 0, "mlaTq"), (kl, 4, "mlaTk")):
                    for h in range(LH):
                        for tt in range(2):
                            c = (h % 2) * TOK + 128 * tt
                            i = nc.tensor.transpose(ps[0:LD, b + h // 2, c:c + 128], m[:, 8 * tt + h, :], ident)
                    i.then_inc(*PE.sig(l, name))
                ev(AC, "mlaTk")
                attention(l, 1, MLA_FILL, lambda n: qTl[:, n, :], lambda n: kTl[:, n, :], lambda tt, n: vl[:, tt, 64 * n:64 * n + 64])
                pe.wait_ge(o_split, 8 * l + 8)
                pe.wait_ge(gate_evac, 24 * l + 24)
                for i in range(12):
                    if 12 * l + i >= 4:
                        pe.wait_ge(merge_read, 12 * l + i - 3)
                    u, n = AT["branch", l] + i, i % 3
                    s = u % SLOTS
                    pe.wait_ge(split_ready, u + 1)
                    for d in range(2):
                        o = bank(4 + i % 4, d * TOK, (d + 1) * TOK)
                        for k in range(4):
                            w, c = slice(k * 256 + d * 128, k * 256 + d * 128 + 128), 8 + 4 * n + k
                            mm(o, w_hi[:, s, w], a_hi[:, c, :], start=(k == 0), stop=False)
                            mm(o, w_hi[:, s, w], a_lo[:, c, :], start=False, stop=False)
                            q = mm(o, w_lo[:, s, w], a_hi[:, c, :], start=False, stop=(k == 3))
                    q.then_inc(unit_used, 1)
                for k in range(KC):
                    pe.wait_ge(mix_split, 4 * l + k // 2 + 1)
                    km(AT["out", l] + k, k, k == 0, k == KC - 1)

            def even(t):
                n0 = AT["ev_in"]
                for i in range(8):
                    b = (0, 1, 2, 3, 4, 5, 0, 1)[i]
                    if i >= 6:
                        pe.wait_ge(pair_read, i - 5)
                    for q in range(2):
                        fm(n0 + 2 * i + q, bank(b, q * TOK, (q + 1) * TOK), 0, t if i == 0 and q == 0 else None)
                for i in range(4):
                    fm(n0 + 16 + i, bank(6 + i // 2, (i % 2) * TOK, (i % 2 + 1) * TOK))
                pe.wait_ge(*DV2.at(0, "ysc_lo"))
                for k in range(4):
                    km(AT["ev_out"] + k, 8 + k, k == 0, False)
                pe.wait_ge(*DV2.at(0, "cf"))
                for i in range(4):
                    e = mm(bank(4, 0, TOK), ones[:], cf[:, i, :], start=(i == 0), stop=(i == 3))
                e.then_inc(*PE2.sig(0, "mean"))
                pe.wait_ge(*AC2.at(0, "lnsq"))
                for c in range(4):
                    for j in range(TT):
                        e = mm(bank(5, j, j + 1), tmp[:, c, 128 * j:128 * j + 128], ones[:, 0:1], start=(c == 0 and j == 0),
                               stop=(c == 3), skip_group_check=True)
                e.then_inc(*PE2.sig(0, "lnstat"))
                pe.wait_ge(*DV2.at(0, "lndiag"))
                mm(bank(6, 0, TOK), ones[:], diag[:]).then_inc(*PE2.sig(0, "lnbc"))
                pe.wait_ge(*DV2.at(0, "o2_lo"))
                for k in range(4, 8):
                    km(AT["ev_out"] + k, 8 + k, False, k == 7)

            def odd(t):
                n0 = AT["lru_in"]
                for i in range(8):
                    fm(n0 + i, bank(i // 2, (i % 2) * TOK, (i % 2 + 1) * TOK), 0, t if i == 0 else None)
                for g in range(5):
                    if g == 3:
                        pe.wait_ge(*DV2.at(0, "xc"))
                        pe.wait_ge(late_loaded, 16)
                        pe.wait_ge(dil_copy, 2)
                        for name, b, step in (("wa", 6, "r"), ("wx", 4, "i")):
                            lo = LATE[name][0]
                            for i in range(4):
                                e = mm(bank(b + i // 2, (i % 2) * TOK, (i % 2 + 1) * TOK), late[:, lo + 128 * i:lo + 128 * i + 128], xc[:, i, :])
                            e.then_inc(*PE2.sig(0, step))
                    if g >= 2:
                        pe.wait_ge(*((lru_copy, 2 * g - 2) if g < 4 else AC2.at(0, "ith")))
                    b = (4, 6, 0, 2, 4)[g]
                    if g < 4:
                        for i in range(4):
                            tm(AT["dil_in"] + 4 * g + i, b, 512, 2, 2 * i, i == 0, i == 3)
                    else:
                        for i in range(2):
                            tm(AT["dil_in"] + 16 + i, b, 256, 4, 4 * i, i == 0, i == 1)
                pe.wait_ge(*DV2.at(0, "dqk"))
                pe.wait_ge(dil_copy, 5)
                for qk in range(2):
                    for c in range(6):
                        for tt in range(2):
                            o = (c % 2) * TOK + 128 * tt
                            e = nc.tensor.transpose(bank(3 * qk + c // 2, o, o + 128),
                                                    qkv[:, tt, DW * qk + 128 * c:DW * qk + 128 * c + 128], ident)
                e.then_inc(*PE2.sig(0, "dilT"))
                pe.wait_ge(*AC2.at(0, "dilT"))

                def scores(h):
                    if h >= 2:
                        pe.wait_ge(d_pt, h - 1)
                    r = slice(64 * (h % 2), 64 * (h % 2) + 64)
                    for g in range(DG):
                        q, k, b = qTd[r, 2 * g + h // 2, :], kTd[r, 2 * g + h // 2, :], 3 * (h % 2) + g
                        mm(bank(b, 0, 128), q[:, 0:128], k[:, 0:128])
                        e = mm(bank(b, 128, 384), q[:, 128:256], k)
                    e.then_inc(d_scores, 1)

                def turn(h):
                    pe.wait_ge(d_p, h + 1)
                    for g in range(DG):
                        for b in range(3):
                            e = nc.tensor.transpose(bank(3 * (h % 2) + g, 128 * b, 128 * b + 128),
                                                    Pd[h % 2][:, g, 128 * b:128 * b + 128], ident)
                    e.then_inc(d_ptps, 1)

                def pv(h):
                    pe.wait_ge(d_pt, h + 1)
                    r = 64 * (h % 2)
                    o = ps[r:r + 64, 6 + h // 2, 0:TOK]
                    for g in range(DG):
                        vd = [qkv[:, tt, 2 * DW + 64 * (4 * g + h):2 * DW + 64 * (4 * g + h) + 64] for tt in range(2)]
                        mm(o, vd[0], PTd[h % 2][:, g, 0:256], start=(g == 0), stop=False, skip_group_check=True)
                        e = mm(o[:, 128:256], vd[1], PTd[h % 2][:, g, 256:384], start=False, stop=(g == DG - 1),
                               skip_group_check=True)
                    if h % 2:
                        e.then_inc(d_o, 1)
                scores(0)
                for h in range(DH):
                    if h < 3:
                        scores(h + 1)
                    turn(h)
                    if h:
                        pv(h - 1)
                pv(3)
                pe.wait_ge(*DV2.at(0, "ylru_lo"))
                for k in range(6):
                    if k >= 4:
                        pe.wait_ge(d_lo, k - 3)
                    km(AT["od_out"] + k, 8 + k, k == 0, k == 5)

            t, F = 0, 0
            for l in range(DEPTH):
                ffn(AT["ffa", l], F, t); F += FT; t += 1
                norm(t)
                mixer(l, t); t += 1
                ffn(AT["ffb", l], F, t); F += FT; t += 1

            for i, mix in enumerate((even, odd)):
                norm(t)
                mix(t); t += 1
                ffn(AT["ffn", i], F, t); F += FT; t += 1


def kernel(**inputs):
    import concourse.bacc as bacc
    from concourse.bass_utils import run_bass_kernel_spmd as run

    a = {k: np.asarray(v) for k, v in inputs.items()}
    stream = np.zeros((UNITS, PART, UC), np.float32)

    def fm(u, w):
        n = w.shape[1] // 128
        stream[u:u + n] = w.reshape(8, 128, n, 128).transpose(2, 1, 0, 3).reshape(n, 128, UC)

    def tm(u, w, kts=2):
        n, c = w.shape[0] // (128 * kts), w.shape[1]
        stream[u:u + n].reshape(n, 128, kts, UC // kts)[:, :, :, :c] = w.reshape(n, kts, 128, c).transpose(0, 2, 1, 3)

    def km(u, w):
        stream[u:u + w.shape[0] // 128] = w.reshape(-1, 128, DM)

    def ffn(u, gate, up, down):
        g = np.empty((3 * FT, 128, UC), np.float32)
        gt, ut = (w.reshape(8, 128, FT, 128).transpose(2, 1, 0, 3).reshape(FT, 128, UC) for w in (gate, up))
        dt = down.reshape(FT, 128, DM)
        g[0], g[1] = gt[0], ut[0]
        g[2:3 * FT - 1:3], g[3:3 * FT - 1:3], g[4:3 * FT - 1:3], g[3 * FT - 1] = gt[1:], ut[1:], dt[:-1], dt[-1]
        stream[u:u + 3 * FT] = g

    for l in range(DEPTH):
        for n in ("ffa", "ffb"):
            w = a[n + "_w_in"][l]
            ffn(AT[n, l], w[:, :FF], w[:, FF:], a[n + "_w_out"][l])
        cuts = np.cumsum([QR, KVR, LR, 512, 512, 512, GH, GH, 512, 1536])
        cq, ckv, kr, gq, gk, gv, gb, ga, gz, m, gl = np.split(a["w_in"][l], cuts, axis=1)
        tm(AT["small", l], np.concatenate([cq, ckv, kr, gb, ga], 1))
        fm(AT["gdn", l], np.concatenate([gq, gk, gv], 1))
        fm(AT["z", l], gz)
        for i in range(3):
            tm(AT["moba", l] + 4 * i, m[:, 512 * i:512 * i + 512])
        for i in range(3):
            fm(AT["gates_" + "abc"[i], l], gl[:, 1024 * i:1024 * i + 1024])
        uq, ukv = a["mla_w_uq"][l], a["mla_w_ukv"][l]
        tm(AT["up", l], uq[:, :512])
        tm(AT["up", l] + 1, uq[:, 512:])
        stream[AT["up", l] + 2] = ukv.reshape(128, LH, 2, 64).transpose(0, 2, 1, 3).reshape(128, UC)
        b = a["w_branch"][l].reshape(3, 4, 128, 4, 256).transpose(3, 0, 2, 1, 4).reshape(12, 128, UC)
        stream[AT["branch", l]:AT["branch", l] + 12] = b
        km(AT["out", l], a["w_out"][l])
        ffn(AT["ffn", l], a["ffn_w_gate_2"][l], a["ffn_w_up_2"][l], a["ffn_w_down_2"][l])
    scb, scc, scx, cfa, cfg = (w.reshape(DM, 4, 128) for w in np.split(a["ev_w_in_2"][0], 5, axis=1))
    fm(AT["ev_in"], np.stack([cfa, cfg], 2).reshape(DM, 1024))
    fm(AT["ev_in"] + 8, np.stack([scc, scx], 2).reshape(DM, 1024))
    fm(AT["ev_in"] + 16, scb.reshape(DM, 512))
    km(AT["ev_out"], a["ev_w_out_2"][0])
    od = a["od_w_in_2"][0]
    fm(AT["lru_in"], od[:, :1024])
    for i in range(4):
        tm(AT["dil_in"] + 4 * i, od[:, 1024 + 512 * i:1536 + 512 * i])
    tm(AT["dil_in"] + 16, od[:, 3072:], 4)
    km(AT["od_out"], a["od_w_out_2"][0])

    params = np.zeros((PART, N_HALVED + N_WHOLE), np.float32)

    def put(name, v, where=WHOLE, base=N_HALVED):
        lo, hi = where[name]
        params[:, base + lo:base + hi] = v

    def feat(v):
        return np.moveaxis(v.reshape(*v.shape[:-1], -1, 128), -1, 0)

    halved = lambda name, v: put(name, v, HALVED, 0)
    taps = lambda v: np.swapaxes(feat(v), 1, 2).reshape(128, -1)
    for l in range(DEPTH):
        halved(("gconv", l), taps(a["gdn_conv"][l]))
        halved(("gout", l), a["gdn_out_norm"][l][:, None])
        halved(("fconv", l), taps(np.concatenate([a["ffn_conv_w_2"][l], a["ffn_conv_b_2"][l][None]])))
        for n, k in (("ffa", "ffa_norm"), ("mix", "mix_norm"), ("ffb", "ffb_norm"), ("mix2", "mix_norm_g_2"),
                     ("ffn2", "ffn_norm_g_2")):
            put((n, l), feat(a[k][l]))
        put(("cgain", l), feat(np.concatenate([a["mla_cq_norm"][l], a["mla_ckv_norm"][l]])))
        for n, k in (("mlaq", "mla_q_norm"), ("mlak", "mla_k_norm"), ("mobaq", "moba_q_norm"), ("mobak", "moba_k_norm"),
                     ("alog", "gdn_a_log"), ("dtb", "gdn_dt_bias")):
            put((n, l), a[k][l][None])
    halved("cfconv", taps(a["ev_cf_conv_w_2"][0]))
    halved("lng", feat(a["ev_cf_ln_g_2"][0]))
    halved("lnb", feat(a["ev_cf_ln_b_2"][0]))
    halved("lru_ba", feat(a["od_lru_ba_2"][0]))
    halved("lru_bx", feat(a["od_lru_bx_2"][0]))
    put("scconv", taps(a["ev_sc_conv_w_2"][0]))
    put("cfbias", feat(a["ev_cf_conv_b_2"][0]))
    put("lruconv", taps(a["od_lru_conv_w_2"][0]))
    put("lrubias", feat(a["od_lru_conv_b_2"][0]))
    put("lam", feat(a["od_lru_lam_2"][0]))
    put("dilq", a["od_q_norm_g_2"][0][None])
    put("dilk", a["od_k_norm_g_2"][0][None])

    con, late = constants()
    for name, k in (("wa", "od_lru_wa_2"), ("wx", "od_lru_wx_2")):
        lo, _ = LATE[name]
        for h in range(8):
            r, c = 64 * (h % 2), lo + 128 * (h // 2) + 64 * (h % 2)
            late[r:r + 64, c:c + 64] = a[k][0][h]

    xt = np.ascontiguousarray(a["x"][0].reshape(TOK, KC, 128).transpose(2, 1, 0))
    nc = bacc.Bacc("TRN2", target_bir_lowering=False, num_devices=1)
    arrays = {"stream": stream, "params": params, "consts": con, "late": late, "x_in": xt}
    args = [nc.dram_tensor(k, v.shape, F32, kind="ExternalInput").ap() for k, v in arrays.items()]
    args.append(nc.dram_tensor("out", (PART, KC, TOK), F32, kind="ExternalOutput").ap())
    build(nc, *args)
    r = run(nc, [arrays], core_ids=[0])
    return r.results[0]["out"].transpose(2, 1, 0).reshape(1, TOK, DM)
```
